# Optimizing a Trainium2 kernel written in Bass

```python
import math
import jax, jax.numpy as jnp
from jax import lax
import numpy as np

D_MODEL = 1024
BATCH = 1
SEQ = 512
DEPTH = 1

CHUNK = 64
EPS = 1e-6
LRU_WIDTH = D_MODEL
LRU_BLOCKS = 16
LRU_BLOCK = LRU_WIDTH // LRU_BLOCKS
CONV_WIDTH = 4
LRU_C = 8.0
N_Q_HEADS = 16
N_KV_HEADS = 4
HEAD_DIM = 64
Q_GROUP = N_Q_HEADS // N_KV_HEADS
ATTN_WIDTH = N_Q_HEADS * HEAD_DIM
KV_WIDTH = N_KV_HEADS * HEAD_DIM
WINDOW = 128
WINDOW_CHUNKS = WINDOW // CHUNK
ROPE_THETA = 500000.0
ROPE_DIM = HEAD_DIM // 4
PEER_HEADS = 8
N_KEYS = 128
N_EXPERTS = N_KEYS * N_KEYS
PEER_QDIM = 256
PEER_HALF = PEER_QDIM // 2
PEER_TOPK = 16
PEER_TOKEN_BLOCK = 128
IN_SPLITS = [LRU_WIDTH, LRU_WIDTH, ATTN_WIDTH, KV_WIDTH, KV_WIDTH, D_MODEL, D_MODEL]
IN_COLS = sum(IN_SPLITS)
IN_OFFSETS = [int(o) for o in np.cumsum(IN_SPLITS)[:-1]]

kernel_name = "hybrid_rglru_swa_peer_block"

def rmsnorm(x, g):
    xf = x.astype(jnp.float32)
    y = xf * lax.rsqrt(jnp.mean(xf * xf, axis=-1, keepdims=True) + EPS) * g.astype(jnp.float32)
    return y.astype(x.dtype)

def rope_tables(seq):
    pos = jnp.arange(seq, dtype=jnp.float32)
    inv_freq = ROPE_THETA ** (-jnp.arange(0, ROPE_DIM, 2, dtype=jnp.float32) / ROPE_DIM)
    ang = pos[:, None] * inv_freq[None, :]
    return jnp.cos(ang), jnp.sin(ang)

def partial_rope(x, cos, sin):
    half = ROPE_DIM // 2
    x1 = x[..., :half].astype(jnp.float32)
    x2 = x[..., half:ROPE_DIM].astype(jnp.float32)
    c = cos[None, :, None, :]
    s = sin[None, :, None, :]
    rot = jnp.concatenate([x1 * c - x2 * s, x2 * c + x1 * s], axis=-1).astype(x.dtype)
    return jnp.concatenate([rot, x[..., ROPE_DIM:]], axis=-1)

def rglru_branch(xb, gb, conv_w, conv_b, w_rg, b_rg, w_ig, b_ig, lru_L):
    B, S, _ = xb.shape
    xp = jnp.pad(xb, ((0, 0), (CONV_WIDTH - 1, 0), (0, 0)))
    xc = conv_b + sum(conv_w[k] * xp[:, k:k + S] for k in range(CONV_WIDTH))
    xblk = xc.reshape(B, S, LRU_BLOCKS, LRU_BLOCK)
    r = jax.nn.sigmoid(jnp.einsum('bsnd,nde->bsne', xblk, w_rg) + b_rg).reshape(B, S, LRU_WIDTH)
    i = jax.nn.sigmoid(jnp.einsum('bsnd,nde->bsne', xblk, w_ig) + b_ig).reshape(B, S, LRU_WIDTH)
    log_a = LRU_C * r.astype(jnp.float32) * jax.nn.log_sigmoid(lru_L.astype(jnp.float32))
    a = jnp.exp(log_a)
    mult = jnp.sqrt(-jnp.expm1(2.0 * log_a))
    u = mult * (i * xc).astype(jnp.float32)

    def combine(lhs, rhs):
        a1, b1 = lhs
        a2, b2 = rhs
        return a1 * a2, a2 * b1 + b2

    _, h = lax.associative_scan(combine, (a, u), axis=1)
    return (h * jax.nn.gelu(gb.astype(jnp.float32))).astype(xb.dtype)

def sliding_window_attention(q, k, v, sinks):
    B, S = q.shape[0], q.shape[1]
    nc = S // CHUNK
    qc = q.reshape(B, nc, CHUNK, N_KV_HEADS, Q_GROUP, HEAD_DIM)
    pad = (WINDOW_CHUNKS - 1) * CHUNK
    kp = jnp.pad(k, ((0, 0), (pad, 0), (0, 0), (0, 0))).reshape(B, nc + WINDOW_CHUNKS - 1, CHUNK, N_KV_HEADS, HEAD_DIM)
    vp = jnp.pad(v, ((0, 0), (pad, 0), (0, 0), (0, 0))).reshape(B, nc + WINDOW_CHUNKS - 1, CHUNK, N_KV_HEADS, HEAD_DIM)
    kb = jnp.concatenate([kp[:, w:w + nc] for w in range(WINDOW_CHUNKS)], axis=2)
    vb = jnp.concatenate([vp[:, w:w + nc] for w in range(WINDOW_CHUNKS)], axis=2)
    scores = jnp.einsum('bnqhgd,bnkhd->bnhgqk', qc, kb).astype(jnp.float32) / math.sqrt(HEAD_DIM)
    key_chunk = (jnp.arange(nc)[:, None] - (WINDOW_CHUNKS - 1)
                 + jnp.arange(WINDOW_CHUNKS * CHUNK)[None, :] // CHUNK)
    valid = (key_chunk >= 0)[None, :, None, None, None, :]
    scores = jnp.where(valid, scores, -1e30)
    sink = sinks.astype(jnp.float32).reshape(N_KV_HEADS, Q_GROUP)[None, None, :, :, None, None]
    m = jnp.maximum(jnp.max(scores, axis=-1, keepdims=True), sink)
    p = jnp.exp(scores - m)
    probs = p / (jnp.sum(p, axis=-1, keepdims=True) + jnp.exp(sink - m))
    out = jnp.einsum('bnhgqk,bnkhd->bnqhgd', probs.astype(vb.dtype), vb)
    return out.reshape(B, S, ATTN_WIDTH)

def peer_ffn(xn, w_q, b_q, sub_keys, u_emb, v_emb):
    B, S, D = xn.shape
    T = B * S
    xt = xn.reshape(T, D)
    q = (xt @ w_q + b_q).reshape(T, PEER_HEADS, 2, PEER_HALF)
    s = jnp.einsum('thpd,hpkd->thpk', q, sub_keys).astype(jnp.float32)
    s_top, i_top = lax.top_k(s, PEER_TOPK)
    cand = s_top[:, :, 0, :, None] + s_top[:, :, 1, None, :]
    cand_idx = i_top[:, :, 0, :, None] * N_KEYS + i_top[:, :, 1, None, :]
    best, pos = lax.top_k(cand.reshape(T, PEER_HEADS, PEER_TOPK * PEER_TOPK), PEER_TOPK)
    expert = jnp.take_along_axis(cand_idx.reshape(T, PEER_HEADS, PEER_TOPK * PEER_TOPK), pos, axis=-1)
    gates = jax.nn.softmax(best, axis=-1)
    nb = T // PEER_TOKEN_BLOCK

    def block(args):
        xb, eb, gb = args
        u = jnp.take(u_emb, eb, axis=0)
        act = jax.nn.gelu(jnp.einsum('td,thkd->thk', xb, u).astype(jnp.float32))
        vsel = jnp.take(v_emb, eb, axis=0)
        return jnp.einsum('thk,thkd->td', (gb * act).astype(vsel.dtype), vsel)

    out = lax.map(block, (xt.reshape(nb, PEER_TOKEN_BLOCK, D),
                          expert.reshape(nb, PEER_TOKEN_BLOCK, PEER_HEADS, PEER_TOPK),
                          gates.reshape(nb, PEER_TOKEN_BLOCK, PEER_HEADS, PEER_TOPK)))
    return out.reshape(B, S, D)

def setup_inputs(seed: int = 0) -> dict:
    key = jax.random.key(seed)
    ks = jax.random.split(key, 24)
    f32 = jnp.float32
    L = DEPTH

    def nrm(k, shape, scale):
        return jax.random.normal(k, shape, f32) * scale

    a0 = jax.random.uniform(ks[10], (L, LRU_WIDTH), f32, 0.9, 0.999)
    return {
        "x": nrm(ks[0], (BATCH, SEQ, D_MODEL), 1.0),
        "norm_mix_g": 1.0 + nrm(ks[1], (L, D_MODEL), 0.02),
        "w_in": nrm(ks[2], (L, D_MODEL, IN_COLS), D_MODEL ** -0.5),
        "b_in": nrm(ks[3], (L, IN_COLS), 0.02),
        "conv_w": nrm(ks[4], (L, CONV_WIDTH, LRU_WIDTH), CONV_WIDTH ** -0.5),
        "conv_b": nrm(ks[5], (L, LRU_WIDTH), 0.02),
        "w_rg": nrm(ks[6], (L, LRU_BLOCKS, LRU_BLOCK, LRU_BLOCK), LRU_BLOCK ** -0.5),
        "b_rg": nrm(ks[7], (L, LRU_BLOCKS, LRU_BLOCK), 0.02),
        "w_ig": nrm(ks[8], (L, LRU_BLOCKS, LRU_BLOCK, LRU_BLOCK), LRU_BLOCK ** -0.5),
        "b_ig": nrm(ks[9], (L, LRU_BLOCKS, LRU_BLOCK), 0.02),
        "lru_L": jnp.log(a0) - jnp.log1p(-a0),
        "q_norm_g": 1.0 + nrm(ks[11], (L, HEAD_DIM), 0.02),
        "k_norm_g": 1.0 + nrm(ks[12], (L, HEAD_DIM), 0.02),
        "attn_sinks": nrm(ks[13], (L, N_Q_HEADS), 0.5),
        "w_o_lru": nrm(ks[14], (L, LRU_WIDTH, D_MODEL), LRU_WIDTH ** -0.5),
        "w_o_attn": nrm(ks[15], (L, ATTN_WIDTH, D_MODEL), ATTN_WIDTH ** -0.5),
        "w_out": nrm(ks[16], (L, D_MODEL, D_MODEL), D_MODEL ** -0.5),
        "norm_ffn_g": 1.0 + nrm(ks[17], (L, D_MODEL), 0.02),
        "peer_w_q": nrm(ks[18], (L, D_MODEL, PEER_HEADS * PEER_QDIM), D_MODEL ** -0.5),
        "peer_b_q": nrm(ks[19], (L, PEER_HEADS * PEER_QDIM), 0.02),
        "peer_sub_keys": nrm(ks[20], (L, PEER_HEADS, 2, N_KEYS, PEER_HALF), PEER_HALF ** -0.5),
        "peer_u": nrm(ks[21], (L, N_EXPERTS, D_MODEL), D_MODEL ** -0.5),
        "peer_v": nrm(ks[22], (L, N_EXPERTS, D_MODEL), 0.5),
    }

def reference(x, norm_mix_g, w_in, b_in, conv_w, conv_b, w_rg, b_rg, w_ig, b_ig, lru_L,
              q_norm_g, k_norm_g, attn_sinks, w_o_lru, w_o_attn, w_out, norm_ffn_g,
              peer_w_q, peer_b_q, peer_sub_keys, peer_u, peer_v):
    B, S, _ = x.shape
    cos, sin = rope_tables(S)
    h = x
    for l in range(DEPTH):
        xn = rmsnorm(h, norm_mix_g[l])
        proj = xn @ w_in[l] + b_in[l]
        lru_x, lru_g, q, k, v, g_lru, g_attn = jnp.split(proj, IN_OFFSETS, axis=-1)
        y_lru = rglru_branch(lru_x, lru_g, conv_w[l], conv_b[l], w_rg[l], b_rg[l],
                             w_ig[l], b_ig[l], lru_L[l])
        q = rmsnorm(q.reshape(B, S, N_Q_HEADS, HEAD_DIM), q_norm_g[l])
        k = rmsnorm(k.reshape(B, S, N_KV_HEADS, HEAD_DIM), k_norm_g[l])
        v = v.reshape(B, S, N_KV_HEADS, HEAD_DIM)
        q = partial_rope(q, cos, sin)
        k = partial_rope(k, cos, sin)
        y_attn = sliding_window_attention(q, k, v, attn_sinks[l])
        merged = (jax.nn.sigmoid(g_lru) * (y_lru @ w_o_lru[l])
                  + jax.nn.sigmoid(g_attn) * (y_attn @ w_o_attn[l]))
        h = h + merged @ w_out[l]
        hn = rmsnorm(h, norm_ffn_g[l])
        h = h + peer_ffn(hn, peer_w_q[l], peer_b_q[l], peer_sub_keys[l], peer_u[l], peer_v[l])
    return h.astype(x.dtype)


_drawn_inputs = setup_inputs


def setup_inputs(seed=0):
    import zlib

    import numpy as np

    out = dict(_drawn_inputs(seed))
    spreads = {}
    factors = {'b_rg': 19.624, 'b_ig': 16.038, 'q_norm_g': 5.186, 'k_norm_g': 5.924, 'attn_sinks': 8.0}
    for name, (base, spread) in spreads.items():
        noise = np.random.default_rng([zlib.crc32(name.encode()), seed]).standard_normal(out[name].shape)
        drawn = base * np.exp(spread * noise) if base else spread * noise
        out[name] = __import__('jax').numpy.asarray(drawn.astype(out[name].dtype))
    for name, factor in factors.items():
        out[name] = (out[name] * factor).astype(out[name].dtype)
    return out
```

```python
from contextlib import ExitStack

import numpy as np

import concourse.bass as bass
from concourse import mybir

F32 = mybir.dt.float32
F32R = mybir.dt.float32r
BF16 = mybir.dt.bfloat16
U16 = mybir.dt.uint16
ALU = mybir.AluOpType
ACT = mybir.ActivationFunctionType
X = mybir.AxisListType.X

P = 128
T = 512
D = 1024
KB = D // P
EPS = 1e-6
CHUNK = 64
HEAD_DIM = 64
N_KV = 4
PAIRS = 8
CHUNKS = T // CHUNK
LRU_C = 8.0
N_KEYS = 128
TOPK = 16
PEER_HEADS = 8
TBLOCKS = T // P
LOWEST = -3.0e38

KV_TILES, Q_TILES, X_TILES = 0, 4, 12
OA_TILES, G_TILES, OL_TILES = 20, 28, 36
GATE_TILES, OUT_TILES, PQ_TILES = 44, 60, 68
U_TILES, V_TILES = 84, 212
ALL_TILES = 340
TOK0 = 4
W_IN_FIRST = [24, 25, 26, 27] + list(range(16, 24)) + list(range(0, 8))
W_IN_G = list(range(8, 16))
W_IN_GATES = [c for m in range(8) for c in (36 + m, 28 + m)]

_WIDTHS = [("b_in", 84), ("conv_w", 32), ("conv_b", 8), ("b_rg", 8), ("b_ig", 8), ("lru_L", 8),
           ("g_mix", 8), ("g_ffn", 8), ("g_q", 1), ("g_k", 1), ("sinks", 8)]
VEC = {}
_at = 0
for _name, _w in _WIDTHS:
    VEC[_name] = _at
    _at += _w
N_VEC = _at


class Steps:

    def __init__(self, eng, sem):
        self.eng, self.sem, self.n = eng, sem, 0

    def do(self, instruction):
        instruction.then_inc(self.sem, 1)
        self.n += 1
        return self.n

    def wait(self, n=None):
        self.eng.wait_ge(self.sem, n or self.n)

    def restart(self):
        if self.n:
            self.eng.wait_ge(self.sem, self.n)
            self.eng.sem_inc(self.sem, -self.n)
            self.n = 0


def build(nc, x_t, dense_w, u_t, v_t, gates_w, sub_keys, vecs, rope, mats, out):
    act_dram = nc.dram_tensor("act_scratch", [32, P, 4 * T], F32, kind="Internal").ap()
    g_dram = nc.dram_tensor("g_scratch", [16, P, P * 32], F32, kind="Internal").ap()

    with ExitStack() as ctx:
        def sb(name, shape, dt, scope=ctx):
            return scope.enter_context(nc.sbuf_tensor(name, shape, dt))

        def sem(name):
            return ctx.enter_context(nc.semaphore(name))

        bank = [ctx.enter_context(nc.psum_tensor(f"bank{i}", [P, 512], F32)) for i in range(8)]
        SC0, SC1, TR0, TR1, PV, MI = 2, 3, 4, 5, 6, 7

        raw = sb("raw", [P, 4, D], F32)
        w_hi = sb("w_hi", [P, 2, D], F32R)
        w_lo = sb("w_lo", [P, 2, D], F32R)
        vec = sb("vec", [P, N_VEC], F32)
        mat = sb("mat", [P, 2, P], F32)
        ident, rot = mat[:, 0, :], mat[:, 1, :]
        x_hi = sb("x_hi", [P, KB, T], F32R)
        x_lo = sb("x_lo", [P, KB, T], F32R)
        ones = sb("ones", [P, P], F32)
        stat = sb("stat", [P, T], F32)

        front = ExitStack()
        xc = sb("xc", [P, KB, T], F32, front)
        buf_a = sb("buf_a", [P, KB, T], F32, front)
        lru_in = sb("lru_in", [P, KB, T + 3], F32, front)
        y_hi = sb("y_hi", [P, KB, T], F32R, front)
        y_lo = sb("y_lo", [P, KB, T], F32R, front)
        blocks = sb("blocks", [P, P], F32, front)
        tmp = sb("tmp", [P, 2, T], F32, front)
        tmp2 = sb("tmp2", [P, 2, T], F32, front)
        lam = sb("lam", [P, 8, 8], F32, front)
        attn = ExitStack()
        kdup = sb("kdup", [P, N_KV, T], F32, attn)
        v_raw = sb("v_raw", [P, 2, T], F32, attn)
        vwin = sb("vwin", [P, CHUNKS, 2 * P], F32, attn)
        ropes = sb("ropes", [P, 2, T], F32, attn)
        prob = sb("prob", [P, PAIRS, P], F32, attn)
        prob_t = sb("prob_t", [P, PAIRS, P], F32, attn)
        soft = sb("soft", [P, 6, PAIRS], F32, attn)
        attn.close()
        lru = ExitStack()
        rb = sb("rb", [P, KB, T], F32, lru)
        gw = sb("gw", [P, 2, D], F32, lru)
        ib = lru_in[:, :, 3:3 + T]
        lru.close()
        front.close()

        peer = ExitStack()
        x1 = sb("x1", [P, KB, T], F32, peer)
        rout = ExitStack()
        q_pk = sb("q_pk", [P, 2, T], F32, rout)
        keys = sb("keys", [P, 2 * PEER_HEADS, N_KEYS], F32, rout)
        iota_e = sb("iota_e", [P, N_KEYS, 16], BF16, rout)
        iota_k = sb("iota_k", [P, 16], BF16, rout)
        i_t = sb("i_t", [P, T], BF16, rout)
        j_t = sb("j_t", [P, T], BF16, rout)
        g_t = [sb(f"g_t{n}", [P, T], BF16, rout) for n in range(3)]
        act_out = sb("act_out", [P, 2, 4, T], F32, rout)
        topk = ExitStack()
        s_blk = sb("s_blk", [P, 2 * PEER_HEADS, N_KEYS], F32, topk)
        s = sb("s", [P, TBLOCKS, 2 * PEER_HEADS, N_KEYS], F32, topk)
        s_rest = sb("s_rest", [P, 2, N_KEYS], F32, topk)
        top_s = sb("top_s", [P, 2, 16], F32, topk)
        top_i = sb("top_i", [P, PEER_HEADS, 2, 16], U16, topk)
        top_f = sb("top_f", [P, PEER_HEADS, 2, 16], BF16, topk)
        cand = sb("cand", [P, 16, 16], F32, topk)
        cand_rest = sb("cand_rest", [P, 256], F32, topk)
        best = sb("best", [P, PEER_HEADS, 16], F32, topk)
        pos = sb("pos", [P, PEER_HEADS * 16], U16, topk)
        half_i = sb("half_i", [P, 2, P], U16, topk)
        half_f = sb("half_f", [P, 2, P], BF16, topk)
        pick = sb("pick", [P, 2, P, 16], BF16, topk)
        sel = sb("sel", [P, 3, P], F32, topk)
        g_rest = sb("g_rest", [P, 2, P], F32, topk)
        esum = sb("esum", [P, 2, PEER_HEADS], F32, topk)
        topk.close()
        scat = ExitStack()
        eq_i = sb("eq_i", [P, N_KEYS, 16], BF16, scat)
        eq_j = sb("eq_j", [P, 2, N_KEYS, 16], BF16, scat)
        gi = [sb(f"gi{n}", [P, 2, N_KEYS, 16], BF16, scat) for n in range(3)]
        g_out = sb("g_out", [P, 2, N_KEYS, 32], F32, scat)
        scat.close()
        rout.close()
        act_in = sb("act_in", [P, 2, 4, T], F32, peer)
        g_in = sb("g_in", [P, 2, 16, 4, 32], F32, peer)
        e_hi = sb("e_hi", [P, 2, 4, T], F32R, peer)
        e_lo = sb("e_lo", [P, 2, 4, T], F32R, peer)
        peer.close()

        raw_ready = [sem(f"raw_ready{i}") for i in range(4)]
        hi_ready, lo_ready = sem("hi_ready"), sem("lo_ready")
        tile_done = sem("tile_done")
        bank_free = sem("bank_free")
        x_loaded, vec_loaded, mat_loaded = sem("x_loaded"), sem("vec_loaded"), sem("mat_loaded")
        rope_loaded, gw_loaded = sem("rope_loaded"), sem("gw_loaded")
        x1_loaded, keys_loaded = sem("x1_loaded"), sem("keys_loaded")
        consts_ready, iota_ready = sem("consts_ready"), sem("iota_ready")
        act_step, dve_step = sem("act_step"), sem("dve_step")
        sq_ready, ss_ready, ms_ready = sem("sq_ready"), sem("ss_ready"), sem("ms_ready")
        rms_ready, xn_ready, xhi_ready, xlo_ready = (
            sem("rms_ready"), sem("xn_ready"), sem("xhi_ready"), sem("xlo_ready"))
        head_raw, head_gained, head_mm = sem("head_raw"), sem("head_gained"), sem("head_mm")
        head_ms, head_rms, head_done = sem("head_ms"), sem("head_rms"), sem("head_done")
        v_evac, vt_ready, vt_evac = sem("v_evac"), sem("vt_ready"), sem("vt_evac")
        scores_ready, scores_read, shifted = sem("scores_ready"), sem("scores_read"), sem("shifted")
        exp_ready, probs_ready = sem("exp_ready"), sem("probs_ready")
        pt_psum, pt_ready, pv_ready, pv_hi, pv_lo = (
            sem("pt_psum"), sem("pt_ready"), sem("pv_ready"), sem("pv_hi"), sem("pv_lo"))
        lru_evac, conv_ready, gate_mm, gate_sig = (
            sem("lru_evac"), sem("conv_ready"), sem("gate_mm"), sem("gate_sig"))
        lam_e, lam_ready = sem("lam_e"), sem("lam_ready")
        gated, decay_ready, square_ready, root_ready, h_ready = (
            sem("gated"), sem("decay_ready"), sem("square_ready"), sem("root_ready"), sem("h_ready"))
        gelu_ready, y_ready, y_hi_ready, y_lo_ready = (
            sem("gelu_ready"), sem("y_ready"), sem("y_hi_ready"), sem("y_lo_ready"))
        sig_ready, merged_ready, m_hi_ready, m_lo_ready = (
            sem("sig_ready"), sem("merged_ready"), sem("m_hi_ready"), sem("m_lo_ready"))
        s_mm, s_evac, best_ready, gexp_ready, sel_ready, sel_t, sel_evac = (
            sem("s_mm"), sem("s_evac"), sem("best_ready"), sem("gexp_ready"), sem("sel_ready"),
            sem("sel_t"), sem("sel_evac"))
        onehot_ready, tok_done, g_evac = sem("onehot_ready"), sem("tok_done"), sem("g_evac")
        act_stored = [sem(f"act_stored{i}") for i in range(2)]
        g_stored = [sem(f"g_stored{i}") for i in range(2)]
        act_loaded = [sem(f"act_loaded{i}") for i in range(2)]
        g_loaded = [sem(f"g_loaded{i}") for i in range(2)]
        e_ready, e_hi_ready, e_lo_ready = sem("e_ready"), sem("e_hi_ready"), sem("e_lo_ready")
        out_ready, out_stored = sem("out_ready"), sem("out_stored")

        block = ctx.enter_context(nc.Block())

        def window(c):
            return (0, CHUNK) if c == 0 else (CHUNK * (c - 1), 2 * CHUNK)

        def chunks_at(n):
            first = X_TILES + 2
            if n == OA_TILES:
                return range(n - first, CHUNKS)
            return [n - first] if first <= n < OA_TILES else []

        def col(name, m=0):
            return vec[:, VEC[name] + m:VEC[name] + m + 1]

        @block.sync
        def _(sp):
            sp.dma_start(buf_a[:], x_t).then_inc(x_loaded, 16)
            sp.dma_start(vec[:], vecs).then_inc(vec_loaded, 16)
            sp.dma_start(mat[:], mats).then_inc(mat_loaded, 16)
            sp.dma_start(ropes[:], rope).then_inc(rope_loaded, 16)

            def load_tiles(source, it, base, n=4):
                for c in range(n):
                    if isinstance(it, int) and base + n * it + c < 4:
                        pass
                    else:
                        sp.wait_ge(hi_ready, it * n + (base + c - 3))
                        sp.wait_ge(lo_ready, it * n + (base + c - 3))
                    sp.dma_start(raw[:, c % 4, :], source[it * n + c]).then_inc(raw_ready[c % 4], 16)

            load_tiles(dense_w, 0, 0)
            with sp.Fori(1, 6) as it:
                load_tiles(dense_w, it, 0)
            sp.wait_ge(pv_lo, CHUNKS)
            sp.dma_start(gw[:], gates_w).then_inc(gw_loaded, 16)
            with sp.Fori(6, 11) as it:
                load_tiles(dense_w, it, 0)
            sp.wait_ge(h_ready, 8)
            sp.dma_start(x1[:], x_t).then_inc(x1_loaded, 16)
            with sp.Fori(11, 18) as it:
                load_tiles(dense_w, it, 0)
            sp.wait_ge(xlo_ready, 2)
            sp.dma_start(keys[:], sub_keys).then_inc(keys_loaded, 16)
            with sp.Fori(18, 21) as it:
                load_tiles(dense_w, it, 0)
            with sp.Fori(0, 32) as it:
                load_tiles(u_t, it, U_TILES)

            def load_group(it, k):
                if not (isinstance(it, int) and it == 0):
                    sp.wait_ge(e_lo_ready, it * 2 + (k - 1))
                sp.dma_start(act_in[:, k, :, :], act_dram[it * 2 + k]
                             .rearrange("p (c t) -> p c t", c=4)).then_inc(act_loaded[k], 16)
                src = g_dram[:, :, bass.ds(it * 256 + k * 128, 128)]
                sp.dma_start(g_in[:, k, :, :, :].rearrange("p b c t -> p b (c t)"),
                             src.rearrange("b p n -> p b n")).then_inc(g_loaded[k], 16)

            load_tiles(v_t, 0, V_TILES)
            for k in range(2):
                sp.wait_ge(act_stored[k], 16 * 16)
                sp.wait_ge(g_stored[k], 16 * 8)
            sp.wait_ge(tok_done, TOK0 + T // 4)
            load_group(0, 0)
            load_group(0, 1)
            load_tiles(v_t, 1, V_TILES)
            with sp.Fori(1, 16) as it:
                for k in range(2):
                    load_group(it, k)
                    for c in range(4):
                        sp.wait_ge(hi_ready, it * 8 + (V_TILES + 4 * k + c - 3))
                        sp.wait_ge(lo_ready, it * 8 + (V_TILES + 4 * k + c - 3))
                        sp.dma_start(raw[:, c, :], v_t[it * 8 + (4 * k + c)]).then_inc(raw_ready[c], 16)
            for m in range(KB):
                sp.wait_ge(out_ready, m + 1)
                sp.dma_start(out[:, m, :], x1[:, m, :]).then_inc(out_stored, 16)
            sp.wait_ge(out_stored, 16 * KB)

        @block.gpsimd
        def _(pool):
            def lo(it, base, c):
                pool.wait_ge(hi_ready, it * 4 + (base + c + 1))
                if not (isinstance(it, int) and c < 2):
                    pool.wait_ge(tile_done, it * 4 + (base + c - 1))
                pool.tensor_tensor(w_lo[:, c % 2, :], raw[:, c, :], w_hi[:, c % 2, :].bitcast(F32),
                                   ALU.subtract).then_inc(lo_ready, 1)

            for c in range(4):
                lo(0, 0, c)
            with pool.Fori(1, 18) as it:
                for c in range(4):
                    lo(it, 0, c)
            pool.wait_ge(xlo_ready, 2)
            nc.gpsimd.iota(iota_k[:], pattern=[[1, 16]], base=0, channel_multiplier=0,
                           allow_small_or_imprecise_dtypes=True)
            nc.gpsimd.iota(iota_e[:], pattern=[[1, N_KEYS], [0, 16]], base=0, channel_multiplier=0,
                           allow_small_or_imprecise_dtypes=True).then_inc(iota_ready, 1)
            with pool.Fori(18, 85) as it:
                for c in range(4):
                    lo(it, 0, c)

        @block.scalar
        def _(act):
            step = Steps(act, act_step)

            def hi(n, it=None, slot=None):
                slot = n % 4 if slot is None else slot
                if it is None:
                    act.wait_ge(raw_ready[slot], 16 * (n // 4 + 1))
                    if n >= 2:
                        act.wait_ge(tile_done, n - 1)
                else:
                    a, per = it
                    act.wait_ge(raw_ready[slot], a * (4 * per) + 16 * (n // 4 + 1))
                    act.wait_ge(tile_done, a * per + (n - 1))
                nc.scalar.activation(w_hi[:, slot % 2, :], raw[:, slot, :], ACT.Copy).then_inc(hi_ready, 1)

            def rms(src, scratch, first):
                nc.scalar.activation(scratch[:, 0:4, :], src[:, 0:4, :], ACT.Square).then_inc(sq_ready, 1)
                nc.scalar.activation(scratch[:, 4:8, :], src[:, 4:8, :], ACT.Square).then_inc(sq_ready, 1)
                act.wait_ge(ms_ready, first + 1)
                nc.scalar.activation(stat[:], stat[:], ACT.Sqrt).then_inc(rms_ready, 1)
                for k in range(KB):
                    act.wait_ge(xn_ready, KB * first + k + 1)
                    nc.scalar.activation(x_hi[:, k, :], scratch[:, k, :], ACT.Copy).then_inc(xhi_ready, 1)

            act.wait_ge(vec_loaded, 16)
            act.wait_ge(lam_e, 1)
            nc.scalar.activation(lam[:, 1, :], lam[:, 0, :], ACT.Exp).then_inc(lam_e, 1)
            hi(0)
            act.wait_ge(x_loaded, 16)
            rms(buf_a, lru_in[:, :, 0:T], 0)

            def evac(n):
                ps, b = bank[n % 2][:], col("b_in", n)
                if n < 2 or Q_TILES <= n < X_TILES:
                    j = n if n < 2 else n - 2
                    act.wait_ge(head_done, j - 1) if j >= 2 else None
                    nc.scalar.activation(tmp2[:, j % 2, :], ps, ACT.Square, bias=b)
                    dst = tmp[:, j % 2, :] if n < 2 else buf_a[:, n - Q_TILES, :]
                    nc.scalar.activation(dst, ps, ACT.Identity, bias=b).then_inc(bank_free, 1)
                elif n < Q_TILES:
                    nc.scalar.activation(v_raw[:, n - 2, :], ps, ACT.Identity, bias=b).then_inc(bank_free, 1)
                elif n < OA_TILES:
                    m = n - X_TILES
                    nc.scalar.activation(lru_in[:, m, 3:3 + T], ps, ACT.Identity, bias=b).then_inc(bank_free, 1)
                elif n < G_TILES:
                    nc.scalar.activation(buf_a[:, n - OA_TILES, :], ps, ACT.Copy).then_inc(bank_free, 1)
                elif n < OL_TILES:
                    m = n - G_TILES
                    if m >= 2:
                        act.wait_ge(y_ready, m - 1)
                    nc.scalar.activation(tmp[:, m % 2, :], ps, ACT.Gelu_apprx_tanh, bias=b)\
                        .then_inc(bank_free, 1)

            def head_root(j):
                act.wait_ge(head_ms, j + 1)
                nc.scalar.activation(tmp2[:, j % 2, :], tmp2[:, j % 2, :], ACT.Sqrt).then_inc(head_rms, 1)

            def softmax(c):
                _, kw = window(c)
                act.wait_ge(shifted, c + 1)
                nc.scalar.activation(prob[:, :, 0:kw], prob[:, :, 0:kw], ACT.Exp)
                nc.scalar.activation(soft[:, 2, :], soft[:, 1, :], ACT.Exp).then_inc(exp_ready, 1)

            def probs_turned(c):
                _, kw = window(c)
                act.wait_ge(pt_psum, c + 1)
                if c:
                    act.wait_ge(pv_ready, c)
                for g in range(2):
                    last = nc.scalar.activation(prob_t[0:kw, 4 * g:4 * g + 4, :], bank[TR0 + g][0:kw, :]
                                                .rearrange("p (a q) -> p a q", a=4), ACT.Copy)
                last.then_inc(pt_ready, 1)

            def attention_out(c):
                act.wait_ge(pv_ready, c + 1)
                nc.scalar.activation(y_hi[:, :, CHUNK * c:CHUNK * (c + 1)],
                                     bank[PV][:].rearrange("p (a q) -> p a q", a=PAIRS),
                                     ACT.Copy).then_inc(pv_hi, 1)

            def gate_sigmoids(m):
                b0 = (SC0, TR0)[m % 2]
                act.wait_ge(gate_mm, m + 1)
                nc.scalar.activation(rb[:, m, :], bank[b0][:], ACT.Sigmoid, bias=col("b_rg", m))
                nc.scalar.activation(ib[:, m, :], bank[b0 + 1][:], ACT.Sigmoid, bias=col("b_ig", m))\
                    .then_inc(gate_sig, 1)

            def decay(m):
                act.wait_ge(gated, m + 1)
                step.wait(step.do(nc.scalar.activation(xc[:, m, :], rb[:, m, :], ACT.Tanh,
                                                       scale=lam[:, 6, m:m + 1])))
                nc.scalar.activation(rb[:, m, :], rb[:, m, :], ACT.Exp, scale=lam[:, 7, m:m + 1])\
                    .then_inc(decay_ready, 1)

            def root(m):
                act.wait_ge(square_ready, m + 1)
                nc.scalar.activation(xc[:, m, :], xc[:, m, :], ACT.Sqrt).then_inc(root_ready, 1)

            def y_upper(m):
                act.wait_ge(y_ready, m + 1)
                nc.scalar.activation(y_hi[:, m, :], tmp2[:, m % 2, :], ACT.Copy).then_inc(y_hi_ready, 1)

            for n in range(OL_TILES + 1):
                hi(n + 1)
                if n >= 1:
                    act.wait_ge(tile_done, n)
                    evac(n - 1)
                if n in (2, 3) or 6 <= n < 14:
                    head_root(n - 2 if n < 4 else n - 4)
                for c in chunks_at(n):
                    softmax(c)
                    if c:
                        attention_out(c - 1)
                    probs_turned(c)
                    if c == CHUNKS - 1:
                        attention_out(c)
                if n == OA_TILES:
                    act.wait_ge(lam_ready, 1)
                if n in (22, 23, 24, 25):
                    gate_sigmoids(2 * (n - 22))
                    gate_sigmoids(2 * (n - 22) + 1)
                if n in (26, 27):
                    for m in range(4 * (n - 26), 4 * (n - 26) + 4):
                        decay(m)
                if n == 28:
                    for m in range(8):
                        root(m)
                if n >= G_TILES + 2:
                    y_upper(n - G_TILES - 2)
            y_upper(7)

            def ol_body(it, c):
                nc.scalar.activation(rb[:, bass.ds(it * 4 + c, 1), :], bank[c % 2][:]
                                     .rearrange("p (a t) -> p a t", a=1), ACT.Copy).then_inc(bank_free, 1)

            def shifted_loop(first, rounds, body):
                with act.Fori(0, rounds) as it:
                    for c in range(4):
                        hi(first + c + 2, (it, 4), (c + 2) % 4)
                        act.wait_ge(tile_done, it * 4 + (first + c + 1))
                        act.wait_ge(vec_loaded, 16)
                        body(it, c)

            shifted_loop(OL_TILES, 2, ol_body)

            def gate_body(it, c):
                b = vec[:, bass.ds(it * 4 + (VEC["b_in"] + GATE_TILES + c), 1)]
                act.wait_ge(merged_ready, it * 2 + (c // 2))
                act.wait_ge(vec_loaded, 16)
                nc.scalar.activation(tmp[:, c % 2, :], bank[c % 2][:], ACT.Sigmoid, bias=b)\
                    .then_inc(bank_free, 1)
                if c % 2:
                    act.wait_ge(merged_ready, it * 2 + (c // 2 + 1))
                    act.wait_ge(vec_loaded, 16)
                    nc.scalar.activation(y_hi[:, bass.ds(it * 2 + c // 2, 1), :],
                                         tmp2[:, 0:1, :], ACT.Copy).then_inc(m_hi_ready, 1)

            shifted_loop(GATE_TILES, 4, gate_body)
            shifted_loop(OUT_TILES, 2, lambda it, c: None)
            act.wait_ge(bank_free, PQ_TILES)
            rms(x1, lru_in[:, :, 0:T], 1)

            def pq_body(it, c):
                b = vec[:, bass.ds(it * 4 + (VEC["b_in"] + PQ_TILES + c), 1)]
                act.wait_ge(s_mm, it * 4 + c)
                act.wait_ge(vec_loaded, 16)
                nc.scalar.activation(q_pk[:, c % 2, :], bank[c % 2][:], ACT.Identity, bias=b)\
                    .then_inc(bank_free, 1)

            shifted_loop(PQ_TILES, 4, pq_body)

            def gelu(it, per, base, c):
                k = (c // 4) % 2
                if c % 4 == 0:
                    act.wait_ge(act_stored[k], it * (2 * per) + (2 * base + 16 * (c // 8)))
                    act.wait_ge(vec_loaded, 16)
                nc.scalar.activation(act_out[:, k, c % 4, :], bank[c % 2][:], ACT.Gelu_apprx_tanh)\
                    .then_inc(bank_free, 1)
                if c % 4 == 3:
                    act.wait_ge(bank_free, it * per + (U_TILES + base + c + 1))
                    nc.scalar.dma_start(act_dram[it * (per // 4) + (base // 4 + c // 4)],
                                        act_out[:, k, :, :].rearrange("p c t -> p (c t)"))\
                        .then_inc(act_stored[k], 16)

            with act.Fori(0, 4) as it:
                for c in range(16):
                    hi(U_TILES + c + 2, (it, 16), (c + 2) % 4)
                    act.wait_ge(tile_done, it * 16 + (U_TILES + c + 1))
                    gelu(it, 16, 0, c)
                act.wait_ge(best_ready, it + 1)
                nc.scalar.activation(best[:], best[:], ACT.Exp).then_inc(gexp_ready, 1)

            with act.Fori(0, 8) as it:
                for c in range(8):
                    hi(U_TILES + 64 + c + 2, (it, 8), (c + 2) % 4)
                    act.wait_ge(tile_done, it * 8 + (U_TILES + 64 + c + 1))
                    gelu(it, 8, 64, c)
                    k = c // 4
                    if c % 4 == 0:
                        act.wait_ge(g_stored[k], it * 16)
                        act.wait_ge(vec_loaded, 16)
                    for h in range(2):
                        act.wait_ge(tok_done, it * 16 + (TOK0 + 2 * c + h + 1))
                        t0 = 8 * (c % 4) + 4 * h
                        nc.scalar.activation(g_out[:, k, :, t0:t0 + 4].rearrange("p i t -> p t i"),
                                             bank[2 + h][:].rearrange("p (t i) -> p t i", t=4),
                                             ACT.Copy).then_inc(g_evac, 1)
                    if c % 4 == 3:
                        act.wait_ge(g_evac, it * 16 + (2 * c + 2))
                        nc.scalar.dma_start(g_dram[it * 2 + k],
                                            g_out[:, k, :, :].rearrange("p i t -> p (i t)"))\
                            .then_inc(g_stored[k], 16)

            def e_upper(k, it=None):
                g = k if it is None else it * 2 + k
                act.wait_ge(e_ready, g + 1)
                nc.scalar.activation(e_hi[:, k, :, :], act_in[:, k, :, :], ACT.Copy)\
                    .then_inc(e_hi_ready, 1)

            e_upper(0)
            with act.Fori(0, 15) as it:
                for c in range(8):
                    hi(V_TILES + c + 2, (it, 8), (c + 2) % 4)
                    if c % 4 == 0:
                        k = (c // 4 + 1) % 2
                        act.wait_ge(tile_done, it * 8 + (V_TILES + 4 * (c // 4)))
                        act.wait_ge(e_ready, it * 2 + (c // 4 + 2))
                        nc.scalar.activation(e_hi[:, k, :, :], act_in[:, k, :, :], ACT.Copy)\
                            .then_inc(e_hi_ready, 1)
            for c in range(8):
                n = V_TILES + 120 + c
                if n + 2 < ALL_TILES:
                    hi(n + 2)
                if c == 0:
                    act.wait_ge(tile_done, n)
                    act.wait_ge(e_ready, 32)
                    nc.scalar.activation(e_hi[:, 1, :, :], act_in[:, 1, :, :], ACT.Copy)\
                        .then_inc(e_hi_ready, 1)

        @block.vector
        def _(dve):
            step = Steps(dve, dve_step)
            v = nc.vector

            def chain(ins):
                step.wait(step.do(ins))

            chain(v.memset(ones[:], 1.0))
            chain(v.memset(blocks[:], 0.0))
            for h in range(2):
                chain(v.memset(blocks[64 * h:64 * h + 64, 64 * h:64 * h + 64], 1.0))
            v.memset(lam[:, 2, :], 0.0).then_inc(consts_ready, 1)

            L = vec[:, VEC["lru_L"]:VEC["lru_L"] + 8]
            dve.wait_ge(vec_loaded, 16)
            chain(v.tensor_scalar(lam[:, 3, :], L, -1.0, None, ALU.mult))
            v.tensor_tensor(lam[:, 0, :], L, lam[:, 3, :], ALU.min).then_inc(lam_e, 1)
            dve.wait_ge(lam_e, 2)
            e, s_, z, poly = lam[:, 1, :], lam[:, 3, :], lam[:, 4, :], lam[:, 5, :]
            chain(v.tensor_scalar(s_, e, 2.0, None, ALU.add))
            chain(v.reciprocal(z, s_))
            chain(v.tensor_tensor(s_, e, z, ALU.mult))
            chain(v.tensor_tensor(z, s_, s_, ALU.mult))
            terms = 9
            chain(v.tensor_scalar(poly, z, 1.0 / (2 * terms + 1), 1.0 / (2 * terms - 1), ALU.mult, ALU.add))
            for n in range(terms - 2, -1, -1):
                chain(v.tensor_tensor(poly, poly, z, ALU.mult))
                chain(v.tensor_scalar(poly, poly, 1.0 / (2 * n + 1), None, ALU.add))
            chain(v.tensor_tensor(poly, poly, s_, ALU.mult))
            chain(v.tensor_scalar(poly, poly, 2.0, None, ALU.mult))
            chain(v.tensor_scalar(z, L, 0.0, None, ALU.min))
            chain(v.tensor_tensor(z, z, poly, ALU.subtract))
            chain(v.tensor_scalar(lam[:, 6, :], z, -LRU_C, None, ALU.mult))
            v.tensor_scalar(lam[:, 7, :], z, LRU_C, None, ALU.mult).then_inc(lam_ready, 1)

            def rms(src, scratch, gain, first):
                dve.wait_ge(ss_ready, first + 1)
                v.tensor_scalar(stat[:], bank[MI][:], 1.0 / D, EPS, ALU.mult, ALU.add).then_inc(ms_ready, 1)
                dve.wait_ge(rms_ready, first + 1)
                chain(v.reciprocal(stat[:], stat[:]))
                for k in range(KB):
                    v.scalar_tensor_tensor(out=scratch[:, k, :], in0=src[:, k, :], scalar=col(gain, k),
                                           in1=stat[:], op0=ALU.mult, op1=ALU.mult).then_inc(xn_ready, 1)
                for k in range(KB):
                    dve.wait_ge(xhi_ready, KB * first + k + 1)
                    ins = v.tensor_tensor(x_lo[:, k, :], scratch[:, k, :], x_hi[:, k, :].bitcast(F32),
                                          ALU.subtract)
                    if k == KB - 1:
                        ins.then_inc(xlo_ready, 1)

            rms(buf_a, lru_in[:, :, 0:T], "g_mix", 0)
            dve.wait_ge(xlo_ready, 1)
            chain(v.memset(lru_in[:, :, 0:3], 0.0))

            def head_gain(j):
                dve.wait_ge(bank_free, (j if j < 2 else j + 2) + 1)
                x = tmp[:, j % 2, :] if j < 2 else buf_a[:, j - 2, :]
                if j < 2:
                    v.tensor_scalar(x, x, col("g_k"), None, ALU.mult).then_inc(head_gained, 1)
                else:
                    v.tensor_scalar(x, x, col("g_q"), HEAD_DIM ** -0.5, ALU.mult, ALU.mult)\
                        .then_inc(head_gained, 1)

            def head_finish(j):
                x = tmp[:, j % 2, :] if j < 2 else buf_a[:, j - 2, :]
                root = tmp2[:, j % 2, :]
                dve.wait_ge(head_mm, j + 1)
                v.tensor_scalar(root, bank[TR0][:], 1.0 / HEAD_DIM, EPS, ALU.mult, ALU.add)\
                    .then_inc(head_ms, 1)
                if j == 0:
                    dve.wait_ge(rope_loaded, 16)
                chain(v.tensor_tensor(x, x, ropes[:, 0, :], ALU.mult))
                chain(v.tensor_tensor(stat[:], bank[TR1][:], ropes[:, 1, :], ALU.mult))
                chain(v.tensor_tensor(x, x, stat[:], ALU.add))
                dve.wait_ge(head_rms, j + 1)
                chain(v.reciprocal(root, root))
                if j < 2:
                    for h in range(2):
                        part = slice(64 * h, 64 * h + 64)
                        for to in range(2):
                            last = v.tensor_tensor(kdup[64 * to:64 * to + 64, 2 * j + h, :],
                                                   x[part, :], root[part, :], ALU.mult)
                            if (h, to) != (1, 1):
                                chain(last)
                else:
                    last = v.tensor_tensor(x, x, root, ALU.mult)
                last.then_inc(head_done, 1)

            def v_window(w):
                _, kw = window(w)
                dve.wait_ge(vt_ready, w + 1)
                v.tensor_copy(vwin[0:kw, w, :], bank[(MI, PV)[w % 2]][0:kw, 0:2 * P]).then_inc(vt_evac, 1)

            def conv(m):
                dve.wait_ge(bank_free, X_TILES + m + 1)
                w = [col("conv_w", 8 * k + m) for k in range(4)]
                chain(v.tensor_scalar(xc[:, m, :], lru_in[:, m, 3:3 + T], w[3], col("conv_b", m),
                                      ALU.mult, ALU.add))
                for k in range(3):
                    ins = v.scalar_tensor_tensor(out=xc[:, m, :], in0=lru_in[:, m, k:k + T], scalar=w[k],
                                                 in1=xc[:, m, :], op0=ALU.mult, op1=ALU.add)
                    if k < 2:
                        chain(ins)
                ins.then_inc(conv_ready, 1)

            def soft_shift(c):
                _, kw = window(c)
                dve.wait_ge(scores_ready, c + 1)
                sc = [bank[SC0 + g][:].rearrange("p (a k) -> p a k", a=4)[:, :, 0:kw] for g in range(2)]
                for g in range(2):
                    last = step.do(v.tensor_reduce(soft[:, 0, 4 * g:4 * g + 4], sc[g], X, ALU.max))
                step.wait(last)
                chain(v.tensor_tensor(soft[:, 0, :], soft[:, 0, :],
                                      vec[:, VEC["sinks"]:VEC["sinks"] + 8], ALU.max))
                if c:
                    dve.wait_ge(pt_psum, c)
                step.do(v.tensor_tensor(soft[:, 1, :], vec[:, VEC["sinks"]:VEC["sinks"] + 8],
                                        soft[:, 0, :], ALU.subtract))
                step.wait()
                for g in range(2):
                    mx = soft[:, 0, 4 * g:4 * g + 4].unsqueeze(2).to_broadcast([P, 4, kw])
                    last = v.tensor_tensor(prob[:, 4 * g:4 * g + 4, 0:kw], sc[g], mx, ALU.subtract)
                    if g == 0:
                        chain(last)
                last.then_inc(shifted, 1)

            def soft_norm(c):
                _, kw = window(c)
                dve.wait_ge(exp_ready, c + 1)
                chain(v.tensor_reduce(soft[:, 3, :], prob[:, :, 0:kw], X, ALU.add))
                chain(v.tensor_tensor(soft[:, 3, :], soft[:, 3, :], soft[:, 2, :], ALU.add))
                chain(v.reciprocal(soft[:, 4, :], soft[:, 3, :]))
                v.tensor_tensor(prob[:, :, 0:kw], prob[:, :, 0:kw],
                                soft[:, 4, :].unsqueeze(2).to_broadcast([P, PAIRS, kw]),
                                ALU.mult).then_inc(probs_ready, 1)

            def attention_lower(c):
                dve.wait_ge(pv_hi, c + 1)
                cols = slice(CHUNK * c, CHUNK * (c + 1))
                v.tensor_tensor(y_lo[:, :, cols], bank[PV][:].rearrange("p (a q) -> p a q", a=PAIRS),
                                y_hi[:, :, cols].bitcast(F32), ALU.subtract).then_inc(pv_lo, 1)

            def gate_input(m):
                dve.wait_ge(gate_sig, m + 1)
                v.tensor_tensor(ib[:, m, :], ib[:, m, :], xc[:, m, :], ALU.mult).then_inc(gated, 1)

            def square(m):
                dve.wait_ge(decay_ready, m + 1)
                if m:
                    dve.wait_ge(square_ready, m)
                chain(v.tensor_tensor(stat[:], rb[:, m, :], rb[:, m, :], ALU.mult))
                v.scalar_tensor_tensor(out=xc[:, m, :], in0=stat[:], scalar=1.0, in1=xc[:, m, :],
                                       op0=ALU.add, op1=ALU.mult).then_inc(square_ready, 1)

            def scan(m):
                dve.wait_ge(root_ready, m + 1)
                chain(v.tensor_tensor(ib[:, m, :], ib[:, m, :], xc[:, m, :], ALU.mult))
                v.tensor_tensor_scan(ib[:, m, :], rb[:, m, :], ib[:, m, :], 0.0,
                                     ALU.mult, ALU.add).then_inc(h_ready, 1)

            def lru_out(m):
                dve.wait_ge(bank_free, G_TILES + m + 1)
                dve.wait_ge(h_ready, 8)
                if m >= 2:
                    dve.wait_ge(y_lo_ready, m - 1)
                v.tensor_tensor(tmp2[:, m % 2, :], ib[:, m, :], tmp[:, m % 2, :], ALU.mult)\
                    .then_inc(y_ready, 1)

            def lru_lower(m):
                dve.wait_ge(y_hi_ready, m + 1)
                v.tensor_tensor(y_lo[:, m, :], tmp2[:, m % 2, :], y_hi[:, m, :].bitcast(F32),
                                ALU.subtract).then_inc(y_lo_ready, 1)

            for n in range(1, OL_TILES + 1):
                if n == 1 or n == 2 or 5 <= n < 13:
                    j = n - 1 if n < 3 else n - 3
                    head_gain(j)
                    head_finish(j)
                if 5 <= n < 13:
                    v_window(n - 5)
                if X_TILES + 1 <= n <= X_TILES + 8:
                    conv(n - X_TILES - 1)
                for c in chunks_at(n):
                    soft_shift(c)
                    soft_norm(c)
                    if c:
                        attention_lower(c - 1)
                    if c == CHUNKS - 1:
                        attention_lower(c)
                if n in (22, 23, 24, 25):
                    gate_input(2 * (n - 22))
                    gate_input(2 * (n - 22) + 1)
                if n in (26, 27):
                    for m in range(4 * (n - 26), 4 * (n - 26) + 4):
                        square(m)
                if n == 28:
                    for m in range(8):
                        scan(m)
                if n > G_TILES:
                    if n > G_TILES + 1:
                        lru_lower(n - G_TILES - 2)
                    lru_out(n - G_TILES - 1)
            lru_lower(7)
            step.restart()

            with dve.Fori(0, 4) as it:
                for k in range(2):
                    m = bass.ds(it * 2 + k, 1)
                    dve.wait_ge(m_lo_ready, it * 2 + k)
                    dve.wait_ge(bank_free, it * 4 + (GATE_TILES + 2 * k + 1))
                    dve.wait_ge(vec_loaded, 16)
                    step.do(v.tensor_tensor(tmp2[:, 0:1, :], tmp[:, 0:1, :], buf_a[:, m, :], ALU.mult))
                    dve.wait_ge(bank_free, it * 4 + (GATE_TILES + 2 * k + 2))
                    dve.wait_ge(vec_loaded, 16)
                    step.do(v.tensor_tensor(tmp2[:, 1:2, :], tmp[:, 1:2, :], rb[:, m, :], ALU.mult))
                    step.wait()
                    v.tensor_tensor(tmp2[:, 0:1, :], tmp2[:, 0:1, :], tmp2[:, 1:2, :], ALU.add)\
                        .then_inc(merged_ready, 1)
                    dve.wait_ge(m_hi_ready, it * 2 + (k + 1))
                    dve.wait_ge(vec_loaded, 16)
                    v.tensor_tensor(y_lo[:, m, :], tmp2[:, 0:1, :], y_hi[:, m, :].bitcast(F32),
                                    ALU.subtract).then_inc(m_lo_ready, 1)
                step.restart()
            dve.wait_ge(x1_loaded, 16)
            with dve.Fori(0, 2) as it:
                for c in range(4):
                    m = bass.ds(it * 4 + c, 1)
                    dve.wait_ge(tile_done, it * 4 + (OUT_TILES + c + 1))
                    dve.wait_ge(vec_loaded, 16)
                    v.tensor_tensor(x1[:, m, :], x1[:, m, :],
                                    bank[c % 2][:].rearrange("p (a t) -> p a t", a=1),
                                    ALU.add).then_inc(bank_free, 1)
            rms(x1, lru_in[:, :, 0:T], "g_ffn", 1)
            dve.wait_ge(iota_ready, 1)
            with dve.Fori(0, 4) as it:
                for c in range(4):
                    dve.wait_ge(s_mm, it * 4 + (c + 1))
                    dve.wait_ge(vec_loaded, 16)
                    v.tensor_copy(s[:, :, bass.ds(it * 4 + c, 1), :],
                                  bank[2 + c % 2][:].rearrange("p (b a k) -> p b a k", b=4, a=1))\
                        .then_inc(s_evac, 1)

            step.restart()

            with dve.Fori(0, TBLOCKS) as it:
                dve.wait_ge(s_evac, 16)
                chain(v.tensor_copy(s_blk[:], s[:, bass.ds(it, 1), :, :].rearrange("p a l k -> p (a l) k")))
                for h in range(PEER_HEADS):
                    lists = [s_blk[:, 2 * h + p, :] for p in range(2)]
                    lo_, hi_ = slice(0, 8), slice(8, 16)
                    a = [step.do(v.max(top_s[:, p, lo_], lists[p])) for p in range(2)]
                    d = []
                    for p in range(2):
                        step.wait(a[p])
                        step.do(v.max_index(top_i[:, h, p, lo_], top_s[:, p, lo_], lists[p]))
                        d.append(step.do(v.match_replace(s_rest[:, p, :], top_s[:, p, lo_], lists[p],
                                                         LOWEST)))
                    e = []
                    for p in range(2):
                        step.wait(d[p])
                        e.append(step.do(v.max(top_s[:, p, hi_], s_rest[:, p, :])))
                    for p in range(2):
                        step.wait(e[p])
                        step.do(v.max_index(top_i[:, h, p, hi_], top_s[:, p, hi_], s_rest[:, p, :]))
                    chain(v.tensor_tensor(cand[:], top_s[:, 0, :].unsqueeze(2).to_broadcast([P, 16, 16]),
                                          top_s[:, 1, :].unsqueeze(1).to_broadcast([P, 16, 16]), ALU.add))
                    flat = cand[:].rearrange("p a b -> p (a b)")
                    chain(v.max(best[:, h, lo_], flat))
                    step.do(v.max_index(pos[:, 16 * h:16 * h + 8], best[:, h, lo_], flat))
                    chain(v.match_replace(cand_rest[:], best[:, h, lo_], flat, LOWEST))
                    chain(v.max(best[:, h, hi_], cand_rest[:]))
                    step.do(v.max_index(pos[:, 16 * h + 8:16 * h + 16], best[:, h, hi_], cand_rest[:]))
                step.wait()
                step.do(v.tensor_copy(esum[:, 0, :], best[:, :, 0]))
                step.do(v.tensor_single_scalar(half_i[:, 0, :], pos[:], 4, ALU.logical_shift_right))
                step.do(v.tensor_single_scalar(half_i[:, 1, :], pos[:], 15, ALU.bitwise_and))
                step.do(v.tensor_copy(top_f[:], top_i[:]))
                step.wait()
                v.tensor_tensor(best[:], best[:], esum[:, 0, :].unsqueeze(2)
                                .to_broadcast([P, PEER_HEADS, 16]), ALU.subtract).then_inc(best_ready, 1)
                chain(v.tensor_copy(half_f[:], half_i[:]))
                for p in range(2):
                    step.do(v.tensor_tensor(pick[:, p, :, :],
                                            half_f[:, p, :].unsqueeze(2).to_broadcast([P, P, 16]),
                                            iota_k[:].unsqueeze(1).to_broadcast([P, P, 16]), ALU.is_equal))
                step.wait()
                for p in range(2):
                    own = pick[:, p, :, :].rearrange("q (h k) a -> q h k a", h=PEER_HEADS)
                    step.do(v.tensor_tensor(own, own, top_f[:, :, p, :].unsqueeze(2)
                                            .to_broadcast([P, PEER_HEADS, 16, 16]), ALU.mult))
                step.wait()
                for p in range(2):
                    step.do(v.tensor_reduce(sel[:, p, :], pick[:, p, :, :], X, ALU.add))
                dve.wait_ge(gexp_ready, it + 1)
                step.wait()
                chain(v.tensor_reduce(esum[:, 0, :], best[:], X, ALU.add))
                chain(v.reciprocal(esum[:, 1, :], esum[:, 0, :]))
                v.tensor_tensor(sel[:, 2, :].rearrange("p (h k) -> p h k", h=PEER_HEADS), best[:],
                                esum[:, 1, :].unsqueeze(2).to_broadcast([P, PEER_HEADS, 16]),
                                ALU.mult).then_inc(sel_ready, 1)
                dve.wait_ge(sel_t, it + 1)
                t = bass.ds(it * P, P)
                chain(v.tensor_copy(g_rest[:, 0, :], bank[4][:, 2 * P:3 * P]))
                step.do(v.tensor_copy(i_t[:, t], bank[4][:, 0:P]))
                step.do(v.tensor_copy(j_t[:, t], bank[4][:, P:2 * P]))
                chain(v.tensor_copy(g_t[0][:, t], g_rest[:, 0, :]))
                chain(v.tensor_tensor(g_rest[:, 1, :], g_rest[:, 0, :], g_t[0][:, t], ALU.subtract))
                chain(v.tensor_copy(g_t[1][:, t], g_rest[:, 1, :]))
                chain(v.tensor_tensor(g_rest[:, 0, :], g_rest[:, 1, :], g_t[1][:, t], ALU.subtract))
                step.do(v.tensor_copy(g_t[2][:, t], g_rest[:, 0, :]))
                step.restart()

            def onehot(it, c):
                k = c % 2
                t = bass.ds(it * 64 + 16 * c, 16)

                def over_keys(x):
                    return x[:, t].unsqueeze(1).to_broadcast([P, N_KEYS, 16])
                dve.wait_ge(tok_done, it * 16 + (TOK0 + 4 * (c - 1)))
                dve.wait_ge(vec_loaded, 16)
                step.do(v.tensor_tensor(eq_j[:, k, :, :], iota_e[:], over_keys(j_t), ALU.is_equal))
                dve.wait_ge(onehot_ready, it * 4 + c)
                dve.wait_ge(vec_loaded, 16)
                step.do(v.tensor_tensor(eq_i[:], iota_e[:], over_keys(i_t), ALU.is_equal))
                step.wait()
                for n in range(3):
                    last = v.tensor_tensor(gi[n][:, k, :, :], eq_i[:], over_keys(g_t[n]), ALU.mult)
                    if n < 2:
                        step.do(last)
                step.wait()
                last.then_inc(onehot_ready, 1)
                return last

            with dve.Fori(0, 8) as it:
                for c in range(4):
                    onehot(it, c)
                step.restart()

            def gate_times(k):
                return v.tensor_tensor(
                    act_in[:, k, :, :].rearrange("p c (b t) -> p c b t", b=16),
                    act_in[:, k, :, :].rearrange("p c (b t) -> p c b t", b=16),
                    g_in[:, k, :, :, :].rearrange("p b c t -> p c b t"), ALU.mult)

            with dve.Fori(0, 16) as it:
                for k in range(2):
                    dve.wait_ge(act_loaded[k], it * 16 + 16)
                    dve.wait_ge(g_loaded[k], it * 16 + 16)
                    gate_times(k).then_inc(e_ready, 1)
                    dve.wait_ge(e_hi_ready, it * 2 + (k + 1))
                    v.tensor_tensor(e_lo[:, k, :, :], act_in[:, k, :, :], e_hi[:, k, :, :].bitcast(F32),
                                    ALU.subtract).then_inc(e_lo_ready, 1)
            dve.wait_ge(tile_done, ALL_TILES)
            for m in range(KB):
                v.tensor_tensor(x1[:, m, :], x1[:, m, :], bank[m][:], ALU.add).then_inc(out_ready, 1)

        @block.tensor
        def _(pe):
            mm = nc.tensor.matmul

            def dense(c, ps, right_hi, right_lo):
                for k in range(KB):
                    w = w_hi[:, c % 2, P * k:P * (k + 1)]
                    mm(ps, w, right_hi[:, k, :], start=(k == 0), stop=False)
                    mm(ps, w, right_lo[:, k, :], start=False, stop=False)
                return [(w_lo[:, c % 2, P * k:P * (k + 1)], right_hi[:, k, :]) for k in range(KB)]

            def tile(n, right_hi, right_lo, it=None, per=4):
                off = (lambda x: x) if it is None else (lambda x: it * per + x)
                pe.wait_ge(hi_ready, off(n + 1))
                if it is not None or n >= 2:
                    pe.wait_ge(bank_free, off(n - 1))
                ps = bank[n % 2][:]
                lows = dense(n, ps, right_hi, right_lo)
                pe.wait_ge(lo_ready, off(n + 1))
                for k, (w, r) in enumerate(lows):
                    last = mm(ps, w, r, start=False, stop=(k == KB - 1))
                last.then_inc(tile_done, 1)

            def sum_squares(scratch, first):
                for k in range(KB):
                    pe.wait_ge(sq_ready, 2 * first + 1 + k // 4)
                    last = mm(bank[MI][:], ones[:], scratch[:, k, :], start=(k == 0), stop=(k == KB - 1))
                last.then_inc(ss_ready, 1)

            def head(j):
                x = tmp[:, j % 2, :] if j < 2 else buf_a[:, j - 2, :]
                pe.wait_ge(head_gained, j + 1)
                if j:
                    pe.wait_ge(head_done, j)
                mm(bank[TR0][:], blocks[:], tmp2[:, j % 2, :], start=True, stop=True)
                mm(bank[TR1][:], rot, x, start=True, stop=True).then_inc(head_mm, 1)

            def turn_v(w):
                t0, kw = window(w)
                if w >= 2:
                    pe.wait_ge(vt_evac, w - 1)
                for a in range(2):
                    last = nc.tensor.transpose(bank[(MI, PV)[w % 2]][0:kw, P * a:P * (a + 1)],
                                               v_raw[:, a, t0:t0 + kw], ident)
                last.then_inc(vt_ready, 1)

            def scores(c):
                t0, kw = window(c)
                if c:
                    pe.wait_ge(shifted, c)
                for p in range(PAIRS):
                    for h in range(2):
                        part = slice(64 * h, 64 * h + 64)
                        last = mm(bank[SC0 + p // 4][part, P * (p % 4):P * (p % 4) + kw],
                                  buf_a[part, p, CHUNK * c:CHUNK * (c + 1)],
                                  kdup[part, p // 2, t0:t0 + kw], start=True, stop=True)
                last.then_inc(scores_ready, 1)

            def turn_probs(c):
                _, kw = window(c)
                pe.wait_ge(probs_ready, c + 1)
                if c:
                    pe.wait_ge(pt_ready, c)
                for p in range(PAIRS):
                    last = nc.tensor.transpose(bank[TR0 + p // 4][0:kw, P * (p % 4):P * (p % 4 + 1)],
                                               prob[:, p, 0:kw], ident)
                last.then_inc(pt_psum, 1)

            def weigh(c):
                _, kw = window(c)
                pe.wait_ge(pt_ready, c + 1)
                if c:
                    pe.wait_ge(pv_lo, c)
                for kv in range(N_KV):
                    for h in range(2):
                        at = P * (kv // 2) + 64 * (kv % 2)
                        last = mm(bank[PV][64 * h:64 * h + 64, P * kv:P * (kv + 1)],
                                  vwin[0:kw, c, at:at + 64],
                                  prob_t[0:kw, 2 * kv:2 * kv + 2, 64 * h:64 * h + 64],
                                  start=True, stop=True)
                last.then_inc(pv_ready, 1)

            def lru_gates(m):
                b0 = (SC0, TR0)[m % 2]
                pe.wait_ge(conv_ready, m + 1)
                if m >= 2:
                    pe.wait_ge(gate_sig, m - 1)
                for g in range(2):
                    last = mm(bank[b0 + g][:], gw[:, g, P * m:P * (m + 1)], xc[:, m, :],
                              start=True, stop=True)
                last.then_inc(gate_mm, 1)

            pe.wait_ge(consts_ready, 1)
            sum_squares(lru_in[:, :, 0:T], 0)
            pe.wait_ge(xlo_ready, 1)
            pe.wait_ge(mat_loaded, 16)
            for n in range(OL_TILES):
                if n in (2, 3) or 6 <= n < 14:
                    head(n - 2 if n < 4 else n - 4)
                if 5 <= n < 13:
                    if n == 5:
                        pe.wait_ge(bank_free, 4)
                    turn_v(n - 5)
                for c in chunks_at(n):
                    if c == 0:
                        pe.wait_ge(head_done, 10)
                        pe.wait_ge(vt_evac, CHUNKS)
                    scores(c)
                    if c:
                        weigh(c - 1)
                    if n == OA_TILES:
                        turn_probs(c)
                if n == OA_TILES:
                    weigh(CHUNKS - 1)
                    pe.wait_ge(pv_lo, CHUNKS)
                if n == 22:
                    pe.wait_ge(gw_loaded, 16)
                if 22 <= n < 26:
                    lru_gates(2 * (n - 22))
                    lru_gates(2 * (n - 22) + 1)
                if OA_TILES <= n < G_TILES:
                    tile(n, y_hi, y_lo)
                else:
                    tile(n, x_hi, x_lo)
                if n < OA_TILES:
                    for c in chunks_at(n):
                        turn_probs(c)

            def stage(first, rounds, right_hi, right_lo):
                with pe.Fori(0, rounds) as it:
                    for c in range(4):
                        tile(first + c, right_hi, right_lo, it)

            pe.wait_ge(y_lo_ready, KB)
            stage(OL_TILES, 2, y_hi, y_lo)
            stage(GATE_TILES, 4, x_hi, x_lo)
            pe.wait_ge(m_lo_ready, KB)
            stage(OUT_TILES, 2, y_hi, y_lo)
            sum_squares(lru_in[:, :, 0:T], 1)
            pe.wait_ge(xlo_ready, 2)
            pe.wait_ge(keys_loaded, 16)

            def key_scores(it, c):
                pe.wait_ge(bank_free, it * 4 + (PQ_TILES + c + 1))
                pe.wait_ge(s_evac, it * 4 + max(c - 1, 0))
                for b in range(TBLOCKS):
                    last = mm(bank[2 + c % 2][:, P * b:P * (b + 1)], q_pk[:, c % 2, P * b:P * (b + 1)],
                              keys[:, bass.ds(it * 4 + c, 1), :], start=True, stop=True)
                last.then_inc(s_mm, 1)

            with pe.Fori(0, 4) as it:
                for c in range(4):
                    tile(PQ_TILES + c, x_hi, x_lo, it)
                    if c:
                        key_scores(it, c - 1)
                key_scores(it, 3)

            with pe.Fori(0, TBLOCKS) as it:
                for c in range(16):
                    tile(U_TILES + c, x_hi, x_lo, it, 16)
                pe.wait_ge(sel_ready, it + 1)
                for k in range(3):
                    last = nc.tensor.transpose(bank[4][:, P * k:P * (k + 1)], sel[:, k, :], ident)
                last.then_inc(sel_t, 1)

            pe.sem_inc(tok_done, TOK0)
            with pe.Fori(0, 8) as it:
                for c in range(8):
                    tile(U_TILES + 64 + c, x_hi, x_lo, it, 8)
                    k = (c // 2) % 2
                    pe.wait_ge(onehot_ready, it * 4 + (c // 2 + 1))
                    for h in range(2):
                        pe.wait_ge(g_evac, it * 16 + max(2 * c + h - 1, 0))
                        for t in range(4):
                            at = 8 * (c % 2) + 4 * h + t
                            for n in range(3):
                                last = mm(bank[2 + h][:, P * t:P * (t + 1)], eq_j[:, k, :, at],
                                          gi[n][:, k, :, at], start=(n == 0), stop=(n == 2))
                        last.then_inc(tok_done, 1)

            def experts(it, first, final):
                for c in range(8):
                    k = c // 4
                    if isinstance(it, int):
                        off = it * 8 + V_TILES + c
                        group = it * 2 + k + 1
                    else:
                        off = it * 8 + (V_TILES + c)
                        group = it * 2 + (k + 1)
                    pe.wait_ge(hi_ready, off + 1)
                    if c % 4 == 0:
                        pe.wait_ge(e_lo_ready, group)
                    start, stop = first and c == 0, final and c == 7
                    for m in range(KB):
                        w = w_hi[:, c % 2, P * m:P * (m + 1)]
                        mm(bank[m][:], w, e_hi[:, k, c % 4, :], start=start, stop=False)
                        mm(bank[m][:], w, e_lo[:, k, c % 4, :], start=False, stop=False)
                    pe.wait_ge(lo_ready, off + 1)
                    for m in range(KB):
                        last = mm(bank[m][:], w_lo[:, c % 2, P * m:P * (m + 1)],
                                  e_hi[:, k, c % 4, :], start=False, stop=stop)
                    last.then_inc(tile_done, 1)

            pe.wait_ge(bank_free, V_TILES)
            pe.wait_ge(g_evac, T // 4)
            experts(0, True, False)
            with pe.Fori(1, 15) as it:
                experts(it, False, False)
            experts(15, False, True)


_NAMES = ["x_t", "dense_w", "u_t", "v_t", "gates_w", "sub_keys", "vecs", "rope", "mats"]


def _columns(a, n):
    return np.ascontiguousarray(np.asarray(a).reshape(n, P).T)


def _tiles(w):
    w = np.asarray(w)
    return w.reshape(KB, P, -1, P).transpose(2, 1, 0, 3).reshape(-1, P, D)


def _rope_tables():
    dim = HEAD_DIM // 4
    half = dim // 2
    inv = np.float32(500000.0) ** (-np.arange(0, dim, 2, dtype=np.float32) / np.float32(dim))
    ang = np.arange(T, dtype=np.float32)[None, :] * inv.astype(np.float32)[:, None]
    table = np.zeros((HEAD_DIM, 2, T), np.float32)
    table[:, 0] = 1.0
    table[0:half, 0] = table[half:dim, 0] = np.cos(ang)
    table[0:half, 1] = table[half:dim, 1] = np.sin(ang)
    return np.concatenate([table, table])


def _matrices():
    dim = HEAD_DIM // 4
    half = dim // 2
    swap = np.zeros((P, P), np.float32)
    for h in range(2):
        for d in range(half):
            a, b = HEAD_DIM * h + d, HEAD_DIM * h + half + d
            swap[b, a] = -1.0
            swap[a, b] = 1.0
    return np.ascontiguousarray(np.stack([np.eye(P, dtype=np.float32), swap], axis=1))


def kernel(**inputs):
    import concourse.bacc as bacc
    from concourse.bass_utils import run_bass_kernel_spmd

    a = {k: np.asarray(v) for k, v in inputs.items()}
    w_in, b_in = _tiles(a["w_in"][0]), a["b_in"][0].reshape(-1, P)
    dense_w = np.concatenate([
        w_in[W_IN_FIRST], _tiles(a["w_o_attn"][0]), w_in[W_IN_G], _tiles(a["w_o_lru"][0]),
        w_in[W_IN_GATES], _tiles(a["w_out"][0]), _tiles(a["peer_w_q"][0])])
    none = np.zeros((KB, P), np.float32)
    biases = np.concatenate([b_in[W_IN_FIRST], none, b_in[W_IN_G], none, b_in[W_IN_GATES], none,
                             a["peer_b_q"][0].reshape(-1, P)])
    gates_w = np.zeros((P, 2, KB, P), np.float32)
    for g, name in enumerate(("w_rg", "w_ig")):
        w = a[name][0].reshape(KB, 2, 64, 64)
        for h in range(2):
            gates_w[64 * h:64 * h + 64, g, :, 64 * h:64 * h + 64] = w[:, h].transpose(1, 0, 2)
    sinks = np.repeat(a["attn_sinks"][0].reshape(PAIRS, 2).T, CHUNK, axis=0)
    vecs = np.concatenate([
        biases.T, _columns(a["conv_w"][0], 32), _columns(a["conv_b"][0], 8), _columns(a["b_rg"][0], 8),
        _columns(a["b_ig"][0], 8), _columns(a["lru_L"][0], 8), _columns(a["norm_mix_g"][0], 8),
        _columns(a["norm_ffn_g"][0], 8), np.tile(a["q_norm_g"][0], 2)[:, None],
        np.tile(a["k_norm_g"][0], 2)[:, None], sinks], axis=1)
    arrays = {
        "x_t": a["x"][0].T.reshape(KB, P, T).transpose(1, 0, 2),
        "dense_w": dense_w,
        "u_t": a["peer_u"][0].reshape(N_KEYS, N_KEYS, KB, P).transpose(0, 3, 2, 1).reshape(N_KEYS, P, D),
        "v_t": a["peer_v"][0].reshape(N_KEYS, P, D),
        "gates_w": gates_w.reshape(P, 2, D),
        "sub_keys": a["peer_sub_keys"][0].reshape(16, N_KEYS, P).transpose(2, 0, 1),
        "vecs": vecs,
        "rope": _rope_tables(),
        "mats": _matrices(),
    }
    arrays = {k: np.ascontiguousarray(v) for k, v in arrays.items()}
    nc = bacc.Bacc("TRN2", target_bir_lowering=False, num_devices=1)
    aps = [nc.dram_tensor(n, arrays[n].shape, F32, kind="ExternalInput").ap() for n in _NAMES]
    out = nc.dram_tensor("out", [P, KB, T], F32, kind="ExternalOutput").ap()
    build(nc, *aps, out)
    r = run_bass_kernel_spmd(nc, [arrays], core_ids=[0])
    y = np.asarray(r.results[0]["out"])
    return np.ascontiguousarray(y.transpose(2, 1, 0).reshape(1, T, D))
```

```python
from contextlib import ExitStack

import numpy as np

import concourse.bass as bass
from concourse import mybir

F32 = mybir.dt.float32
F32R = mybir.dt.float32r
BF16 = mybir.dt.bfloat16
U16 = mybir.dt.uint16
ALU = mybir.AluOpType
ACT = mybir.ActivationFunctionType
X = mybir.AxisListType.X

P = 128
T = 512
D = 1024
KB = D // P
EPS = 1e-6
CHUNK = 64
HEAD_DIM = 64
N_KV = 4
PAIRS = 8
CHUNKS = T // CHUNK
LRU_C = 8.0
N_KEYS = 128
TOPK = 16
PEER_HEADS = 8
TBLOCKS = T // P
LOWEST = -3.0e38

KV_TILES, Q_TILES, X_TILES = 0, 4, 12
OA_TILES, G_TILES, OL_TILES = 20, 28, 36
GATE_TILES, OUT_TILES, PQ_TILES = 44, 60, 68
U_TILES, V_TILES = 84, 212
ALL_TILES = 340
BASE = 8
DMA_BASE = 16
W_IN_FIRST = [24, 25, 26, 27] + list(range(16, 24)) + list(range(0, 8))
W_IN_G = list(range(8, 16))
W_IN_GATES = [c for m in range(8) for c in (36 + m, 28 + m)]

_WIDTHS = [("b_in", 84), ("conv_w", 32), ("conv_b", 8), ("b_rg", 8), ("b_ig", 8), ("lru_L", 8),
           ("g_mix", 8), ("g_ffn", 8), ("g_q", 1), ("g_k", 1), ("sinks", 8)]
VEC = {}
_at = 0
for _name, _w in _WIDTHS:
    VEC[_name] = _at
    _at += _w
N_VEC = _at


class Steps:

    def __init__(self, eng, sem):
        self.eng, self.sem, self.n = eng, sem, 0

    def do(self, instruction):
        instruction.then_inc(self.sem, 1)
        self.n += 1
        return self.n

    def wait(self, n=None):
        self.eng.wait_ge(self.sem, n or self.n)

    def restart(self):
        if self.n:
            self.eng.wait_ge(self.sem, self.n)
            self.eng.sem_inc(self.sem, -self.n)
            self.n = 0


def build(nc, x_t, dense_w, u_t, v_t, gates_w, sub_keys, vecs, rope, mats, out):
    act_dram = nc.dram_tensor("act_scratch", [32, P, 4 * T], F32, kind="Internal").ap()
    g_dram = nc.dram_tensor("g_scratch", [16, P, P * 32], F32, kind="Internal").ap()

    with ExitStack() as ctx:
        def sb(name, shape, dt, scope=ctx):
            return scope.enter_context(nc.sbuf_tensor(name, shape, dt))

        def sem(name):
            return ctx.enter_context(nc.semaphore(name))

        bank = [ctx.enter_context(nc.psum_tensor(f"bank{i}", [P, 512], F32)) for i in range(8)]
        SC0, SC1, TR0, TR1, PV, MI = 2, 3, 4, 5, 6, 7

        raw = sb("raw", [P, 4, D], F32)
        w_hi = sb("w_hi", [P, 2, D], F32R)
        w_lo = sb("w_lo", [P, 2, D], F32R)
        vec = sb("vec", [P, N_VEC], F32)
        mat = sb("mat", [P, 2, P], F32)
        ident, rot = mat[:, 0, :], mat[:, 1, :]
        ones = sb("ones", [P, P], F32)
        stat = sb("stat", [P, T], F32)

        front = ExitStack()
        x_hi = sb("x_hi", [P, KB, T], F32R, front)
        x_lo = sb("x_lo", [P, KB, T], F32R, front)
        xc = sb("xc", [P, KB, T], F32, front)
        buf_a = sb("buf_a", [P, KB, T], F32, front)
        lru_in = sb("lru_in", [P, KB, T + 3], F32, front)
        y_hi = sb("y_hi", [P, KB, T], F32R, front)
        y_lo = sb("y_lo", [P, KB, T], F32R, front)
        blocks = sb("blocks", [P, P], F32, front)
        tmp = sb("tmp", [P, 2, T], F32, front)
        tmp2 = sb("tmp2", [P, 2, T], F32, front)
        lam = sb("lam", [P, 8, 8], F32, front)
        attn = ExitStack()
        kdup = sb("kdup", [P, N_KV, T], F32, attn)
        v_raw = sb("v_raw", [P, 2, T], F32, attn)
        vwin = sb("vwin", [P, CHUNKS, 2 * P], F32, attn)
        ropes = sb("ropes", [P, 2, T], F32, attn)
        prob = sb("prob", [P, PAIRS, P], F32, attn)
        prob_t = sb("prob_t", [P, PAIRS, P], F32, attn)
        soft = sb("soft", [P, 6, PAIRS], F32, attn)
        attn.close()
        lru = ExitStack()
        rb = sb("rb", [P, KB, T], F32, lru)
        gw = sb("gw", [P, 2, D], F32, lru)
        ib = lru_in[:, :, 3:3 + T]
        lru.close()
        front.close()

        peer = ExitStack()
        act_out = sb("act_out", [P, 2, 4, T], F32, peer)
        g_in = sb("g_in", [P, 2, 16, 4, 32], F32, peer)
        x1 = sb("x1", [P, KB, T], F32, peer)
        h_hi = sb("h_hi", [P, KB, T], F32R, peer)
        h_lo = sb("h_lo", [P, KB, T], F32R, peer)
        rout = ExitStack()
        q_pk = sb("q_pk", [P, 2, T], F32, rout)
        keys = sb("keys", [P, 2 * PEER_HEADS, N_KEYS], F32, rout)
        iota_e = sb("iota_e", [P, N_KEYS, 16], BF16, rout)
        iota_k = sb("iota_k", [P, 16], BF16, rout)
        i_t = sb("i_t", [P, T], BF16, rout)
        j_t = sb("j_t", [P, T], BF16, rout)
        g_t = [sb(f"g_t{n}", [P, T], BF16, rout) for n in range(3)]
        topk = ExitStack()
        s = sb("s", [P, TBLOCKS, 2 * PEER_HEADS, N_KEYS], F32, topk)
        queries = ExitStack()
        xg = sb("xg", [P, KB, T], F32, queries)
        queries.close()
        s_blk = sb("s_blk", [P, 2 * PEER_HEADS, N_KEYS], F32, topk)
        s_rest = sb("s_rest", [P, 2, N_KEYS], F32, topk)
        top_s = sb("top_s", [P, 2, 16], F32, topk)
        top_i = sb("top_i", [P, PEER_HEADS, 2, 16], U16, topk)
        top_f = sb("top_f", [P, PEER_HEADS, 2, 16], BF16, topk)
        cand = sb("cand", [P, 16, 16], F32, topk)
        cand_rest = sb("cand_rest", [P, 256], F32, topk)
        best = sb("best", [P, PEER_HEADS, 16], F32, topk)
        pos = sb("pos", [P, PEER_HEADS * 16], U16, topk)
        half_i = sb("half_i", [P, 2, P], U16, topk)
        half_f = sb("half_f", [P, 2, P], BF16, topk)
        pick = sb("pick", [P, 2, P, 16], BF16, topk)
        sel = sb("sel", [P, 3, P], F32, topk)
        g_rest = sb("g_rest", [P, 2, P], F32, topk)
        esum = sb("esum", [P, 2, PEER_HEADS], F32, topk)
        topk.close()
        scat = ExitStack()
        eq_i = sb("eq_i", [P, N_KEYS, 16], BF16, scat)
        eq_j = sb("eq_j", [P, 2, N_KEYS, 16], BF16, scat)
        gi = [sb(f"gi{n}", [P, 2, N_KEYS, 16], BF16, scat) for n in range(3)]
        g_out = sb("g_out", [P, 2, N_KEYS, 32], F32, scat)
        scat.close()
        act_in = sb("act_in", [P, 2, 4, T], F32, rout)
        e_hi = sb("e_hi", [P, 2, 4, T], F32R, rout)
        e_lo = sb("e_lo", [P, 2, 4, T], F32R, rout)
        rout.close()
        peer.close()

        raw_ready = [sem(f"raw_ready{i}") for i in range(4)]
        hi_ready, lo_ready = sem("hi_ready"), sem("lo_ready")
        tile_done = sem("tile_done")
        bank_free = sem("bank_free")
        x_loaded = [sem(f"x_loaded{k}") for k in range(KB)]
        vec_loaded, mat_loaded = sem("vec_loaded"), sem("mat_loaded")
        rope_loaded, gw_loaded = sem("rope_loaded"), sem("gw_loaded")
        x1_loaded, keys_loaded = sem("x1_loaded"), sem("keys_loaded")
        consts_ready, iota_ready = sem("consts_ready"), sem("iota_ready")
        act_step, dve_step = sem("act_step"), sem("dve_step")
        sq_ready, sq_read, ss_ready, ms_ready, sum_ready = (
            sem("sq_ready"), sem("sq_read"), sem("ss_ready"), sem("ms_ready"), sem("sum_ready"))
        xg_ready, xg_hi, xg_lo = sem("xg_ready"), sem("xg_hi"), sem("xg_lo")
        rms_ready, xn_ready, xhi_ready, xlo_ready = (
            sem("rms_ready"), sem("xn_ready"), sem("xhi_ready"), sem("xlo_ready"))
        kv_biased, q_ready = sem("kv_biased"), sem("q_ready")
        head_raw, head_gained, head_mm = sem("head_raw"), sem("head_gained"), sem("head_mm")
        head_ms, head_rms, head_done = sem("head_ms"), sem("head_rms"), sem("head_done")
        v_evac, vt_ready, vt_evac = sem("v_evac"), sem("vt_ready"), sem("vt_evac")
        scores_ready, scores_read, shifted = sem("scores_ready"), sem("scores_read"), sem("shifted")
        exp_ready, probs_ready = sem("exp_ready"), sem("probs_ready")
        pt_psum, pt_ready, pv_ready, pv_hi, pv_lo = (
            sem("pt_psum"), sem("pt_ready"), sem("pv_ready"), sem("pv_hi"), sem("pv_lo"))
        lru_evac, conv_ready, gate_mm, gate_sig = (
            sem("lru_evac"), sem("conv_ready"), sem("gate_mm"), sem("gate_sig"))
        lam_e, lam_ready = sem("lam_e"), sem("lam_ready")
        gated, decay_ready, square_ready, root_ready, h_ready = (
            sem("gated"), sem("decay_ready"), sem("square_ready"), sem("root_ready"), sem("h_ready"))
        gelu_ready, y_ready, y_hi_ready, y_lo_ready = (
            sem("gelu_ready"), sem("y_ready"), sem("y_hi_ready"), sem("y_lo_ready"))
        sig_ready, merged_ready, m_hi_ready, m_lo_ready = (
            sem("sig_ready"), sem("merged_ready"), sem("m_hi_ready"), sem("m_lo_ready"))
        s_mm, s_evac, best_ready, gexp_ready, sel_ready, sel_t, sel_evac = (
            sem("s_mm"), sem("s_evac"), sem("best_ready"), sem("gexp_ready"), sem("sel_ready"),
            sem("sel_t"), sem("sel_evac"))
        onehot_ready, tok_done, g_evac = sem("onehot_ready"), sem("tok_done"), sem("g_evac")
        act_stored = [sem(f"act_stored{i}") for i in range(2)]
        g_stored = [sem(f"g_stored{i}") for i in range(2)]
        act_loaded = [sem(f"act_loaded{i}") for i in range(2)]
        g_loaded = [sem(f"g_loaded{i}") for i in range(2)]
        e_ready, e_hi_ready, e_lo_ready = sem("e_ready"), sem("e_hi_ready"), sem("e_lo_ready")
        bank_done, out_ready, out_stored = sem("bank_done"), sem("out_ready"), sem("out_stored")

        block = ctx.enter_context(nc.Block())

        def window(c):
            return (0, CHUNK) if c == 0 else (CHUNK * (c - 1), 2 * CHUNK)

        def chunks_at(n):
            first = X_TILES + 2
            if n == OA_TILES:
                return range(n - first, CHUNKS)
            return [n - first] if first <= n < OA_TILES else []

        def col(name, m=0):
            return vec[:, VEC[name] + m:VEC[name] + m + 1]

        @block.sync
        def _(sp):
            sp.dma_start(vec[:], vecs).then_inc(vec_loaded, 16)
            for k in range(KB):
                sp.dma_start(buf_a[:, k, :], x_t[:, k, :]).then_inc(x_loaded[k], 16)
                if k == 1:
                    sp.dma_start(raw[:, 0, :], dense_w[0]).then_inc(raw_ready[0], 16)

            def load_tiles(source, it, base, n=4):
                for c in range(n):
                    if isinstance(it, int) and base + n * it + c < 4:
                        pass
                    else:
                        sp.wait_ge(hi_ready, it * n + (base + c - 3))
                        sp.wait_ge(lo_ready, it * n + (base + c - 3))
                    sp.dma_start(raw[:, c % 4, :], source[it * n + c]).then_inc(raw_ready[c % 4], 16)

            for n in range(1, 4):
                sp.dma_start(raw[:, n, :], dense_w[n]).then_inc(raw_ready[n], 16)
            sp.dma_start(mat[:], mats).then_inc(mat_loaded, 16)
            sp.dma_start(ropes[:], rope).then_inc(rope_loaded, 16)
            with sp.Fori(1, 6) as it:
                load_tiles(dense_w, it, 0)
            sp.wait_ge(pv_lo, CHUNKS)
            sp.dma_start(gw[:], gates_w).then_inc(gw_loaded, 16)
            with sp.Fori(6, 11) as it:
                load_tiles(dense_w, it, 0)
            sp.wait_ge(h_ready, 8)
            sp.dma_start(x1[:], x_t).then_inc(x1_loaded, 16)
            with sp.Fori(11, 18) as it:
                load_tiles(dense_w, it, 0)
            sp.wait_ge(tile_done, PQ_TILES)
            sp.dma_start(keys[:], sub_keys).then_inc(keys_loaded, 16)
            with sp.Fori(18, 21) as it:
                load_tiles(dense_w, it, 0)

            def load_group(it, k):
                if not (isinstance(it, int) and it == 0):
                    sp.wait_ge(e_lo_ready, it * 2 + (k - 1))
                sp.dma_start(act_in[:, k, :, :], act_dram[it * 2 + k]
                             .rearrange("p (c t) -> p c t", c=4)).then_inc(act_loaded[k], 16)
                src = g_dram[:, :, bass.ds(it * 256 + k * 128, 128)]
                sp.dma_start(g_in[:, k, :, :, :].rearrange("p b c t -> p b (c t)"),
                             src.rearrange("b p n -> p b n")).then_inc(g_loaded[k], 16)

            with sp.Fori(0, 26) as it:
                load_tiles(u_t, it, U_TILES)
            for k in range(2):
                sp.wait_ge(act_stored[k], DMA_BASE + 16 * 8)
                sp.wait_ge(g_stored[k], DMA_BASE + 16 * 8)
            sp.wait_ge(tok_done, BASE + T // 4)
            load_group(0, 0)
            load_group(0, 1)
            with sp.Fori(26, 32) as it:
                load_tiles(u_t, it, U_TILES)
            load_tiles(v_t, 0, V_TILES)
            load_tiles(v_t, 1, V_TILES)
            for k in range(2):
                sp.wait_ge(act_stored[k], DMA_BASE + 16 * 16)
            with sp.Fori(1, 16) as it:
                for k in range(2):
                    load_group(it, k)
                    for c in range(4):
                        sp.wait_ge(hi_ready, it * 8 + (V_TILES + 4 * k + c - 3))
                        sp.wait_ge(lo_ready, it * 8 + (V_TILES + 4 * k + c - 3))
                        sp.dma_start(raw[:, c, :], v_t[it * 8 + (4 * k + c)]).then_inc(raw_ready[c], 16)
            for m in range(KB):
                sp.wait_ge(out_ready, m + 1)
                sp.dma_start(out[:, m, :], x1[:, m, :]).then_inc(out_stored, 16)
            sp.wait_ge(out_stored, 16 * KB)

        @block.gpsimd
        def _(pool):
            def lo(it, base, c):
                pool.wait_ge(hi_ready, it * 4 + (base + c + 1))
                if not (isinstance(it, int) and c < 2):
                    pool.wait_ge(tile_done, it * 4 + (base + c - 1))
                pool.tensor_tensor(w_lo[:, c % 2, :], raw[:, c, :], w_hi[:, c % 2, :].bitcast(F32),
                                   ALU.subtract).then_inc(lo_ready, 1)

            for c in range(4):
                lo(0, 0, c)
            with pool.Fori(1, 18) as it:
                for c in range(4):
                    lo(it, 0, c)
            pool.wait_ge(tile_done, PQ_TILES)
            nc.gpsimd.iota(iota_k[:], pattern=[[1, 16]], base=0, channel_multiplier=0,
                           allow_small_or_imprecise_dtypes=True)
            nc.gpsimd.iota(iota_e[:], pattern=[[1, N_KEYS], [0, 16]], base=0, channel_multiplier=0,
                           allow_small_or_imprecise_dtypes=True).then_inc(iota_ready, 1)
            with pool.Fori(18, 85) as it:
                for c in range(4):
                    lo(it, 0, c)

        @block.scalar
        def _(act):
            act.sem_inc(merged_ready, BASE)
            for k in range(2):
                act.sem_inc(act_stored[k], DMA_BASE)
                act.sem_inc(g_stored[k], DMA_BASE)
            step = Steps(act, act_step)

            def hi(n, it=None, slot=None):
                slot = n % 4 if slot is None else slot
                if it is None:
                    act.wait_ge(raw_ready[slot], 16 * (n // 4 + 1))
                    if n >= 2:
                        act.wait_ge(tile_done, n - 1)
                else:
                    a, per = it
                    act.wait_ge(raw_ready[slot], a * (4 * per) + 16 * (n // 4 + 1))
                    act.wait_ge(tile_done, a * per + (n - 1))
                nc.scalar.activation(w_hi[:, slot % 2, :], raw[:, slot, :], ACT.Copy).then_inc(hi_ready, 1)

            def squares(src, k, first, ready, value):
                act.wait_ge(ready, value)
                if k >= 2:
                    act.wait_ge(sq_read, KB * first + k - 1)
                elif first:
                    act.wait_ge(m_lo_ready, BASE + KB)
                nc.scalar.activation(tmp2[:, k % 2, :], src[:, k, :], ACT.Square).then_inc(sq_ready, 1)

            def gained_upper(k, first):
                src, dst = (xg, x_hi) if first else (lru_in[:, :, 0:T], y_hi)
                act.wait_ge(xg_ready, KB * first + k + 1)
                nc.scalar.activation(dst[:, k, :], src[:, k, :], ACT.Copy).then_inc(xg_hi, 1)

            def rms_root(first):
                act.wait_ge(ms_ready, first + 1)
                nc.scalar.activation(stat[:], stat[:], ACT.Sqrt).then_inc(rms_ready, 1)

            def normed_upper(k, first):
                src, dst = (xg, h_hi) if first else (lru_in[:, :, 0:T], x_hi)
                act.wait_ge(xn_ready, KB * first + k + 1)
                nc.scalar.activation(dst[:, k, :], src[:, k, :], ACT.Copy).then_inc(xhi_ready, 1)

            act.wait_ge(vec_loaded, 16)
            for k in range(KB):
                squares(buf_a, k, 0, x_loaded[k], 16)
                gained_upper(k, 0)
                if k == 1:
                    hi(0)
            rms_root(0)

            def evac(n):
                ps, b = bank[n % 2][:], col("b_in", n)
                if n < Q_TILES:
                    act.wait_ge(bank_free, n + 1)
                    dst = tmp[:, n, :] if n < 2 else v_raw[:, n - 2, :]
                    if n < 2:
                        step.wait(step.do(nc.scalar.activation(tmp2[:, n, :], dst, ACT.Square, bias=b)))
                    nc.scalar.activation(dst, dst, ACT.Identity, bias=b).then_inc(kv_biased, 1)
                elif n < X_TILES:
                    j = n - 2
                    act.wait_ge(head_done, j - 1)
                    nc.scalar.activation(tmp2[:, j % 2, :], ps, ACT.Square, bias=b)
                    nc.scalar.activation(buf_a[:, n - Q_TILES, :], ps, ACT.Identity, bias=b)\
                        .then_inc(bank_free, 1)
                elif n < OA_TILES:
                    m = n - X_TILES
                    nc.scalar.activation(lru_in[:, m, 3:3 + T], ps, ACT.Identity, bias=b).then_inc(bank_free, 1)
                elif n < G_TILES:
                    nc.scalar.activation(buf_a[:, n - OA_TILES, :], ps, ACT.Copy).then_inc(bank_free, 1)
                elif n < OL_TILES:
                    m = n - G_TILES
                    if m >= 2:
                        act.wait_ge(y_ready, m - 1)
                    nc.scalar.activation(tmp[:, m % 2, :], ps, ACT.Gelu_apprx_tanh, bias=b)\
                        .then_inc(bank_free, 1)

            def head_root(j):
                act.wait_ge(head_ms, j + 1)
                nc.scalar.activation(tmp2[:, j % 2, :], tmp2[:, j % 2, :], ACT.Sqrt).then_inc(head_rms, 1)

            def softmax(c):
                _, kw = window(c)
                act.wait_ge(shifted, c + 1)
                nc.scalar.activation(prob[:, :, 0:kw], prob[:, :, 0:kw], ACT.Exp)
                nc.scalar.activation(soft[:, 2, :], soft[:, 1, :], ACT.Exp).then_inc(exp_ready, 1)

            def probs_turned(c):
                _, kw = window(c)
                act.wait_ge(pt_psum, c + 1)
                if c:
                    act.wait_ge(pv_ready, c)
                for g in range(2):
                    last = nc.scalar.activation(prob_t[0:kw, 4 * g:4 * g + 4, :], bank[TR0 + g][0:kw, :]
                                                .rearrange("p (a q) -> p a q", a=4), ACT.Copy)
                last.then_inc(pt_ready, 1)

            def attention_out(c):
                act.wait_ge(pv_ready, c + 1)
                nc.scalar.activation(y_hi[:, :, CHUNK * c:CHUNK * (c + 1)],
                                     bank[PV][:].rearrange("p (a q) -> p a q", a=PAIRS),
                                     ACT.Copy).then_inc(pv_hi, 1)

            def gate_sigmoids(m):
                b0 = (SC0, TR0)[m % 2]
                act.wait_ge(gate_mm, m + 1)
                nc.scalar.activation(rb[:, m, :], bank[b0][:], ACT.Sigmoid, bias=col("b_rg", m))
                nc.scalar.activation(ib[:, m, :], bank[b0 + 1][:], ACT.Sigmoid, bias=col("b_ig", m))\
                    .then_inc(gate_sig, 1)

            def decay(m):
                act.wait_ge(gated, m + 1)
                step.wait(step.do(nc.scalar.activation(xc[:, m, :], rb[:, m, :], ACT.Tanh,
                                                       scale=lam[:, 6, m:m + 1])))
                nc.scalar.activation(rb[:, m, :], rb[:, m, :], ACT.Exp, scale=lam[:, 7, m:m + 1])\
                    .then_inc(decay_ready, 1)

            def root(m):
                act.wait_ge(square_ready, m + 1)
                nc.scalar.activation(xc[:, m, :], xc[:, m, :], ACT.Sqrt).then_inc(root_ready, 1)

            def y_upper(m):
                act.wait_ge(y_ready, m + 1)
                nc.scalar.activation(y_hi[:, m, :], tmp2[:, m % 2, :], ACT.Copy).then_inc(y_hi_ready, 1)

            for n in range(OL_TILES + 1):
                hi(n + 1)
                if n >= 1:
                    act.wait_ge(tile_done, n)
                    if n == 4:
                        head_root(0)
                    evac(n - 1)
                if n in (1, 2):
                    for k in range(4 * (n - 1), 4 * n):
                        normed_upper(k, 0)
                if n == 2:
                    act.wait_ge(lam_e, 1)
                    nc.scalar.activation(lam[:, 1, :], lam[:, 0, :], ACT.Exp).then_inc(lam_e, 1)
                if 5 <= n < 14:
                    head_root(n - 4)
                for c in chunks_at(n):
                    softmax(c)
                    if c:
                        attention_out(c - 1)
                    probs_turned(c)
                    if c == CHUNKS - 1:
                        attention_out(c)
                if n == OA_TILES:
                    act.wait_ge(lam_ready, 1)
                if n in (22, 23, 24, 25):
                    gate_sigmoids(2 * (n - 22))
                    gate_sigmoids(2 * (n - 22) + 1)
                if n in (26, 27):
                    for m in range(4 * (n - 26), 4 * (n - 26) + 4):
                        decay(m)
                if n == 28:
                    for m in range(8):
                        root(m)
                if n >= G_TILES + 2:
                    y_upper(n - G_TILES - 2)
            y_upper(7)

            def ol_body(it, c):
                nc.scalar.activation(rb[:, bass.ds(it * 4 + c, 1), :], bank[c % 2][:]
                                     .rearrange("p (a t) -> p a t", a=1), ACT.Copy).then_inc(bank_free, 1)

            def shifted_loop(first, rounds, body):
                with act.Fori(0, rounds) as it:
                    for c in range(4):
                        hi(first + c + 2, (it, 4), (c + 2) % 4)
                        act.wait_ge(tile_done, it * 4 + (first + c + 1))
                        act.wait_ge(vec_loaded, 16)
                        body(it, c)

            shifted_loop(OL_TILES, 2, ol_body)

            def gate_body(it, c):
                b = vec[:, bass.ds(it * 4 + (VEC["b_in"] + GATE_TILES + c), 1)]
                act.wait_ge(merged_ready, it * 2 + (BASE + c // 2))
                act.wait_ge(vec_loaded, 16)
                nc.scalar.activation(tmp[:, c % 2, :], bank[c % 2][:], ACT.Sigmoid, bias=b)\
                    .then_inc(bank_free, 1)
                if c % 2:
                    act.wait_ge(merged_ready, it * 2 + (BASE + c // 2 + 1))
                    act.wait_ge(vec_loaded, 16)
                    nc.scalar.activation(y_hi[:, bass.ds(it * 2 + c // 2, 1), :],
                                         tmp2[:, 0:1, :], ACT.Copy).then_inc(m_hi_ready, 1)

            shifted_loop(GATE_TILES, 4, gate_body)
            for m in range(KB):
                hi(OUT_TILES + m + 2)
                squares(x1, m, 1, bank_free, OUT_TILES + m + 1)
                gained_upper(m, 1)
            rms_root(1)

            def query_bias(n, c, b):
                act.wait_ge(bank_free, n + PQ_TILES)
                act.wait_ge(vec_loaded, 16)
                nc.scalar.activation(q_pk[:, c % 2, :], q_pk[:, c % 2, :], ACT.Identity, bias=b)\
                    .then_inc(q_ready, 1)

            for c in range(4):
                hi(PQ_TILES + c + 2)
                query_bias(c + 1, c, col("b_in", PQ_TILES + c))
                for k in range(2 * c, 2 * c + 2):
                    normed_upper(k, 1)
            with act.Fori(1, 4) as it:
                for c in range(4):
                    hi(PQ_TILES + c + 2, (it, 4), (c + 2) % 4)
                    query_bias(it * 4 + (c + 1), c, vec[:, bass.ds(it * 4 + (VEC["b_in"] + PQ_TILES + c), 1)])

            def gelu(it, per, base, c):
                k = (c // 4) % 2
                if c % 4 == 0:
                    act.wait_ge(act_stored[k], it * (2 * per) + (DMA_BASE + 2 * base + 16 * (c // 8)))
                    act.wait_ge(vec_loaded, 16)
                nc.scalar.activation(act_out[:, k, c % 4, :], bank[c % 2][:], ACT.Gelu_apprx_tanh)\
                    .then_inc(bank_free, 1)
                if c % 4 == 3:
                    act.wait_ge(bank_free, it * per + (U_TILES + base + c + 1))
                    nc.scalar.dma_start(act_dram[it * (per // 4) + (base // 4 + c // 4)],
                                        act_out[:, k, :, :].rearrange("p c t -> p (c t)"))\
                        .then_inc(act_stored[k], 16)

            with act.Fori(0, 4) as it:
                for c in range(16):
                    hi(U_TILES + c + 2, (it, 16), (c + 2) % 4)
                    act.wait_ge(tile_done, it * 16 + (U_TILES + c + 1))
                    gelu(it, 16, 0, c)
                    if c == 11:
                        act.wait_ge(best_ready, it + 1)
                        nc.scalar.activation(best[:], best[:], ACT.Exp).then_inc(gexp_ready, 1)

            with act.Fori(0, 4) as it:
                for c in range(8):
                    hi(U_TILES + 64 + c + 2, (it, 8), (c + 2) % 4)
                    act.wait_ge(tile_done, it * 8 + (U_TILES + 64 + c + 1))
                    gelu(it, 8, 64, c)
                    k = (c // 2) % 2
                    if c % 2 == 0:
                        act.wait_ge(g_stored[k], it * 32 + (DMA_BASE + 16 * (c // 4)))
                        act.wait_ge(vec_loaded, 16)
                    for h in range(4):
                        act.wait_ge(tok_done, it * 32 + (BASE + 4 * c + h + 1))
                        t0 = 16 * (c % 2) + 4 * h
                        nc.scalar.activation(g_out[:, k, :, t0:t0 + 4].rearrange("p i t -> p t i"),
                                             bank[2 + h][:].rearrange("p (t i) -> p t i", t=4),
                                             ACT.Copy).then_inc(g_evac, 1)
                    if c % 2 == 1:
                        act.wait_ge(g_evac, it * 32 + (BASE + 4 * c + 4))
                        nc.scalar.dma_start(g_dram[it * 4 + c // 2],
                                            g_out[:, k, :, :].rearrange("p i t -> p (i t)"))\
                            .then_inc(g_stored[k], 16)

            def last_tiles(first):
                with act.Fori(0, 2) as it:
                    for c in range(8):
                        hi(U_TILES + first + c + 2, (it, 8), (c + 2) % 4)
                        act.wait_ge(tile_done, it * 8 + (U_TILES + first + c + 1))
                        gelu(it, 8, first, c)

            last_tiles(96)
            act.wait_ge(e_ready, 1)
            nc.scalar.activation(e_hi[:, 0, :, :], act_in[:, 0, :, :], ACT.Copy).then_inc(e_hi_ready, 1)
            last_tiles(112)
            with act.Fori(0, 15) as it:
                for c in range(8):
                    hi(V_TILES + c + 2, (it, 8), (c + 2) % 4)
                    if c % 4 == 0:
                        k = (c // 4 + 1) % 2
                        act.wait_ge(tile_done, it * 8 + (V_TILES + 4 * (c // 4)))
                        act.wait_ge(e_ready, it * 2 + (c // 4 + 2))
                        nc.scalar.activation(e_hi[:, k, :, :], act_in[:, k, :, :], ACT.Copy)\
                            .then_inc(e_hi_ready, 1)
            for c in range(8):
                n = V_TILES + 120 + c
                if n + 2 < ALL_TILES:
                    hi(n + 2)
                if c == 0:
                    act.wait_ge(tile_done, n)
                    act.wait_ge(e_ready, 32)
                    nc.scalar.activation(e_hi[:, 1, :, :], act_in[:, 1, :, :], ACT.Copy)\
                        .then_inc(e_hi_ready, 1)

        @block.vector
        def _(dve):
            dve.sem_inc(m_lo_ready, BASE)
            dve.sem_inc(onehot_ready, BASE)
            dve.sem_inc(tok_done, BASE)
            step = Steps(dve, dve_step)
            v = nc.vector

            def chain(ins):
                step.wait(step.do(ins))

            chain(v.memset(ones[:], 1.0))
            chain(v.memset(blocks[:], 0.0))
            for h in range(2):
                chain(v.memset(blocks[64 * h:64 * h + 64, 64 * h:64 * h + 64], 1.0))
            v.memset(lam[:, 2, :], 0.0).then_inc(consts_ready, 1)

            def gain_block(src, k, first):
                dst = (xg if first else lru_in[:, :, 0:T])[:, k, :]
                v.tensor_scalar(dst, src[:, k, :], col(("g_mix", "g_ffn")[first], k), None, ALU.mult)\
                    .then_inc(xg_ready, 1)

            def gained_lower(k, first):
                src, hi_, lo_ = (xg, x_hi, x_lo) if first else (lru_in[:, :, 0:T], y_hi, y_lo)
                dve.wait_ge(xg_hi, KB * first + k + 1)
                v.tensor_tensor(lo_[:, k, :], src[:, k, :], hi_[:, k, :].bitcast(F32),
                                ALU.subtract).then_inc(xg_lo, 1)

            def add_square(k, first):
                dve.wait_ge(sq_ready, KB * first + k + 1)
                if k == 0:
                    v.tensor_copy(stat[:], tmp2[:, 0, :]).then_inc(sq_read, 1)
                else:
                    dve.wait_ge(sq_read, KB * first + k)
                    v.tensor_tensor(stat[:], stat[:], tmp2[:, k % 2, :], ALU.add).then_inc(sq_read, 1)

            def rms_mean(first):
                dve.wait_ge(ss_ready, first + 1)
                v.tensor_scalar(stat[:], bank[MI][:], 1.0 / D, EPS, ALU.mult, ALU.add).then_inc(ms_ready, 1)
                dve.wait_ge(rms_ready, first + 1)
                chain(v.reciprocal(stat[:], stat[:]))

            def norm_blocks(ks, first):
                src, hi_, lo_ = (xg, h_hi, h_lo) if first else (lru_in[:, :, 0:T], x_hi, x_lo)
                for k in ks:
                    dve.wait_ge(xg_lo, KB * first + k + 1)
                    v.tensor_tensor(src[:, k, :], src[:, k, :], stat[:], ALU.mult).then_inc(xn_ready, 1)
                for k in ks:
                    dve.wait_ge(xhi_ready, KB * first + k + 1)
                    v.tensor_tensor(lo_[:, k, :], src[:, k, :], hi_[:, k, :].bitcast(F32),
                                    ALU.subtract).then_inc(xlo_ready, 1)

            def kv_scale(n):
                dve.wait_ge(tile_done, n + 1)
                dst = tmp[:, n, :] if n < 2 else v_raw[:, n - 2, :]
                v.tensor_tensor(dst, bank[n % 2][:], stat[:], ALU.mult).then_inc(bank_free, 1)

            dve.wait_ge(vec_loaded, 16)
            for k in range(KB):
                dve.wait_ge(x_loaded[k], 16)
                gain_block(buf_a, k, 0)
                if k:
                    gained_lower(k - 1, 0)
                    add_square(k - 1, 0)
            gained_lower(KB - 1, 0)
            add_square(KB - 1, 0)
            rms_mean(0)

            def decay_rates():
                L = vec[:, VEC["lru_L"]:VEC["lru_L"] + 8]
                dve.wait_ge(vec_loaded, 16)
                chain(v.tensor_scalar(lam[:, 3, :], L, -1.0, None, ALU.mult))
                v.tensor_tensor(lam[:, 0, :], L, lam[:, 3, :], ALU.min).then_inc(lam_e, 1)
                dve.wait_ge(lam_e, 2)
                e, s_, z, poly = lam[:, 1, :], lam[:, 3, :], lam[:, 4, :], lam[:, 5, :]
                chain(v.tensor_scalar(s_, e, 2.0, None, ALU.add))
                chain(v.reciprocal(z, s_))
                chain(v.tensor_tensor(s_, e, z, ALU.mult))
                chain(v.tensor_tensor(z, s_, s_, ALU.mult))
                terms = 9
                chain(v.tensor_scalar(poly, z, 1.0 / (2 * terms + 1), 1.0 / (2 * terms - 1), ALU.mult, ALU.add))
                for n in range(terms - 2, -1, -1):
                    chain(v.tensor_tensor(poly, poly, z, ALU.mult))
                    chain(v.tensor_scalar(poly, poly, 1.0 / (2 * n + 1), None, ALU.add))
                chain(v.tensor_tensor(poly, poly, s_, ALU.mult))
                chain(v.tensor_scalar(poly, poly, 2.0, None, ALU.mult))
                chain(v.tensor_scalar(z, L, 0.0, None, ALU.min))
                chain(v.tensor_tensor(z, z, poly, ALU.subtract))
                chain(v.tensor_scalar(lam[:, 6, :], z, -LRU_C, None, ALU.mult))
                v.tensor_scalar(lam[:, 7, :], z, LRU_C, None, ALU.mult).then_inc(lam_ready, 1)

            def head_gain(j):
                dve.wait_ge(*((kv_biased, j + 1) if j < 2 else (bank_free, j + 3)))
                x = tmp[:, j % 2, :] if j < 2 else buf_a[:, j - 2, :]
                if j < 2:
                    v.tensor_scalar(x, x, col("g_k"), None, ALU.mult).then_inc(head_gained, 1)
                else:
                    v.tensor_scalar(x, x, col("g_q"), HEAD_DIM ** -0.5, ALU.mult, ALU.mult)\
                        .then_inc(head_gained, 1)

            def head_finish(j):
                x = tmp[:, j % 2, :] if j < 2 else buf_a[:, j - 2, :]
                root = tmp2[:, j % 2, :]
                dve.wait_ge(head_mm, j + 1)
                v.tensor_scalar(root, bank[TR0][:], 1.0 / HEAD_DIM, EPS, ALU.mult, ALU.add)\
                    .then_inc(head_ms, 1)
                if j == 0:
                    dve.wait_ge(rope_loaded, 16)
                chain(v.tensor_tensor(x, x, ropes[:, 0, :], ALU.mult))
                chain(v.tensor_tensor(xc[:, 0, :], bank[TR1][:], ropes[:, 1, :], ALU.mult))
                chain(v.tensor_tensor(x, x, xc[:, 0, :], ALU.add))
                dve.wait_ge(head_rms, j + 1)
                chain(v.reciprocal(root, root))
                if j < 2:
                    for h in range(2):
                        part = slice(64 * h, 64 * h + 64)
                        for to in range(2):
                            last = v.tensor_tensor(kdup[64 * to:64 * to + 64, 2 * j + h, :],
                                                   x[part, :], root[part, :], ALU.mult)
                            if (h, to) != (1, 1):
                                chain(last)
                else:
                    last = v.tensor_tensor(x, x, root, ALU.mult)
                last.then_inc(head_done, 1)

            def v_window(w):
                _, kw = window(w)
                dve.wait_ge(vt_ready, w + 1)
                v.tensor_copy(vwin[0:kw, w, :], bank[(MI, PV)[w % 2]][0:kw, 0:2 * P]).then_inc(vt_evac, 1)

            def conv(m):
                dve.wait_ge(bank_free, X_TILES + m + 1)
                w = [col("conv_w", 8 * k + m) for k in range(4)]
                chain(v.tensor_scalar(xc[:, m, :], lru_in[:, m, 3:3 + T], w[3], col("conv_b", m),
                                      ALU.mult, ALU.add))
                for k in range(3):
                    ins = v.scalar_tensor_tensor(out=xc[:, m, :], in0=lru_in[:, m, k:k + T], scalar=w[k],
                                                 in1=xc[:, m, :], op0=ALU.mult, op1=ALU.add)
                    if k < 2:
                        chain(ins)
                ins.then_inc(conv_ready, 1)

            def soft_shift(c):
                _, kw = window(c)
                dve.wait_ge(scores_ready, c + 1)
                sc = [bank[SC0 + g][:].rearrange("p (a k) -> p a k", a=4)[:, :, 0:kw] for g in range(2)]
                for g in range(2):
                    last = step.do(v.tensor_reduce(soft[:, 0, 4 * g:4 * g + 4], sc[g], X, ALU.max))
                step.wait(last)
                chain(v.tensor_tensor(soft[:, 0, :], soft[:, 0, :],
                                      vec[:, VEC["sinks"]:VEC["sinks"] + 8], ALU.max))
                if c:
                    dve.wait_ge(pt_psum, c)
                step.do(v.tensor_tensor(soft[:, 1, :], vec[:, VEC["sinks"]:VEC["sinks"] + 8],
                                        soft[:, 0, :], ALU.subtract))
                step.wait()
                for g in range(2):
                    mx = soft[:, 0, 4 * g:4 * g + 4].unsqueeze(2).to_broadcast([P, 4, kw])
                    last = v.tensor_tensor(prob[:, 4 * g:4 * g + 4, 0:kw], sc[g], mx, ALU.subtract)
                    if g == 0:
                        chain(last)
                last.then_inc(shifted, 1)

            def soft_norm(c):
                _, kw = window(c)
                dve.wait_ge(exp_ready, c + 1)
                chain(v.tensor_reduce(soft[:, 3, :], prob[:, :, 0:kw], X, ALU.add))
                chain(v.tensor_tensor(soft[:, 3, :], soft[:, 3, :], soft[:, 2, :], ALU.add))
                chain(v.reciprocal(soft[:, 4, :], soft[:, 3, :]))
                v.tensor_tensor(prob[:, :, 0:kw], prob[:, :, 0:kw],
                                soft[:, 4, :].unsqueeze(2).to_broadcast([P, PAIRS, kw]),
                                ALU.mult).then_inc(probs_ready, 1)

            def attention_lower(c):
                dve.wait_ge(pv_hi, c + 1)
                cols = slice(CHUNK * c, CHUNK * (c + 1))
                v.tensor_tensor(y_lo[:, :, cols], bank[PV][:].rearrange("p (a q) -> p a q", a=PAIRS),
                                y_hi[:, :, cols].bitcast(F32), ALU.subtract).then_inc(pv_lo, 1)

            def gate_input(m):
                dve.wait_ge(gate_sig, m + 1)
                v.tensor_tensor(ib[:, m, :], ib[:, m, :], xc[:, m, :], ALU.mult).then_inc(gated, 1)

            def square(m):
                dve.wait_ge(decay_ready, m + 1)
                if m:
                    dve.wait_ge(square_ready, m)
                chain(v.tensor_tensor(stat[:], rb[:, m, :], rb[:, m, :], ALU.mult))
                v.scalar_tensor_tensor(out=xc[:, m, :], in0=stat[:], scalar=1.0, in1=xc[:, m, :],
                                       op0=ALU.add, op1=ALU.mult).then_inc(square_ready, 1)

            def scan(m):
                dve.wait_ge(root_ready, m + 1)
                chain(v.tensor_tensor(ib[:, m, :], ib[:, m, :], xc[:, m, :], ALU.mult))
                v.tensor_tensor_scan(ib[:, m, :], rb[:, m, :], ib[:, m, :], 0.0,
                                     ALU.mult, ALU.add).then_inc(h_ready, 1)

            def lru_out(m):
                dve.wait_ge(bank_free, G_TILES + m + 1)
                dve.wait_ge(h_ready, 8)
                if m >= 2:
                    dve.wait_ge(y_lo_ready, m - 1)
                v.tensor_tensor(tmp2[:, m % 2, :], ib[:, m, :], tmp[:, m % 2, :], ALU.mult)\
                    .then_inc(y_ready, 1)

            def lru_lower(m):
                dve.wait_ge(y_hi_ready, m + 1)
                v.tensor_tensor(y_lo[:, m, :], tmp2[:, m % 2, :], y_hi[:, m, :].bitcast(F32),
                                ALU.subtract).then_inc(y_lo_ready, 1)

            for n in range(1, OL_TILES + 1):
                if n <= 4:
                    kv_scale(n - 1)
                if n <= 2:
                    norm_blocks(range(4 * (n - 1), 4 * n), 0)
                if n == 2:
                    decay_rates()
                    dve.wait_ge(xlo_ready, KB)
                    chain(v.memset(lru_in[:, :, 0:3], 0.0))
                if 3 <= n < 13:
                    j = n - 3
                    head_gain(j)
                    head_finish(j)
                if 5 <= n < 13:
                    v_window(n - 5)
                if X_TILES + 1 <= n <= X_TILES + 8:
                    conv(n - X_TILES - 1)
                for c in chunks_at(n):
                    soft_shift(c)
                    soft_norm(c)
                    if c:
                        attention_lower(c - 1)
                    if c == CHUNKS - 1:
                        attention_lower(c)
                if n in (22, 23, 24, 25):
                    gate_input(2 * (n - 22))
                    gate_input(2 * (n - 22) + 1)
                if n in (26, 27):
                    for m in range(4 * (n - 26), 4 * (n - 26) + 4):
                        square(m)
                if n == 28:
                    for m in range(8):
                        scan(m)
                if n > G_TILES:
                    if n > G_TILES + 1:
                        lru_lower(n - G_TILES - 2)
                    lru_out(n - G_TILES - 1)
            lru_lower(7)
            step.restart()

            with dve.Fori(0, 4) as it:
                for k in range(2):
                    m = bass.ds(it * 2 + k, 1)
                    dve.wait_ge(m_lo_ready, it * 2 + (BASE + k))
                    dve.wait_ge(bank_free, it * 4 + (GATE_TILES + 2 * k + 1))
                    dve.wait_ge(vec_loaded, 16)
                    step.do(v.tensor_tensor(tmp2[:, 0:1, :], tmp[:, 0:1, :], buf_a[:, m, :], ALU.mult))
                    dve.wait_ge(bank_free, it * 4 + (GATE_TILES + 2 * k + 2))
                    dve.wait_ge(vec_loaded, 16)
                    step.do(v.tensor_tensor(tmp2[:, 1:2, :], tmp[:, 1:2, :], rb[:, m, :], ALU.mult))
                    step.wait()
                    v.tensor_tensor(tmp2[:, 0:1, :], tmp2[:, 0:1, :], tmp2[:, 1:2, :], ALU.add)\
                        .then_inc(merged_ready, 1)
                    dve.wait_ge(m_hi_ready, it * 2 + (k + 1))
                    dve.wait_ge(vec_loaded, 16)
                    v.tensor_tensor(y_lo[:, m, :], tmp2[:, 0:1, :], y_hi[:, m, :].bitcast(F32),
                                    ALU.subtract).then_inc(m_lo_ready, 1)
                step.restart()
            dve.wait_ge(x1_loaded, 16)
            for m in range(KB):
                dve.wait_ge(tile_done, OUT_TILES + m + 1)
                v.tensor_tensor(x1[:, m, :], x1[:, m, :], bank[m % 2][:], ALU.add).then_inc(bank_free, 1)
                dve.wait_ge(bank_free, OUT_TILES + m + 1)
                gain_block(x1, m, 1)
                if m:
                    gained_lower(m - 1, 1)
                    add_square(m - 1, 1)
            gained_lower(KB - 1, 1)
            add_square(KB - 1, 1)
            rms_mean(1)

            def query_scale(n, c):
                dve.wait_ge(tile_done, n + (PQ_TILES + 1))
                if not isinstance(n, int) or n >= 2:
                    dve.wait_ge(s_mm, n - 1)
                    dve.wait_ge(vec_loaded, 16)
                v.tensor_tensor(q_pk[:, c % 2, :], bank[c % 2][:], stat[:], ALU.mult).then_inc(bank_free, 1)

            def scores_out(n, c):
                dve.wait_ge(s_mm, n + 1)
                dve.wait_ge(vec_loaded, 16)
                at = slice(n, n + 1) if isinstance(n, int) else bass.ds(n, 1)
                v.tensor_copy(s[:, :, at, :],
                              bank[2 + c % 2][:].rearrange("p (b a k) -> p b a k", b=4, a=1))                    .then_inc(s_evac, 1)

            for c in range(4):
                query_scale(c, c)
                norm_blocks(range(2 * c, 2 * c + 2), 1)
                if c:
                    scores_out(c - 1, c - 1)
            with dve.Fori(1, 4) as it:
                for c in range(4):
                    query_scale(it * 4 + c, c)
                    scores_out(it * 4 + (c - 1), c - 1)
            scores_out(15, 15)
            step.restart()
            dve.wait_ge(iota_ready, 1)

            with dve.Fori(0, TBLOCKS) as it:
                dve.wait_ge(s_evac, 16)
                chain(v.tensor_copy(s_blk[:], s[:, bass.ds(it, 1), :, :].rearrange("p a l k -> p (a l) k")))
                for h in range(PEER_HEADS):
                    lists = [s_blk[:, 2 * h + p, :] for p in range(2)]
                    lo_, hi_ = slice(0, 8), slice(8, 16)
                    a = [step.do(v.max(top_s[:, p, lo_], lists[p])) for p in range(2)]
                    d = []
                    for p in range(2):
                        step.wait(a[p])
                        step.do(v.max_index(top_i[:, h, p, lo_], top_s[:, p, lo_], lists[p]))
                        d.append(step.do(v.match_replace(s_rest[:, p, :], top_s[:, p, lo_], lists[p],
                                                         LOWEST)))
                    e = []
                    for p in range(2):
                        step.wait(d[p])
                        e.append(step.do(v.max(top_s[:, p, hi_], s_rest[:, p, :])))
                    for p in range(2):
                        step.wait(e[p])
                        step.do(v.max_index(top_i[:, h, p, hi_], top_s[:, p, hi_], s_rest[:, p, :]))
                    chain(v.tensor_tensor(cand[:], top_s[:, 0, :].unsqueeze(2).to_broadcast([P, 16, 16]),
                                          top_s[:, 1, :].unsqueeze(1).to_broadcast([P, 16, 16]), ALU.add))
                    flat = cand[:].rearrange("p a b -> p (a b)")
                    chain(v.max(best[:, h, lo_], flat))
                    step.do(v.max_index(pos[:, 16 * h:16 * h + 8], best[:, h, lo_], flat))
                    chain(v.match_replace(cand_rest[:], best[:, h, lo_], flat, LOWEST))
                    chain(v.max(best[:, h, hi_], cand_rest[:]))
                    step.do(v.max_index(pos[:, 16 * h + 8:16 * h + 16], best[:, h, hi_], cand_rest[:]))
                step.wait()
                step.do(v.tensor_copy(esum[:, 0, :], best[:, :, 0]))
                step.do(v.tensor_single_scalar(half_i[:, 0, :], pos[:], 4, ALU.logical_shift_right))
                step.do(v.tensor_single_scalar(half_i[:, 1, :], pos[:], 15, ALU.bitwise_and))
                step.do(v.tensor_copy(top_f[:], top_i[:]))
                step.wait()
                v.tensor_tensor(best[:], best[:], esum[:, 0, :].unsqueeze(2)
                                .to_broadcast([P, PEER_HEADS, 16]), ALU.subtract).then_inc(best_ready, 1)
                chain(v.tensor_copy(half_f[:], half_i[:]))
                for p in range(2):
                    step.do(v.tensor_tensor(pick[:, p, :, :],
                                            half_f[:, p, :].unsqueeze(2).to_broadcast([P, P, 16]),
                                            iota_k[:].unsqueeze(1).to_broadcast([P, P, 16]), ALU.is_equal))
                step.wait()
                for p in range(2):
                    own = pick[:, p, :, :].rearrange("q (h k) a -> q h k a", h=PEER_HEADS)
                    step.do(v.tensor_tensor(own, own, top_f[:, :, p, :].unsqueeze(2)
                                            .to_broadcast([P, PEER_HEADS, 16, 16]), ALU.mult))
                step.wait()
                for p in range(2):
                    step.do(v.tensor_reduce(sel[:, p, :], pick[:, p, :, :], X, ALU.add))
                dve.wait_ge(gexp_ready, it + 1)
                step.wait()
                chain(v.tensor_reduce(esum[:, 0, :], best[:], X, ALU.add))
                chain(v.reciprocal(esum[:, 1, :], esum[:, 0, :]))
                v.tensor_tensor(sel[:, 2, :].rearrange("p (h k) -> p h k", h=PEER_HEADS), best[:],
                                esum[:, 1, :].unsqueeze(2).to_broadcast([P, PEER_HEADS, 16]),
                                ALU.mult).then_inc(sel_ready, 1)
                dve.wait_ge(sel_t, it + 1)
                t = bass.ds(it * P, P)
                chain(v.tensor_copy(g_rest[:, 0, :], bank[4][:, 2 * P:3 * P]))
                step.do(v.tensor_copy(i_t[:, t], bank[4][:, 0:P]))
                step.do(v.tensor_copy(j_t[:, t], bank[4][:, P:2 * P]))
                chain(v.tensor_copy(g_t[0][:, t], g_rest[:, 0, :]))
                chain(v.tensor_tensor(g_rest[:, 1, :], g_rest[:, 0, :], g_t[0][:, t], ALU.subtract))
                chain(v.tensor_copy(g_t[1][:, t], g_rest[:, 1, :]))
                chain(v.tensor_tensor(g_rest[:, 0, :], g_rest[:, 1, :], g_t[1][:, t], ALU.subtract))
                step.do(v.tensor_copy(g_t[2][:, t], g_rest[:, 0, :]))
                step.restart()

            def onehot(it, c):
                k = c % 2
                t = bass.ds(it * P + 16 * c, 16)

                def over_keys(x):
                    return x[:, t].unsqueeze(1).to_broadcast([P, N_KEYS, 16])
                dve.wait_ge(tok_done, it * 32 + (BASE + 4 * (c - 1)))
                dve.wait_ge(vec_loaded, 16)
                step.do(v.tensor_tensor(eq_j[:, k, :, :], iota_e[:], over_keys(j_t), ALU.is_equal))
                dve.wait_ge(onehot_ready, it * 8 + (BASE + c))
                dve.wait_ge(vec_loaded, 16)
                step.do(v.tensor_tensor(eq_i[:], iota_e[:], over_keys(i_t), ALU.is_equal))
                step.wait()
                for n in range(3):
                    last = v.tensor_tensor(gi[n][:, k, :, :], eq_i[:], over_keys(g_t[n]), ALU.mult)
                    if n < 2:
                        step.do(last)
                step.wait()
                last.then_inc(onehot_ready, 1)
                return last

            with dve.Fori(0, 4) as it:
                for c in range(8):
                    onehot(it, c)
                step.restart()

            def gate_times(k):
                return v.tensor_tensor(
                    act_in[:, k, :, :].rearrange("p c (b t) -> p c b t", b=16),
                    act_in[:, k, :, :].rearrange("p c (b t) -> p c b t", b=16),
                    g_in[:, k, :, :, :].rearrange("p b c t -> p c b t"), ALU.mult)

            with dve.Fori(0, 16) as it:
                for k in range(2):
                    dve.wait_ge(act_loaded[k], it * 16 + 16)
                    dve.wait_ge(g_loaded[k], it * 16 + 16)
                    gate_times(k).then_inc(e_ready, 1)
                    dve.wait_ge(e_hi_ready, it * 2 + (k + 1))
                    v.tensor_tensor(e_lo[:, k, :, :], act_in[:, k, :, :], e_hi[:, k, :, :].bitcast(F32),
                                    ALU.subtract).then_inc(e_lo_ready, 1)
            for m in range(KB):
                dve.wait_ge(bank_done, m + 1)
                v.tensor_tensor(x1[:, m, :], x1[:, m, :], bank[m][:], ALU.add).then_inc(out_ready, 1)

        @block.tensor
        def _(pe):
            pe.sem_inc(g_evac, BASE)
            mm = nc.tensor.matmul

            def tile(n, right_hi, right_lo, it=None, per=4, when=None, between=None):
                off = (lambda x: x) if it is None else (lambda x: it * per + x)
                pe.wait_ge(hi_ready, off(n + 1))
                if it is not None or n >= 2:
                    pe.wait_ge(bank_free, off(n - 1))
                ps = bank[n % 2][:]
                for k in range(KB):
                    w = w_hi[:, n % 2, P * k:P * (k + 1)]
                    if when:
                        pe.wait_ge(when[0], when[1] + k)
                    mm(ps, w, right_hi[:, k, :], start=(k == 0), stop=False)
                    mm(ps, w, right_lo[:, k, :], start=False, stop=False)
                if between:
                    between()
                pe.wait_ge(lo_ready, off(n + 1))
                for k in range(KB):
                    last = mm(ps, w_lo[:, n % 2, P * k:P * (k + 1)], right_hi[:, k, :],
                              start=False, stop=(k == KB - 1))
                last.then_inc(tile_done, 1)

            def sum_squares(first):
                pe.wait_ge(sq_read, KB * (first + 1))
                mm(bank[MI][:], ones[:], stat[:], start=True, stop=True).then_inc(ss_ready, 1)

            def head(j):
                x = tmp[:, j % 2, :] if j < 2 else buf_a[:, j - 2, :]
                pe.wait_ge(head_gained, j + 1)
                if j:
                    pe.wait_ge(head_done, j)
                mm(bank[TR0][:], blocks[:], tmp2[:, j % 2, :], start=True, stop=True)
                mm(bank[TR1][:], rot, x, start=True, stop=True).then_inc(head_mm, 1)

            def turn_v(w):
                t0, kw = window(w)
                if w >= 2:
                    pe.wait_ge(vt_evac, w - 1)
                for a in range(2):
                    last = nc.tensor.transpose(bank[(MI, PV)[w % 2]][0:kw, P * a:P * (a + 1)],
                                               v_raw[:, a, t0:t0 + kw], ident)
                last.then_inc(vt_ready, 1)

            def scores(c):
                t0, kw = window(c)
                if c:
                    pe.wait_ge(shifted, c)
                for p in range(PAIRS):
                    for h in range(2):
                        part = slice(64 * h, 64 * h + 64)
                        last = mm(bank[SC0 + p // 4][part, P * (p % 4):P * (p % 4) + kw],
                                  buf_a[part, p, CHUNK * c:CHUNK * (c + 1)],
                                  kdup[part, p // 2, t0:t0 + kw], start=True, stop=True)
                last.then_inc(scores_ready, 1)

            def turn_probs(c):
                _, kw = window(c)
                pe.wait_ge(probs_ready, c + 1)
                if c:
                    pe.wait_ge(pt_ready, c)
                for p in range(PAIRS):
                    last = nc.tensor.transpose(bank[TR0 + p // 4][0:kw, P * (p % 4):P * (p % 4 + 1)],
                                               prob[:, p, 0:kw], ident)
                last.then_inc(pt_psum, 1)

            def weigh(c):
                _, kw = window(c)
                pe.wait_ge(pt_ready, c + 1)
                if c:
                    pe.wait_ge(pv_lo, c)
                for kv in range(N_KV):
                    for h in range(2):
                        at = P * (kv // 2) + 64 * (kv % 2)
                        last = mm(bank[PV][64 * h:64 * h + 64, P * kv:P * (kv + 1)],
                                  vwin[0:kw, c, at:at + 64],
                                  prob_t[0:kw, 2 * kv:2 * kv + 2, 64 * h:64 * h + 64],
                                  start=True, stop=True)
                last.then_inc(pv_ready, 1)

            def lru_gates(m):
                b0 = (SC0, TR0)[m % 2]
                pe.wait_ge(conv_ready, m + 1)
                if m >= 2:
                    pe.wait_ge(gate_sig, m - 1)
                for g in range(2):
                    last = mm(bank[b0 + g][:], gw[:, g, P * m:P * (m + 1)], xc[:, m, :],
                              start=True, stop=True)
                last.then_inc(gate_mm, 1)

            pe.wait_ge(consts_ready, 1)
            for n in range(OL_TILES):
                if 4 <= n < 14:
                    if n == 4:
                        pe.wait_ge(mat_loaded, 16)
                        pe.wait_ge(xlo_ready, KB)
                    head(n - 4)
                if 5 <= n < 13:
                    if n == 5:
                        pe.wait_ge(kv_biased, 4)
                    turn_v(n - 5)
                for c in chunks_at(n):
                    if c == 0:
                        pe.wait_ge(head_done, 10)
                        pe.wait_ge(vt_evac, CHUNKS)
                    scores(c)
                    if c:
                        weigh(c - 1)
                    if n == OA_TILES:
                        turn_probs(c)
                if n == OA_TILES:
                    weigh(CHUNKS - 1)
                    pe.wait_ge(pv_lo, CHUNKS)
                if n == 22:
                    pe.wait_ge(gw_loaded, 16)
                if 22 <= n < 26:
                    lru_gates(2 * (n - 22))
                    lru_gates(2 * (n - 22) + 1)
                if n == 0:
                    tile(0, y_hi, y_lo, when=(xg_lo, 1), between=lambda: sum_squares(0))
                elif n < Q_TILES or OA_TILES <= n < G_TILES:
                    tile(n, y_hi, y_lo)
                else:
                    tile(n, x_hi, x_lo)
                if n < OA_TILES:
                    for c in chunks_at(n):
                        turn_probs(c)

            def stage(first, rounds, right_hi, right_lo):
                with pe.Fori(0, rounds) as it:
                    for c in range(4):
                        tile(first + c, right_hi, right_lo, it)

            def stage_by_block(first, ready, right_hi, right_lo):
                for c in range(4):
                    tile(first + c, right_hi, right_lo, when=ready if c == 0 else None)
                with pe.Fori(1, 2) as it:
                    for c in range(4):
                        tile(first + c, right_hi, right_lo, it)

            stage_by_block(OL_TILES, (y_lo_ready, 1), y_hi, y_lo)
            stage(GATE_TILES, 4, x_hi, x_lo)
            stage_by_block(OUT_TILES, (m_lo_ready, BASE + 1), y_hi, y_lo)

            def key_scores(n, c):
                pe.wait_ge(q_ready, n + 1)
                if not isinstance(n, int) or n >= 2:
                    pe.wait_ge(s_evac, n - 1)
                at = slice(n, n + 1) if isinstance(n, int) else bass.ds(n, 1)
                for b in range(TBLOCKS):
                    last = mm(bank[2 + c % 2][:, P * b:P * (b + 1)], q_pk[:, c % 2, P * b:P * (b + 1)],
                              keys[:, at, :], start=True, stop=True)
                last.then_inc(s_mm, 1)

            for c in range(4):
                n = PQ_TILES + c
                if c == 0:
                    tile(n, x_hi, x_lo, when=(xg_lo, KB + 1), between=lambda: sum_squares(1))
                else:
                    tile(n, x_hi, x_lo)
                    if c == 1:
                        pe.wait_ge(keys_loaded, 16)
                    key_scores(c - 1, c - 1)
            with pe.Fori(1, 4) as it:
                for c in range(4):
                    tile(PQ_TILES + c, x_hi, x_lo, it)
                    key_scores(it * 4 + (c - 1), c - 1)
            key_scores(15, 15)

            pe.wait_ge(xlo_ready, 2 * KB)
            with pe.Fori(0, TBLOCKS) as it:
                for c in range(16):
                    tile(U_TILES + c, h_hi, h_lo, it, 16)
                    if c == 13:
                        pe.wait_ge(sel_ready, it + 1)
                        for k in range(3):
                            last = nc.tensor.transpose(bank[4][:, P * k:P * (k + 1)], sel[:, k, :], ident)
                        last.then_inc(sel_t, 1)

            with pe.Fori(0, 4) as it:
                for c in range(8):
                    tile(U_TILES + 64 + c, h_hi, h_lo, it, 8)
                    pe.wait_ge(onehot_ready, it * 8 + (BASE + c + 1))
                    for h in range(4):
                        pe.wait_ge(g_evac, it * 32 + (BASE + 4 * c + h - 3))
                        for t in range(4):
                            for n in range(3):
                                last = mm(bank[2 + h][:, P * t:P * (t + 1)], eq_j[:, c % 2, :, 4 * h + t],
                                          gi[n][:, c % 2, :, 4 * h + t], start=(n == 0), stop=(n == 2))
                        last.then_inc(tok_done, 1)
            with pe.Fori(0, 4) as it:
                for c in range(8):
                    tile(U_TILES + 96 + c, h_hi, h_lo, it, 8)

            def experts(it, first, final):
                for c in range(8):
                    k = c // 4
                    if isinstance(it, int):
                        off = it * 8 + V_TILES + c
                        group = it * 2 + k + 1
                    else:
                        off = it * 8 + (V_TILES + c)
                        group = it * 2 + (k + 1)
                    pe.wait_ge(hi_ready, off + 1)
                    if c % 4 == 0:
                        pe.wait_ge(e_lo_ready, group)
                    if final and c == 7:
                        pe.wait_ge(lo_ready, off + 1)
                        for m in range(KB):
                            w = w_hi[:, 1, P * m:P * (m + 1)]
                            mm(bank[m][:], w, e_hi[:, 1, 3, :], start=False, stop=False)
                            mm(bank[m][:], w, e_lo[:, 1, 3, :], start=False, stop=False)
                            mm(bank[m][:], w_lo[:, 1, P * m:P * (m + 1)], e_hi[:, 1, 3, :],
                               start=False, stop=True).then_inc(bank_done, 1)
                        continue
                    start = first and c == 0
                    order = [m % KB for m in range(2, KB + 2)] if start else range(KB)
                    for m in order:
                        if start and m < 2:
                            pe.wait_ge(bank_free, V_TILES - 1 + m)
                        w = w_hi[:, c % 2, P * m:P * (m + 1)]
                        mm(bank[m][:], w, e_hi[:, k, c % 4, :], start=start, stop=False)
                        mm(bank[m][:], w, e_lo[:, k, c % 4, :], start=False, stop=False)
                    pe.wait_ge(lo_ready, off + 1)
                    for m in range(KB):
                        last = mm(bank[m][:], w_lo[:, c % 2, P * m:P * (m + 1)],
                                  e_hi[:, k, c % 4, :], start=False, stop=False)
                    last.then_inc(tile_done, 1)

            pe.wait_ge(g_evac, BASE + T // 4)
            experts(0, True, False)
            with pe.Fori(1, 15) as it:
                experts(it, False, False)
            experts(15, False, True)


_NAMES = ["x_t", "dense_w", "u_t", "v_t", "gates_w", "sub_keys", "vecs", "rope", "mats"]


def _columns(a, n):
    return np.ascontiguousarray(np.asarray(a).reshape(n, P).T)


def _tiles(w):
    w = np.asarray(w)
    return w.reshape(KB, P, -1, P).transpose(2, 1, 0, 3).reshape(-1, P, D)


def _rope_tables():
    dim = HEAD_DIM // 4
    half = dim // 2
    inv = np.float32(500000.0) ** (-np.arange(0, dim, 2, dtype=np.float32) / np.float32(dim))
    ang = np.arange(T, dtype=np.float32)[None, :] * inv.astype(np.float32)[:, None]
    table = np.zeros((HEAD_DIM, 2, T), np.float32)
    table[:, 0] = 1.0
    table[0:half, 0] = table[half:dim, 0] = np.cos(ang)
    table[0:half, 1] = table[half:dim, 1] = np.sin(ang)
    return np.concatenate([table, table])


def _matrices():
    dim = HEAD_DIM // 4
    half = dim // 2
    swap = np.zeros((P, P), np.float32)
    for h in range(2):
        for d in range(half):
            a, b = HEAD_DIM * h + d, HEAD_DIM * h + half + d
            swap[b, a] = -1.0
            swap[a, b] = 1.0
    return np.ascontiguousarray(np.stack([np.eye(P, dtype=np.float32), swap], axis=1))


def kernel(**inputs):
    import concourse.bacc as bacc
    from concourse.bass_utils import run_bass_kernel_spmd

    a = {k: np.asarray(v) for k, v in inputs.items()}
    w_in, b_in = _tiles(a["w_in"][0]), a["b_in"][0].reshape(-1, P)
    dense_w = np.concatenate([
        w_in[W_IN_FIRST], _tiles(a["w_o_attn"][0]), w_in[W_IN_G], _tiles(a["w_o_lru"][0]),
        w_in[W_IN_GATES], _tiles(a["w_out"][0]), _tiles(a["peer_w_q"][0])])
    none = np.zeros((KB, P), np.float32)
    biases = np.concatenate([b_in[W_IN_FIRST], none, b_in[W_IN_G], none, b_in[W_IN_GATES], none,
                             a["peer_b_q"][0].reshape(-1, P)])
    gates_w = np.zeros((P, 2, KB, P), np.float32)
    for g, name in enumerate(("w_rg", "w_ig")):
        w = a[name][0].reshape(KB, 2, 64, 64)
        for h in range(2):
            gates_w[64 * h:64 * h + 64, g, :, 64 * h:64 * h + 64] = w[:, h].transpose(1, 0, 2)
    sinks = np.repeat(a["attn_sinks"][0].reshape(PAIRS, 2).T, CHUNK, axis=0)
    vecs = np.concatenate([
        biases.T, _columns(a["conv_w"][0], 32), _columns(a["conv_b"][0], 8), _columns(a["b_rg"][0], 8),
        _columns(a["b_ig"][0], 8), _columns(a["lru_L"][0], 8), _columns(a["norm_mix_g"][0], 8),
        _columns(a["norm_ffn_g"][0], 8), np.tile(a["q_norm_g"][0], 2)[:, None],
        np.tile(a["k_norm_g"][0], 2)[:, None], sinks], axis=1)
    arrays = {
        "x_t": a["x"][0].T.reshape(KB, P, T).transpose(1, 0, 2),
        "dense_w": dense_w,
        "u_t": a["peer_u"][0].reshape(N_KEYS, N_KEYS, KB, P).transpose(0, 3, 2, 1).reshape(N_KEYS, P, D),
        "v_t": a["peer_v"][0].reshape(N_KEYS, P, D),
        "gates_w": gates_w.reshape(P, 2, D),
        "sub_keys": a["peer_sub_keys"][0].reshape(16, N_KEYS, P).transpose(2, 0, 1),
        "vecs": vecs,
        "rope": _rope_tables(),
        "mats": _matrices(),
    }
    arrays = {k: np.ascontiguousarray(v) for k, v in arrays.items()}
    nc = bacc.Bacc("TRN2", target_bir_lowering=False, num_devices=1)
    aps = [nc.dram_tensor(n, arrays[n].shape, F32, kind="ExternalInput").ap() for n in _NAMES]
    out = nc.dram_tensor("out", [P, KB, T], F32, kind="ExternalOutput").ap()
    build(nc, *aps, out)
    r = run_bass_kernel_spmd(nc, [arrays], core_ids=[0])
    y = np.asarray(r.results[0]["out"])
    return np.ascontiguousarray(y.transpose(2, 1, 0).reshape(1, T, D))
```

```python
from contextlib import ExitStack

import numpy as np

import concourse.bass as bass
from concourse import mybir

F32 = mybir.dt.float32
F32R = mybir.dt.float32r
BF16 = mybir.dt.bfloat16
U16 = mybir.dt.uint16
ALU = mybir.AluOpType
ACT = mybir.ActivationFunctionType
X = mybir.AxisListType.X

P = 128
T = 512
D = 1024
KB = D // P
EPS = 1e-6
CHUNK = 64
HEAD_DIM = 64
N_KV = 4
PAIRS = 8
CHUNKS = T // CHUNK
LRU_C = 8.0
N_KEYS = 128
PEER_HEADS = 8
TBLOCKS = T // P
LOWEST = -3.0e38

Q_TILES, X_TILES = 4, 12
G_FIRST, OA_TILES, G_TILES, OL_TILES = 20, 22, 28, 36
GATE_TILES, OUT_TILES, PQ_TILES = 44, 60, 68
U_TILES, V_TILES = 84, 212
ALL_TILES = 340
BASE = 8
DMA_BASE = 16
GATES_WITH = {22: (0, 1), 23: (2, 3, 4), 24: (5, 6, 7)}
DECAYS_WITH = {25: (0, 1, 2), 26: (3, 4, 5), 27: (6, 7)}
ROOTS_WITH = 28
W_IN_FIRST = [24, 25, 26, 27] + list(range(16, 24)) + list(range(0, 8))
W_IN_G = list(range(8, 16))
W_IN_GATES = [c for m in range(8) for c in (36 + m, 28 + m)]

_WIDTHS = [("b_in", 84), ("conv_w", 32), ("conv_b", 8), ("b_rg", 8), ("b_ig", 8), ("lru_L", 8),
           ("g_mix", 8), ("g_ffn", 8), ("g_q", 1), ("g_k", 1), ("sinks", 8)]
VEC = {}
_at = 0
for _name, _w in _WIDTHS:
    VEC[_name] = _at
    _at += _w
N_VEC = _at


class Steps:

    def __init__(self, eng, sem):
        self.eng, self.sem, self.n = eng, sem, 0

    def do(self, instruction):
        instruction.then_inc(self.sem, 1)
        self.n += 1
        return self.n

    def wait(self, n=None):
        self.eng.wait_ge(self.sem, n or self.n)

    def restart(self):
        if self.n:
            self.eng.wait_ge(self.sem, self.n)
            self.eng.sem_inc(self.sem, -self.n)
            self.n = 0


def build(nc, x_t, dense_w, u_t, v_t, gates_w, sub_keys, vecs, rope, mats, out):
    act_dram = nc.dram_tensor("act_scratch", [32, P, 4 * T], F32, kind="Internal").ap()
    g_dram = nc.dram_tensor("g_scratch", [16, P, P * 32], F32, kind="Internal").ap()

    with ExitStack() as ctx:
        def sb(name, shape, dt, scope=ctx):
            return scope.enter_context(nc.sbuf_tensor(name, shape, dt))

        def sem(name):
            return ctx.enter_context(nc.semaphore(name))

        bank = [ctx.enter_context(nc.psum_tensor(f"bank{i}", [P, 512], F32)) for i in range(8)]
        SC0, SC1, TR0, TR1, PV, MI = 2, 3, 4, 5, 6, 7

        raw = sb("raw", [P, 4, D], F32)
        w_hi = sb("w_hi", [P, 2, D], F32R)
        w_lo = sb("w_lo", [P, 2, D], F32R)
        vec = sb("vec", [P, N_VEC], F32)
        mat = sb("mat", [P, 2, P], F32)
        ident, rot = mat[:, 0, :], mat[:, 1, :]
        ones = sb("ones", [P, P], F32)
        stat = sb("stat", [P, T], F32)

        front = ExitStack()
        x_hi = sb("x_hi", [P, KB, T], F32R, front)
        x_lo = sb("x_lo", [P, KB, T], F32R, front)
        xc = sb("xc", [P, KB, T], F32, front)
        buf_a = sb("buf_a", [P, KB, T], F32, front)
        lru_in = sb("lru_in", [P, KB, T + 3], F32, front)
        y_hi = sb("y_hi", [P, KB, T], F32R, front)
        y_lo = sb("y_lo", [P, KB, T], F32R, front)
        blocks = sb("blocks", [P, P], F32, front)
        tmp = sb("tmp", [P, 2, T], F32, front)
        tmp2 = sb("tmp2", [P, 2, T], F32, front)
        lam = sb("lam", [P, 8, 8], F32, front)
        gw = sb("gw", [P, 2, D], F32, front)
        attn = ExitStack()
        kdup = sb("kdup", [P, N_KV, T], F32, attn)
        v_raw = sb("v_raw", [P, 2, T], F32, attn)
        vwin = sb("vwin", [P, CHUNKS, 2 * P], F32, attn)
        ropes = sb("ropes", [P, 2, T], F32, attn)
        q_diag = sb("q_diag", [P, PAIRS, P], F32, attn)
        prob = sb("prob", [P, PAIRS, P], F32, attn)
        prob_t = sb("prob_t", [P, PAIRS, P], F32, attn)
        soft = sb("soft", [P, 6, PAIRS], F32, attn)
        q_rms = sb("q_rms", [P, PAIRS, TBLOCKS, 2], F32, attn)
        q_fac = sb("q_fac", [P, CHUNKS, PAIRS], F32, attn)
        attn.close()
        lru = ExitStack()
        rb = sb("rb", [P, KB, T], F32, lru)
        ib = lru_in[:, :, 3:3 + T]
        lru.close()
        front.close()

        peer = ExitStack()
        act_out = sb("act_out", [P, 2, 4, T], F32, peer)
        g_in = sb("g_in", [P, 2, 16, 4, 32], F32, peer)
        x1 = sb("x1", [P, KB, T], F32, peer)
        h_hi = sb("h_hi", [P, KB, T], F32R, peer)
        h_lo = sb("h_lo", [P, KB, T], F32R, peer)
        rout = ExitStack()
        q_pk = sb("q_pk", [P, 2, T], F32, rout)
        keys = sb("keys", [P, 2 * PEER_HEADS, N_KEYS], F32, rout)
        iota_e = sb("iota_e", [P, N_KEYS, 16], BF16, rout)
        iota_k = sb("iota_k", [P, 16], BF16, rout)
        i_t = sb("i_t", [P, T], BF16, rout)
        j_t = sb("j_t", [P, T], BF16, rout)
        g_t = [sb(f"g_t{n}", [P, T], BF16, rout) for n in range(3)]
        topk = ExitStack()
        s = sb("s", [P, TBLOCKS, 2 * PEER_HEADS, N_KEYS], F32, topk)
        queries = ExitStack()
        xg = sb("xg", [P, KB, T], F32, queries)
        queries.close()
        s_blk = sb("s_blk", [P, 2 * PEER_HEADS, N_KEYS], F32, topk)
        s_rest = sb("s_rest", [P, 2, N_KEYS], F32, topk)
        top_s = sb("top_s", [P, 2, 16], F32, topk)
        top_i = sb("top_i", [P, PEER_HEADS, 2, 16], U16, topk)
        top_f = sb("top_f", [P, PEER_HEADS, 2, 16], BF16, topk)
        cand = sb("cand", [P, 16, 16], F32, topk)
        cand_rest = sb("cand_rest", [P, 256], F32, topk)
        best = sb("best", [P, PEER_HEADS, 16], F32, topk)
        pos = sb("pos", [P, PEER_HEADS * 16], U16, topk)
        half_i = sb("half_i", [P, 2, P], U16, topk)
        half_f = sb("half_f", [P, 2, P], BF16, topk)
        pick = sb("pick", [P, 2, P, 16], BF16, topk)
        sel = sb("sel", [P, 3, P], F32, topk)
        g_rest = sb("g_rest", [P, 2, P], F32, topk)
        esum = sb("esum", [P, 2, PEER_HEADS], F32, topk)
        topk.close()
        scat = ExitStack()
        eq_i = sb("eq_i", [P, N_KEYS, 16], BF16, scat)
        eq_j = sb("eq_j", [P, 2, N_KEYS, 16], BF16, scat)
        gi = [sb(f"gi{n}", [P, 2, N_KEYS, 16], BF16, scat) for n in range(3)]
        g_out = sb("g_out", [P, 2, N_KEYS, 32], F32, scat)
        scat.close()
        act_in = sb("act_in", [P, 2, 4, T], F32, rout)
        e_hi = sb("e_hi", [P, 2, 4, T], F32R, rout)
        e_lo = sb("e_lo", [P, 2, 4, T], F32R, rout)
        rout.close()
        peer.close()

        raw_ready = [sem(f"raw_ready{i}") for i in range(4)]
        hi_ready, lo_ready = sem("hi_ready"), sem("lo_ready")
        tile_done = sem("tile_done")
        bank_free = sem("bank_free")
        x_loaded = [sem(f"x_loaded{k}") for k in range(KB)]
        vec_loaded, mat_loaded = sem("vec_loaded"), sem("mat_loaded")
        rope_loaded, gw_loaded = sem("rope_loaded"), sem("gw_loaded")
        x1_loaded, keys_loaded = sem("x1_loaded"), sem("keys_loaded")
        consts_ready, iota_ready = sem("consts_ready"), sem("iota_ready")
        act_step, dve_step = sem("act_step"), sem("dve_step")
        sq_ready, sq_read, ss_ready, ms_ready = (
            sem("sq_ready"), sem("sq_read"), sem("ss_ready"), sem("ms_ready"))
        xg_ready, xg_hi, xg_lo = sem("xg_ready"), sem("xg_hi"), sem("xg_lo")
        rms_ready, xn_ready, xhi_ready, xlo_ready = (
            sem("rms_ready"), sem("xn_ready"), sem("xhi_ready"), sem("xlo_ready"))
        kv_biased, q_ready = sem("kv_biased"), sem("q_ready")
        head_gained, head_mm = sem("head_gained"), sem("head_mm")
        head_ms, head_rms, head_done = sem("head_ms"), sem("head_rms"), sem("head_done")
        fac_ready, kdup_ready = sem("fac_ready"), sem("kdup_ready")
        vt_ready, vt_evac = sem("vt_ready"), sem("vt_evac")
        diag_ready, scores_ready, shifted = sem("diag_ready"), sem("scores_ready"), sem("shifted")
        exp_ready, probs_ready = sem("exp_ready"), sem("probs_ready")
        pt_psum, pt_ready, pv_ready, pv_hi, pv_lo = (
            sem("pt_psum"), sem("pt_ready"), sem("pv_ready"), sem("pv_hi"), sem("pv_lo"))
        conv_ready, gate_mm, gate_sig = sem("conv_ready"), sem("gate_mm"), sem("gate_sig")
        lam_e, lam_ready = sem("lam_e"), sem("lam_ready")
        gated, decay_ready, square_ready, root_ready, h_ready = (
            sem("gated"), sem("decay_ready"), sem("square_ready"), sem("root_ready"), sem("h_ready"))
        y_ready, y_hi_ready, y_lo_ready = sem("y_ready"), sem("y_hi_ready"), sem("y_lo_ready")
        merged_ready, m_hi_ready, m_lo_ready = (
            sem("merged_ready"), sem("m_hi_ready"), sem("m_lo_ready"))
        s_mm, s_evac, best_ready, gexp_ready, sel_ready, sel_t = (
            sem("s_mm"), sem("s_evac"), sem("best_ready"), sem("gexp_ready"), sem("sel_ready"),
            sem("sel_t"))
        onehot_ready, tok_done, g_evac = sem("onehot_ready"), sem("tok_done"), sem("g_evac")
        act_stored = [sem(f"act_stored{i}") for i in range(2)]
        g_stored = [sem(f"g_stored{i}") for i in range(2)]
        act_loaded = [sem(f"act_loaded{i}") for i in range(2)]
        g_loaded = [sem(f"g_loaded{i}") for i in range(2)]
        e_ready, e_hi_ready, e_lo_ready = sem("e_ready"), sem("e_hi_ready"), sem("e_lo_ready")
        bank_done, out_ready, out_stored = sem("bank_done"), sem("out_ready"), sem("out_stored")

        block = ctx.enter_context(nc.Block())

        def window(c):
            return (0, CHUNK) if c == 0 else (CHUNK * (c - 1), 2 * CHUNK)

        def chunks_at(n):
            first = X_TILES + 2
            return [n - first] if first <= n < OA_TILES else []

        def col(name, m=0):
            return vec[:, VEC[name] + m:VEC[name] + m + 1]

        @block.sync
        def _(sp):
            sp.dma_start(vec[:], vecs).then_inc(vec_loaded, 16)
            for k in range(KB):
                sp.dma_start(buf_a[:, k, :], x_t[:, k, :]).then_inc(x_loaded[k], 16)
                if k == 1:
                    sp.dma_start(raw[:, 0, :], dense_w[0]).then_inc(raw_ready[0], 16)

            def load_tiles(source, it, base, n=4):
                for c in range(n):
                    if isinstance(it, int) and base + n * it + c < 4:
                        pass
                    else:
                        sp.wait_ge(hi_ready, it * n + (base + c - 3))
                        sp.wait_ge(lo_ready, it * n + (base + c - 3))
                    sp.dma_start(raw[:, c % 4, :], source[it * n + c]).then_inc(raw_ready[c % 4], 16)

            for n in range(1, 4):
                sp.dma_start(raw[:, n, :], dense_w[n]).then_inc(raw_ready[n], 16)
            sp.dma_start(mat[:], mats).then_inc(mat_loaded, 16)
            sp.dma_start(ropes[:], rope).then_inc(rope_loaded, 16)
            load_tiles(dense_w, 1, 0)
            sp.dma_start(gw[:], gates_w).then_inc(gw_loaded, 16)
            with sp.Fori(2, 11) as it:
                load_tiles(dense_w, it, 0)
            sp.wait_ge(h_ready, 8)
            sp.dma_start(x1[:], x_t).then_inc(x1_loaded, 16)
            with sp.Fori(11, 18) as it:
                load_tiles(dense_w, it, 0)
            sp.wait_ge(tile_done, PQ_TILES)
            sp.dma_start(keys[:], sub_keys).then_inc(keys_loaded, 16)
            with sp.Fori(18, 21) as it:
                load_tiles(dense_w, it, 0)

            def load_group(it, k):
                if not (isinstance(it, int) and it == 0):
                    sp.wait_ge(e_lo_ready, it * 2 + (k - 1))
                sp.dma_start(act_in[:, k, :, :], act_dram[it * 2 + k]
                             .rearrange("p (c t) -> p c t", c=4)).then_inc(act_loaded[k], 16)
                src = g_dram[:, :, bass.ds(it * 256 + k * 128, 128)]
                sp.dma_start(g_in[:, k, :, :, :].rearrange("p b c t -> p b (c t)"),
                             src.rearrange("b p n -> p b n")).then_inc(g_loaded[k], 16)

            with sp.Fori(0, 26) as it:
                load_tiles(u_t, it, U_TILES)
            for k in range(2):
                sp.wait_ge(act_stored[k], DMA_BASE + 16 * 8)
                sp.wait_ge(g_stored[k], DMA_BASE + 16 * 8)
            sp.wait_ge(tok_done, BASE + T // 4)
            load_group(0, 0)
            load_group(0, 1)
            with sp.Fori(26, 32) as it:
                load_tiles(u_t, it, U_TILES)
            load_tiles(v_t, 0, V_TILES)
            load_tiles(v_t, 1, V_TILES)
            for k in range(2):
                sp.wait_ge(act_stored[k], DMA_BASE + 16 * 16)
            with sp.Fori(1, 16) as it:
                for k in range(2):
                    load_group(it, k)
                    for c in range(4):
                        sp.wait_ge(hi_ready, it * 8 + (V_TILES + 4 * k + c - 3))
                        sp.wait_ge(lo_ready, it * 8 + (V_TILES + 4 * k + c - 3))
                        sp.dma_start(raw[:, c, :], v_t[it * 8 + (4 * k + c)]).then_inc(raw_ready[c], 16)
            for m in range(KB):
                sp.wait_ge(out_ready, m + 1)
                sp.dma_start(out[:, m, :], x1[:, m, :]).then_inc(out_stored, 16)
            sp.wait_ge(out_stored, 16 * KB)

        @block.gpsimd
        def _(pool):
            def lo(it, base, c):
                pool.wait_ge(hi_ready, it * 4 + (base + c + 1))
                if not (isinstance(it, int) and c < 2):
                    pool.wait_ge(tile_done, it * 4 + (base + c - 1))
                pool.tensor_tensor(w_lo[:, c % 2, :], raw[:, c, :], w_hi[:, c % 2, :].bitcast(F32),
                                   ALU.subtract).then_inc(lo_ready, 1)

            for c in range(4):
                lo(0, 0, c)
            with pool.Fori(1, 18) as it:
                for c in range(4):
                    lo(it, 0, c)
            pool.wait_ge(tile_done, PQ_TILES)
            nc.gpsimd.iota(iota_k[:], pattern=[[1, 16]], base=0, channel_multiplier=0,
                           allow_small_or_imprecise_dtypes=True)
            nc.gpsimd.iota(iota_e[:], pattern=[[1, N_KEYS], [0, 16]], base=0, channel_multiplier=0,
                           allow_small_or_imprecise_dtypes=True).then_inc(iota_ready, 1)
            with pool.Fori(18, 85) as it:
                for c in range(4):
                    lo(it, 0, c)

        @block.scalar
        def _(act):
            act.sem_inc(merged_ready, BASE)
            for k in range(2):
                act.sem_inc(act_stored[k], DMA_BASE)
                act.sem_inc(g_stored[k], DMA_BASE)
            step = Steps(act, act_step)

            def hi(n, it=None, slot=None):
                slot = n % 4 if slot is None else slot
                if it is None:
                    act.wait_ge(raw_ready[slot], 16 * (n // 4 + 1))
                    if n >= 2:
                        act.wait_ge(tile_done, n - 1)
                else:
                    a, per = it
                    act.wait_ge(raw_ready[slot], a * (4 * per) + 16 * (n // 4 + 1))
                    act.wait_ge(tile_done, a * per + (n - 1))
                nc.scalar.activation(w_hi[:, slot % 2, :], raw[:, slot, :], ACT.Copy).then_inc(hi_ready, 1)

            def squares(src, k, first, ready, value):
                act.wait_ge(ready, value)
                if k >= 2:
                    act.wait_ge(sq_read, KB * first + k - 1)
                elif first:
                    act.wait_ge(m_lo_ready, BASE + KB)
                nc.scalar.activation(tmp2[:, k % 2, :], src[:, k, :], ACT.Square).then_inc(sq_ready, 1)

            def gained_upper(k, first):
                src, dst = (xg, x_hi) if first else (lru_in[:, :, 0:T], y_hi)
                act.wait_ge(xg_ready, KB * first + k + 1)
                nc.scalar.activation(dst[:, k, :], src[:, k, :], ACT.Copy).then_inc(xg_hi, 1)

            def rms_root(first):
                act.wait_ge(ms_ready, first + 1)
                nc.scalar.activation(stat[:], stat[:], ACT.Sqrt).then_inc(rms_ready, 1)

            def normed_upper(k, first):
                src, dst = (xg, h_hi) if first else (lru_in[:, :, 0:T], x_hi)
                act.wait_ge(xn_ready, KB * first + k + 1)
                nc.scalar.activation(dst[:, k, :], src[:, k, :], ACT.Copy).then_inc(xhi_ready, 1)

            act.wait_ge(vec_loaded, 16)
            for k in range(KB):
                squares(buf_a, k, 0, x_loaded[k], 16)
                gained_upper(k, 0)
                if k == 1:
                    hi(0)
            hi(1)
            rms_root(0)

            def evac(n):
                ps, b = bank[n % 2][:], col("b_in", n)
                if n < Q_TILES:
                    act.wait_ge(bank_free, n + 1)
                    dst = tmp[:, n, :] if n < 2 else v_raw[:, n - 2, :]
                    if n < 2:
                        step.wait(step.do(nc.scalar.activation(tmp2[:, n, :], dst, ACT.Square, bias=b)))
                    nc.scalar.activation(dst, dst, ACT.Identity, bias=b).then_inc(kv_biased, 1)
                elif n < X_TILES:
                    j = n - 2
                    act.wait_ge(head_done, j - 1)
                    nc.scalar.activation(tmp2[:, j % 2, :], ps, ACT.Square, bias=b)
                    nc.scalar.activation(buf_a[:, n - Q_TILES, :], ps, ACT.Identity, bias=b)\
                        .then_inc(bank_free, 1)
                elif n < G_FIRST:
                    m = n - X_TILES
                    nc.scalar.activation(lru_in[:, m, 3:3 + T], ps, ACT.Identity, bias=b).then_inc(bank_free, 1)
                elif OA_TILES <= n < OA_TILES + KB:
                    nc.scalar.activation(buf_a[:, n - OA_TILES, :], ps, ACT.Copy).then_inc(bank_free, 1)
                elif n < OL_TILES:
                    m = n - (G_FIRST if n < OA_TILES else G_TILES)
                    if m >= 2:
                        act.wait_ge(y_ready, m - 1)
                    nc.scalar.activation(tmp[:, m % 2, :], ps, ACT.Gelu_apprx_tanh, bias=b)\
                        .then_inc(bank_free, 1)

            def head_root(j):
                act.wait_ge(head_ms, j + 1)
                nc.scalar.activation(xc[:, 1 + j, :], xc[:, 1 + j, :], ACT.Sqrt).then_inc(head_rms, 1)

            def diagonal(c):
                if c == 0:
                    act.wait_ge(consts_ready, 1)
                    act.wait_ge(head_done, 10)
                else:
                    act.wait_ge(scores_ready, c)
                for h in range(2):
                    part = slice(64 * h, 64 * h + 64)
                    last = nc.scalar.activation(q_diag[part, :, part],
                                                buf_a[part, :, CHUNK * c:CHUNK * (c + 1)], ACT.Copy)
                last.then_inc(diag_ready, 1)

            def softmax(c):
                _, kw = window(c)
                act.wait_ge(shifted, c + 1)
                if c:
                    act.wait_ge(pt_psum, c)
                nc.scalar.activation(soft[:, 2, :], soft[:, 1, :], ACT.Exp)
                for p in range(PAIRS):
                    sc = bank[SC0 + p // 4][:, P * (p % 4):P * (p % 4) + kw]
                    last = nc.scalar.activation(prob[:, p, 0:kw], sc, ACT.Exp,
                                                scale=q_fac[:, c, p:p + 1], bias=soft[:, 5, p:p + 1])
                    if p % 4 == 3:
                        last.then_inc(exp_ready, 1)

            def probs_turned(c):
                _, kw = window(c)
                act.wait_ge(pt_psum, c + 1)
                if c:
                    act.wait_ge(pv_ready, c)
                for g in range(2):
                    last = nc.scalar.activation(prob_t[0:kw, 4 * g:4 * g + 4, :], bank[TR0 + g][0:kw, :]
                                                .rearrange("p (a q) -> p a q", a=4), ACT.Copy)
                last.then_inc(pt_ready, 1)

            def attention_out(c):
                act.wait_ge(pv_ready, c + 1)
                nc.scalar.activation(y_hi[:, :, CHUNK * c:CHUNK * (c + 1)],
                                     bank[PV][:].rearrange("p (a q) -> p a q", a=PAIRS),
                                     ACT.Copy).then_inc(pv_hi, 1)

            def gate_sigmoids(m):
                b0 = (SC0, TR0)[m % 2]
                act.wait_ge(gate_mm, m + 1)
                nc.scalar.activation(rb[:, m, :], bank[b0][:], ACT.Sigmoid, bias=col("b_rg", m))
                nc.scalar.activation(ib[:, m, :], bank[b0 + 1][:], ACT.Sigmoid, bias=col("b_ig", m))\
                    .then_inc(gate_sig, 1)

            def decay(m):
                act.wait_ge(gated, m + 1)
                step.wait(step.do(nc.scalar.activation(xc[:, m, :], rb[:, m, :], ACT.Tanh,
                                                       scale=lam[:, 6, m:m + 1])))
                nc.scalar.activation(rb[:, m, :], rb[:, m, :], ACT.Exp, scale=lam[:, 7, m:m + 1])\
                    .then_inc(decay_ready, 1)

            def root(m):
                act.wait_ge(square_ready, m + 1)
                nc.scalar.activation(xc[:, m, :], xc[:, m, :], ACT.Sqrt).then_inc(root_ready, 1)

            def y_upper(m):
                act.wait_ge(y_ready, m + 1)
                nc.scalar.activation(y_hi[:, m, :], tmp2[:, m % 2, :], ACT.Copy).then_inc(y_hi_ready, 1)

            for n in range(OL_TILES + 1):
                if n >= 1:
                    hi(n + 1)
                    act.wait_ge(tile_done, n)
                    if n != G_FIRST + 1:
                        evac(n - 1)
                if n in (1, 2):
                    for k in range(4 * (n - 1), 4 * n):
                        normed_upper(k, 0)
                if n == X_TILES + 7:
                    act.wait_ge(lam_e, 1)
                    nc.scalar.activation(lam[:, 1, :], lam[:, 0, :], ACT.Exp).then_inc(lam_e, 1)
                if n in (4, 5):
                    head_root(n - 4)
                if n == X_TILES + 1:
                    act.wait_ge(head_ms, 3)
                    nc.scalar.activation(q_rms[:], q_rms[:], ACT.Sqrt).then_inc(head_rms, 1)
                for c in chunks_at(n):
                    softmax(c)
                    if n == G_FIRST + 1:
                        evac(n - 1)
                    if c < CHUNKS - 1:
                        diagonal(c + 1)
                    if c:
                        attention_out(c - 1)
                    probs_turned(c)
                    if c == CHUNKS - 1:
                        attention_out(c)
                if n == X_TILES + 1:
                    diagonal(0)
                if n == OA_TILES:
                    act.wait_ge(lam_ready, 1)
                for m in GATES_WITH.get(n, ()):
                    gate_sigmoids(m)
                for m in DECAYS_WITH.get(n, ()):
                    decay(m)
                if n == ROOTS_WITH:
                    for m in range(8):
                        root(m)
                if n >= G_TILES + 2:
                    y_upper(n - G_TILES - 2)
            y_upper(7)

            def ol_body(it, c):
                nc.scalar.activation(rb[:, bass.ds(it * 4 + c, 1), :], bank[c % 2][:]
                                     .rearrange("p (a t) -> p a t", a=1), ACT.Copy).then_inc(bank_free, 1)

            def shifted_loop(first, rounds, body):
                with act.Fori(0, rounds) as it:
                    for c in range(4):
                        hi(first + c + 2, (it, 4), (c + 2) % 4)
                        act.wait_ge(tile_done, it * 4 + (first + c + 1))
                        act.wait_ge(vec_loaded, 16)
                        body(it, c)

            shifted_loop(OL_TILES, 2, ol_body)

            def gate_body(it, c):
                b = vec[:, bass.ds(it * 4 + (VEC["b_in"] + GATE_TILES + c), 1)]
                act.wait_ge(merged_ready, it * 2 + (BASE + c // 2))
                act.wait_ge(vec_loaded, 16)
                nc.scalar.activation(tmp[:, c % 2, :], bank[c % 2][:], ACT.Sigmoid, bias=b)\
                    .then_inc(bank_free, 1)
                if c % 2:
                    act.wait_ge(merged_ready, it * 2 + (BASE + c // 2 + 1))
                    act.wait_ge(vec_loaded, 16)
                    nc.scalar.activation(y_hi[:, bass.ds(it * 2 + c // 2, 1), :],
                                         tmp2[:, 0:1, :], ACT.Copy).then_inc(m_hi_ready, 1)

            shifted_loop(GATE_TILES, 4, gate_body)
            for m in range(KB):
                hi(OUT_TILES + m + 2)
                squares(x1, m, 1, bank_free, OUT_TILES + m + 1)
                gained_upper(m, 1)
            rms_root(1)

            def query_bias(n, c, b):
                act.wait_ge(bank_free, n + PQ_TILES)
                act.wait_ge(vec_loaded, 16)
                nc.scalar.activation(q_pk[:, c % 2, :], q_pk[:, c % 2, :], ACT.Identity, bias=b)\
                    .then_inc(q_ready, 1)

            for c in range(4):
                hi(PQ_TILES + c + 2)
                query_bias(c + 1, c, col("b_in", PQ_TILES + c))
                for k in range(2 * c, 2 * c + 2):
                    normed_upper(k, 1)
            with act.Fori(1, 4) as it:
                for c in range(4):
                    hi(PQ_TILES + c + 2, (it, 4), (c + 2) % 4)
                    query_bias(it * 4 + (c + 1), c, vec[:, bass.ds(it * 4 + (VEC["b_in"] + PQ_TILES + c), 1)])

            def gelu(it, per, base, c):
                k = (c // 4) % 2
                if c % 4 == 0:
                    act.wait_ge(act_stored[k], it * (2 * per) + (DMA_BASE + 2 * base + 16 * (c // 8)))
                    act.wait_ge(vec_loaded, 16)
                nc.scalar.activation(act_out[:, k, c % 4, :], bank[c % 2][:], ACT.Gelu_apprx_tanh)\
                    .then_inc(bank_free, 1)
                if c % 4 == 3:
                    act.wait_ge(bank_free, it * per + (U_TILES + base + c + 1))
                    nc.scalar.dma_start(act_dram[it * (per // 4) + (base // 4 + c // 4)],
                                        act_out[:, k, :, :].rearrange("p c t -> p (c t)"))\
                        .then_inc(act_stored[k], 16)

            with act.Fori(0, 4) as it:
                for c in range(16):
                    hi(U_TILES + c + 2, (it, 16), (c + 2) % 4)
                    act.wait_ge(tile_done, it * 16 + (U_TILES + c + 1))
                    gelu(it, 16, 0, c)
                    if c == 11:
                        act.wait_ge(best_ready, it + 1)
                        nc.scalar.activation(best[:], best[:], ACT.Exp).then_inc(gexp_ready, 1)

            with act.Fori(0, 4) as it:
                for c in range(8):
                    hi(U_TILES + 64 + c + 2, (it, 8), (c + 2) % 4)
                    act.wait_ge(tile_done, it * 8 + (U_TILES + 64 + c + 1))
                    gelu(it, 8, 64, c)
                    k = (c // 2) % 2
                    if c % 2 == 0:
                        act.wait_ge(g_stored[k], it * 32 + (DMA_BASE + 16 * (c // 4)))
                        act.wait_ge(vec_loaded, 16)
                    for h in range(4):
                        act.wait_ge(tok_done, it * 32 + (BASE + 4 * c + h + 1))
                        t0 = 16 * (c % 2) + 4 * h
                        nc.scalar.activation(g_out[:, k, :, t0:t0 + 4].rearrange("p i t -> p t i"),
                                             bank[2 + h][:].rearrange("p (t i) -> p t i", t=4),
                                             ACT.Copy).then_inc(g_evac, 1)
                    if c % 2 == 1:
                        act.wait_ge(g_evac, it * 32 + (BASE + 4 * c + 4))
                        nc.scalar.dma_start(g_dram[it * 4 + c // 2],
                                            g_out[:, k, :, :].rearrange("p i t -> p (i t)"))\
                            .then_inc(g_stored[k], 16)

            def last_tiles(first):
                with act.Fori(0, 2) as it:
                    for c in range(8):
                        hi(U_TILES + first + c + 2, (it, 8), (c + 2) % 4)
                        act.wait_ge(tile_done, it * 8 + (U_TILES + first + c + 1))
                        gelu(it, 8, first, c)

            last_tiles(96)
            act.wait_ge(e_ready, 1)
            nc.scalar.activation(e_hi[:, 0, :, :], act_in[:, 0, :, :], ACT.Copy).then_inc(e_hi_ready, 1)
            last_tiles(112)
            with act.Fori(0, 15) as it:
                for c in range(8):
                    hi(V_TILES + c + 2, (it, 8), (c + 2) % 4)
                    if c % 4 == 0:
                        k = (c // 4 + 1) % 2
                        act.wait_ge(tile_done, it * 8 + (V_TILES + 4 * (c // 4)))
                        act.wait_ge(e_ready, it * 2 + (c // 4 + 2))
                        nc.scalar.activation(e_hi[:, k, :, :], act_in[:, k, :, :], ACT.Copy)\
                            .then_inc(e_hi_ready, 1)
            for c in range(8):
                n = V_TILES + 120 + c
                if n + 2 < ALL_TILES:
                    hi(n + 2)
                if c == 0:
                    act.wait_ge(tile_done, n)
                    act.wait_ge(e_ready, 32)
                    nc.scalar.activation(e_hi[:, 1, :, :], act_in[:, 1, :, :], ACT.Copy)\
                        .then_inc(e_hi_ready, 1)

        @block.vector
        def _(dve):
            dve.sem_inc(m_lo_ready, BASE)
            dve.sem_inc(onehot_ready, BASE)
            dve.sem_inc(tok_done, BASE)
            step = Steps(dve, dve_step)
            v = nc.vector

            def chain(ins):
                step.wait(step.do(ins))

            chain(v.memset(ones[:], 1.0))
            chain(v.memset(blocks[:], 0.0))
            for h in range(2):
                chain(v.memset(blocks[64 * h:64 * h + 64, 64 * h:64 * h + 64], 1.0))
            v.memset(q_diag[:], 0.0).then_inc(consts_ready, 1)

            def gain_block(src, k, first):
                dst = (xg if first else lru_in[:, :, 0:T])[:, k, :]
                v.tensor_scalar(dst, src[:, k, :], col(("g_mix", "g_ffn")[first], k), None, ALU.mult)\
                    .then_inc(xg_ready, 1)

            def gained_lower(k, first):
                src, hi_, lo_ = (xg, x_hi, x_lo) if first else (lru_in[:, :, 0:T], y_hi, y_lo)
                dve.wait_ge(xg_hi, KB * first + k + 1)
                v.tensor_tensor(lo_[:, k, :], src[:, k, :], hi_[:, k, :].bitcast(F32),
                                ALU.subtract).then_inc(xg_lo, 1)

            def add_square(k, first):
                dve.wait_ge(sq_ready, KB * first + k + 1)
                if k == 0:
                    v.tensor_copy(stat[:], tmp2[:, 0, :]).then_inc(sq_read, 1)
                else:
                    dve.wait_ge(sq_read, KB * first + k)
                    v.tensor_tensor(stat[:], stat[:], tmp2[:, k % 2, :], ALU.add).then_inc(sq_read, 1)

            def rms_mean(first):
                dve.wait_ge(ss_ready, first + 1)
                v.tensor_scalar(stat[:], bank[MI][:], 1.0 / D, EPS, ALU.mult, ALU.add).then_inc(ms_ready, 1)
                dve.wait_ge(rms_ready, first + 1)
                chain(v.reciprocal(stat[:], stat[:]))

            def norm_blocks(ks, first):
                src, hi_, lo_ = (xg, h_hi, h_lo) if first else (lru_in[:, :, 0:T], x_hi, x_lo)
                for k in ks:
                    dve.wait_ge(xg_lo, KB * first + k + 1)
                    v.tensor_tensor(src[:, k, :], src[:, k, :], stat[:], ALU.mult).then_inc(xn_ready, 1)
                for k in ks:
                    dve.wait_ge(xhi_ready, KB * first + k + 1)
                    v.tensor_tensor(lo_[:, k, :], src[:, k, :], hi_[:, k, :].bitcast(F32),
                                    ALU.subtract).then_inc(xlo_ready, 1)

            def kv_scale(n):
                dve.wait_ge(tile_done, n + 1)
                dst = tmp[:, n, :] if n < 2 else v_raw[:, n - 2, :]
                v.tensor_tensor(dst, bank[n % 2][:], stat[:], ALU.mult).then_inc(bank_free, 1)

            dve.wait_ge(vec_loaded, 16)
            for k in range(KB):
                dve.wait_ge(x_loaded[k], 16)
                gain_block(buf_a, k, 0)
                if k:
                    gained_lower(k - 1, 0)
                    add_square(k - 1, 0)
            gained_lower(KB - 1, 0)
            add_square(KB - 1, 0)
            rms_mean(0)

            def decay_rates(part):
                L = vec[:, VEC["lru_L"]:VEC["lru_L"] + 8]
                e, s_, z, poly = lam[:, 1, :], lam[:, 3, :], lam[:, 4, :], lam[:, 5, :]
                terms = 9

                def horner(ns):
                    for n in ns:
                        chain(v.tensor_tensor(poly, poly, z, ALU.mult))
                        chain(v.tensor_scalar(poly, poly, 1.0 / (2 * n + 1), None, ALU.add))
                if part == 0:
                    chain(v.tensor_scalar(s_, L, -1.0, None, ALU.mult))
                    v.tensor_tensor(lam[:, 0, :], L, s_, ALU.min).then_inc(lam_e, 1)
                elif part == 1:
                    dve.wait_ge(lam_e, 2)
                    chain(v.tensor_scalar(s_, e, 2.0, None, ALU.add))
                    chain(v.reciprocal(z, s_))
                    chain(v.tensor_tensor(s_, e, z, ALU.mult))
                    chain(v.tensor_tensor(z, s_, s_, ALU.mult))
                    chain(v.tensor_scalar(poly, z, 1.0 / (2 * terms + 1), 1.0 / (2 * terms - 1),
                                          ALU.mult, ALU.add))
                    horner(range(terms - 2, terms - 4, -1))
                elif part == 2:
                    horner(range(terms - 4, 1, -1))
                else:
                    horner((1, 0))
                    chain(v.tensor_tensor(poly, poly, s_, ALU.mult))
                    chain(v.tensor_scalar(poly, poly, 2.0, None, ALU.mult))
                    chain(v.tensor_scalar(z, L, 0.0, None, ALU.min))
                    chain(v.tensor_tensor(z, z, poly, ALU.subtract))
                    chain(v.tensor_scalar(lam[:, 6, :], z, -LRU_C, None, ALU.mult))
                    v.tensor_scalar(lam[:, 7, :], z, LRU_C, None, ALU.mult).then_inc(lam_ready, 1)

            def head_gain(j):
                dve.wait_ge(*((kv_biased, j + 1) if j < 2 else (bank_free, j + 3)))
                x = tmp[:, j % 2, :] if j < 2 else buf_a[:, j - 2, :]
                if j < 2:
                    v.tensor_scalar(x, x, col("g_k"), None, ALU.mult).then_inc(head_gained, 1)
                else:
                    v.tensor_scalar(x, x, col("g_q"), HEAD_DIM ** -0.5, ALU.mult, ALU.mult)\
                        .then_inc(head_gained, 1)

            def head_finish(j):
                x = tmp[:, j % 2, :] if j < 2 else buf_a[:, j - 2, :]
                b0 = (TR0, SC0)[j % 2]
                dve.wait_ge(head_mm, j + 1)
                if j < 2:
                    v.tensor_scalar(xc[:, 1 + j, :], bank[b0][:], 1.0 / HEAD_DIM, EPS, ALU.mult, ALU.add)\
                        .then_inc(head_ms, 1)
                if j == 0:
                    dve.wait_ge(rope_loaded, 16)
                chain(v.tensor_tensor(x, x, ropes[:, 0, :], ALU.mult))
                chain(v.tensor_tensor(xc[:, 0, :], bank[b0 + 1][:], ropes[:, 1, :], ALU.mult))
                v.tensor_tensor(x, x, xc[:, 0, :], ALU.add).then_inc(head_done, 1)

            def key_factor(j):
                dve.wait_ge(head_rms, j + 1)
                chain(v.reciprocal(xc[:, 1 + j, :], xc[:, 1 + j, :]))

            def keys_out(j):
                for h in range(2):
                    part = slice(64 * h, 64 * h + 64)
                    for to in range(2):
                        v.tensor_tensor(kdup[64 * to:64 * to + 64, 2 * j + h, :], tmp[part, j, :],
                                        xc[part, 1 + j, :], ALU.mult).then_inc(kdup_ready, 1)

            def query_factors():
                flat = q_rms[:].rearrange("q p b h -> q (p b h)")
                v.tensor_scalar(flat, bank[TR0][:, 0:2 * PAIRS * TBLOCKS], 1.0 / HEAD_DIM, EPS,
                                ALU.mult, ALU.add).then_inc(head_ms, 1)
                dve.wait_ge(head_rms, 3)
                chain(v.reciprocal(flat, flat))
                for h in range(2):
                    for odd in range(2):
                        last = v.tensor_copy(
                            q_fac[64 * h:64 * h + 64, odd:CHUNKS:2, :],
                            q_rms[64 * odd:64 * odd + 64, :, :, h].rearrange("q p b -> q b p"))
                        if (h, odd) != (1, 1):
                            step.do(last)
                step.wait()
                last.then_inc(fac_ready, 1)

            def v_window(w):
                _, kw = window(w)
                dve.wait_ge(vt_ready, w + 1)
                v.tensor_copy(vwin[0:kw, w, :], bank[(MI, PV)[w % 2]][0:kw, 0:2 * P]).then_inc(vt_evac, 1)

            def conv(m):
                dve.wait_ge(bank_free, X_TILES + m + 1)
                w = [col("conv_w", 8 * k + m) for k in range(4)]
                chain(v.tensor_scalar(xc[:, m, :], lru_in[:, m, 3:3 + T], w[3], col("conv_b", m),
                                      ALU.mult, ALU.add))
                for k in range(3):
                    ins = v.scalar_tensor_tensor(out=xc[:, m, :], in0=lru_in[:, m, k:k + T], scalar=w[k],
                                                 in1=xc[:, m, :], op0=ALU.mult, op1=ALU.add)
                    if k < 2:
                        chain(ins)
                ins.then_inc(conv_ready, 1)

            def soft_shift(c):
                _, kw = window(c)
                sinks = vec[:, VEC["sinks"]:VEC["sinks"] + 8]
                dve.wait_ge(scores_ready, c + 1)
                if c == 0:
                    dve.wait_ge(fac_ready, 1)
                for g in range(2):
                    sc = bank[SC0 + g][:].rearrange("p (a k) -> p a k", a=4)[:, :, 0:kw]
                    step.do(v.tensor_reduce(soft[:, 0, 4 * g:4 * g + 4], sc, X, ALU.max))
                step.wait()
                chain(v.tensor_tensor(soft[:, 0, :], soft[:, 0, :], q_fac[:, c, :], ALU.mult))
                chain(v.tensor_tensor(soft[:, 0, :], soft[:, 0, :], sinks, ALU.max))
                step.do(v.tensor_tensor(soft[:, 1, :], sinks, soft[:, 0, :], ALU.subtract))
                step.wait()
                v.tensor_scalar(soft[:, 5, :], soft[:, 0, :], -1.0, None, ALU.mult).then_inc(shifted, 1)

            def soft_norm(c):
                _, kw = window(c)
                for g in range(2):
                    dve.wait_ge(exp_ready, 2 * c + g + 1)
                    step.do(v.tensor_reduce(soft[:, 3, 4 * g:4 * g + 4],
                                            prob[:, 4 * g:4 * g + 4, 0:kw], X, ALU.add))
                step.wait()
                chain(v.tensor_tensor(soft[:, 3, :], soft[:, 3, :], soft[:, 2, :], ALU.add))
                chain(v.reciprocal(soft[:, 4, :], soft[:, 3, :]))
                for g in range(2):
                    part = slice(4 * g, 4 * g + 4)
                    v.tensor_tensor(prob[:, part, 0:kw], prob[:, part, 0:kw],
                                    soft[:, 4, part].unsqueeze(2).to_broadcast([P, 4, kw]),
                                    ALU.mult).then_inc(probs_ready, 1)

            def attention_lower(c):
                dve.wait_ge(pv_hi, c + 1)
                cols = slice(CHUNK * c, CHUNK * (c + 1))
                v.tensor_tensor(y_lo[:, :, cols], bank[PV][:].rearrange("p (a q) -> p a q", a=PAIRS),
                                y_hi[:, :, cols].bitcast(F32), ALU.subtract).then_inc(pv_lo, 1)

            def gate_input(m):
                dve.wait_ge(gate_sig, m + 1)
                v.tensor_tensor(ib[:, m, :], ib[:, m, :], xc[:, m, :], ALU.mult).then_inc(gated, 1)

            def square(m):
                dve.wait_ge(decay_ready, m + 1)
                if m:
                    dve.wait_ge(square_ready, m)
                chain(v.tensor_tensor(stat[:], rb[:, m, :], rb[:, m, :], ALU.mult))
                v.scalar_tensor_tensor(out=xc[:, m, :], in0=stat[:], scalar=1.0, in1=xc[:, m, :],
                                       op0=ALU.add, op1=ALU.mult).then_inc(square_ready, 1)

            def scan(m):
                dve.wait_ge(root_ready, m + 1)
                chain(v.tensor_tensor(ib[:, m, :], ib[:, m, :], xc[:, m, :], ALU.mult))
                v.tensor_tensor_scan(ib[:, m, :], rb[:, m, :], ib[:, m, :], 0.0,
                                     ALU.mult, ALU.add).then_inc(h_ready, 1)

            def lru_out(m):
                dve.wait_ge(bank_free, (G_FIRST if m < 2 else G_TILES) + m + 1)
                dve.wait_ge(h_ready, 8)
                if m >= 2:
                    dve.wait_ge(y_lo_ready, m - 1)
                v.tensor_tensor(tmp2[:, m % 2, :], ib[:, m, :], tmp[:, m % 2, :], ALU.mult)\
                    .then_inc(y_ready, 1)

            def lru_lower(m):
                dve.wait_ge(y_hi_ready, m + 1)
                v.tensor_tensor(y_lo[:, m, :], tmp2[:, m % 2, :], y_hi[:, m, :].bitcast(F32),
                                ALU.subtract).then_inc(y_lo_ready, 1)

            for n in range(1, OL_TILES + 1):
                if n <= 4:
                    kv_scale(n - 1)
                if n <= 2:
                    norm_blocks(range(4 * (n - 1), 4 * n), 0)
                if n == 2:
                    dve.wait_ge(xlo_ready, KB)
                    chain(v.memset(lru_in[:, :, 0:3], 0.0))
                if 3 <= n < 13:
                    head_gain(n - 3)
                if 4 <= n < 14:
                    head_finish(n - 4)
                if n == 13:
                    query_factors()
                if n in (6, 8):
                    key_factor((n - 6) // 2)
                if n in (7, 9):
                    keys_out((n - 7) // 2)
                if 5 <= n < 13:
                    v_window(n - 5)
                for c in chunks_at(n):
                    soft_shift(c)
                    if c < CHUNKS - 1:
                        conv(c + 1)
                    soft_norm(c)
                    if c >= 4:
                        decay_rates(c - 4)
                    if c:
                        attention_lower(c - 1)
                    if c == CHUNKS - 1:
                        attention_lower(c)
                if n == X_TILES + 1:
                    conv(0)
                for m in GATES_WITH.get(n, ()):
                    gate_input(m)
                for m in DECAYS_WITH.get(n, ()):
                    square(m)
                if n == ROOTS_WITH:
                    for m in range(8):
                        scan(m)
                if n > G_TILES:
                    if n > G_TILES + 1:
                        lru_lower(n - G_TILES - 2)
                    lru_out(n - G_TILES - 1)
            lru_lower(7)
            step.restart()

            with dve.Fori(0, 4) as it:
                for k in range(2):
                    m = bass.ds(it * 2 + k, 1)
                    dve.wait_ge(m_lo_ready, it * 2 + (BASE + k))
                    dve.wait_ge(bank_free, it * 4 + (GATE_TILES + 2 * k + 1))
                    dve.wait_ge(vec_loaded, 16)
                    step.do(v.tensor_tensor(tmp2[:, 0:1, :], tmp[:, 0:1, :], buf_a[:, m, :], ALU.mult))
                    dve.wait_ge(bank_free, it * 4 + (GATE_TILES + 2 * k + 2))
                    dve.wait_ge(vec_loaded, 16)
                    step.do(v.tensor_tensor(tmp2[:, 1:2, :], tmp[:, 1:2, :], rb[:, m, :], ALU.mult))
                    step.wait()
                    v.tensor_tensor(tmp2[:, 0:1, :], tmp2[:, 0:1, :], tmp2[:, 1:2, :], ALU.add)\
                        .then_inc(merged_ready, 1)
                    dve.wait_ge(m_hi_ready, it * 2 + (k + 1))
                    dve.wait_ge(vec_loaded, 16)
                    v.tensor_tensor(y_lo[:, m, :], tmp2[:, 0:1, :], y_hi[:, m, :].bitcast(F32),
                                    ALU.subtract).then_inc(m_lo_ready, 1)
                step.restart()
            dve.wait_ge(x1_loaded, 16)
            for m in range(KB):
                dve.wait_ge(tile_done, OUT_TILES + m + 1)
                v.tensor_tensor(x1[:, m, :], x1[:, m, :], bank[m % 2][:], ALU.add).then_inc(bank_free, 1)
                dve.wait_ge(bank_free, OUT_TILES + m + 1)
                gain_block(x1, m, 1)
                if m:
                    gained_lower(m - 1, 1)
                    add_square(m - 1, 1)
            gained_lower(KB - 1, 1)
            add_square(KB - 1, 1)
            rms_mean(1)

            def query_scale(n, c):
                dve.wait_ge(tile_done, n + (PQ_TILES + 1))
                if not isinstance(n, int) or n >= 2:
                    dve.wait_ge(s_mm, n - 1)
                    dve.wait_ge(vec_loaded, 16)
                v.tensor_tensor(q_pk[:, c % 2, :], bank[c % 2][:], stat[:], ALU.mult).then_inc(bank_free, 1)

            def scores_out(n, c):
                dve.wait_ge(s_mm, n + 1)
                dve.wait_ge(vec_loaded, 16)
                at = slice(n, n + 1) if isinstance(n, int) else bass.ds(n, 1)
                v.tensor_copy(s[:, :, at, :],
                              bank[2 + c % 2][:].rearrange("p (b a k) -> p b a k", b=4, a=1)).then_inc(s_evac, 1)

            for c in range(4):
                query_scale(c, c)
                norm_blocks(range(2 * c, 2 * c + 2), 1)
                if c:
                    scores_out(c - 1, c - 1)
            with dve.Fori(1, 4) as it:
                for c in range(4):
                    query_scale(it * 4 + c, c)
                    scores_out(it * 4 + (c - 1), c - 1)
            scores_out(15, 15)
            step.restart()
            dve.wait_ge(iota_ready, 1)

            with dve.Fori(0, TBLOCKS) as it:
                dve.wait_ge(s_evac, 16)
                chain(v.tensor_copy(s_blk[:], s[:, bass.ds(it, 1), :, :].rearrange("p a l k -> p (a l) k")))
                for h in range(PEER_HEADS):
                    lists = [s_blk[:, 2 * h + p, :] for p in range(2)]
                    lo_, hi_ = slice(0, 8), slice(8, 16)
                    a = [step.do(v.max(top_s[:, p, lo_], lists[p])) for p in range(2)]
                    d = []
                    for p in range(2):
                        step.wait(a[p])
                        step.do(v.max_index(top_i[:, h, p, lo_], top_s[:, p, lo_], lists[p]))
                        d.append(step.do(v.match_replace(s_rest[:, p, :], top_s[:, p, lo_], lists[p],
                                                         LOWEST)))
                    e = []
                    for p in range(2):
                        step.wait(d[p])
                        e.append(step.do(v.max(top_s[:, p, hi_], s_rest[:, p, :])))
                    for p in range(2):
                        step.wait(e[p])
                        step.do(v.max_index(top_i[:, h, p, hi_], top_s[:, p, hi_], s_rest[:, p, :]))
                    chain(v.tensor_tensor(cand[:], top_s[:, 0, :].unsqueeze(2).to_broadcast([P, 16, 16]),
                                          top_s[:, 1, :].unsqueeze(1).to_broadcast([P, 16, 16]), ALU.add))
                    flat = cand[:].rearrange("p a b -> p (a b)")
                    chain(v.max(best[:, h, lo_], flat))
                    step.do(v.max_index(pos[:, 16 * h:16 * h + 8], best[:, h, lo_], flat))
                    chain(v.match_replace(cand_rest[:], best[:, h, lo_], flat, LOWEST))
                    chain(v.max(best[:, h, hi_], cand_rest[:]))
                    step.do(v.max_index(pos[:, 16 * h + 8:16 * h + 16], best[:, h, hi_], cand_rest[:]))
                step.wait()
                step.do(v.tensor_copy(esum[:, 0, :], best[:, :, 0]))
                step.do(v.tensor_single_scalar(half_i[:, 0, :], pos[:], 4, ALU.logical_shift_right))
                step.do(v.tensor_single_scalar(half_i[:, 1, :], pos[:], 15, ALU.bitwise_and))
                step.do(v.tensor_copy(top_f[:], top_i[:]))
                step.wait()
                v.tensor_tensor(best[:], best[:], esum[:, 0, :].unsqueeze(2)
                                .to_broadcast([P, PEER_HEADS, 16]), ALU.subtract).then_inc(best_ready, 1)
                chain(v.tensor_copy(half_f[:], half_i[:]))
                for p in range(2):
                    step.do(v.tensor_tensor(pick[:, p, :, :],
                                            half_f[:, p, :].unsqueeze(2).to_broadcast([P, P, 16]),
                                            iota_k[:].unsqueeze(1).to_broadcast([P, P, 16]), ALU.is_equal))
                step.wait()
                for p in range(2):
                    own = pick[:, p, :, :].rearrange("q (h k) a -> q h k a", h=PEER_HEADS)
                    step.do(v.tensor_tensor(own, own, top_f[:, :, p, :].unsqueeze(2)
                                            .to_broadcast([P, PEER_HEADS, 16, 16]), ALU.mult))
                step.wait()
                for p in range(2):
                    step.do(v.tensor_reduce(sel[:, p, :], pick[:, p, :, :], X, ALU.add))
                dve.wait_ge(gexp_ready, it + 1)
                step.wait()
                chain(v.tensor_reduce(esum[:, 0, :], best[:], X, ALU.add))
                chain(v.reciprocal(esum[:, 1, :], esum[:, 0, :]))
                v.tensor_tensor(sel[:, 2, :].rearrange("p (h k) -> p h k", h=PEER_HEADS), best[:],
                                esum[:, 1, :].unsqueeze(2).to_broadcast([P, PEER_HEADS, 16]),
                                ALU.mult).then_inc(sel_ready, 1)
                dve.wait_ge(sel_t, it + 1)
                t = bass.ds(it * P, P)
                chain(v.tensor_copy(g_rest[:, 0, :], bank[4][:, 2 * P:3 * P]))
                step.do(v.tensor_copy(i_t[:, t], bank[4][:, 0:P]))
                step.do(v.tensor_copy(j_t[:, t], bank[4][:, P:2 * P]))
                chain(v.tensor_copy(g_t[0][:, t], g_rest[:, 0, :]))
                chain(v.tensor_tensor(g_rest[:, 1, :], g_rest[:, 0, :], g_t[0][:, t], ALU.subtract))
                chain(v.tensor_copy(g_t[1][:, t], g_rest[:, 1, :]))
                chain(v.tensor_tensor(g_rest[:, 0, :], g_rest[:, 1, :], g_t[1][:, t], ALU.subtract))
                step.do(v.tensor_copy(g_t[2][:, t], g_rest[:, 0, :]))
                step.restart()

            def onehot(it, c):
                k = c % 2
                t = bass.ds(it * P + 16 * c, 16)

                def over_keys(x):
                    return x[:, t].unsqueeze(1).to_broadcast([P, N_KEYS, 16])
                dve.wait_ge(tok_done, it * 32 + (BASE + 4 * (c - 1)))
                dve.wait_ge(vec_loaded, 16)
                step.do(v.tensor_tensor(eq_j[:, k, :, :], iota_e[:], over_keys(j_t), ALU.is_equal))
                dve.wait_ge(onehot_ready, it * 8 + (BASE + c))
                dve.wait_ge(vec_loaded, 16)
                step.do(v.tensor_tensor(eq_i[:], iota_e[:], over_keys(i_t), ALU.is_equal))
                step.wait()
                for n in range(3):
                    last = v.tensor_tensor(gi[n][:, k, :, :], eq_i[:], over_keys(g_t[n]), ALU.mult)
                    if n < 2:
                        step.do(last)
                step.wait()
                last.then_inc(onehot_ready, 1)
                return last

            with dve.Fori(0, 4) as it:
                for c in range(8):
                    onehot(it, c)
                step.restart()

            def gate_times(k):
                return v.tensor_tensor(
                    act_in[:, k, :, :].rearrange("p c (b t) -> p c b t", b=16),
                    act_in[:, k, :, :].rearrange("p c (b t) -> p c b t", b=16),
                    g_in[:, k, :, :, :].rearrange("p b c t -> p c b t"), ALU.mult)

            with dve.Fori(0, 16) as it:
                for k in range(2):
                    dve.wait_ge(act_loaded[k], it * 16 + 16)
                    dve.wait_ge(g_loaded[k], it * 16 + 16)
                    gate_times(k).then_inc(e_ready, 1)
                    dve.wait_ge(e_hi_ready, it * 2 + (k + 1))
                    v.tensor_tensor(e_lo[:, k, :, :], act_in[:, k, :, :], e_hi[:, k, :, :].bitcast(F32),
                                    ALU.subtract).then_inc(e_lo_ready, 1)
            for m in range(KB):
                dve.wait_ge(bank_done, m + 1)
                v.tensor_tensor(x1[:, m, :], x1[:, m, :], bank[m][:], ALU.add).then_inc(out_ready, 1)

        @block.tensor
        def _(pe):
            pe.sem_inc(g_evac, BASE)
            mm = nc.tensor.matmul

            def tile(n, right_hi, right_lo, it=None, per=4, when=None, between=None):
                off = (lambda x: x) if it is None else (lambda x: it * per + x)
                pe.wait_ge(hi_ready, off(n + 1))
                if it is not None or n >= 2:
                    pe.wait_ge(bank_free, off(n - 1))
                ps = bank[n % 2][:]

                def upper(k):
                    w = w_hi[:, n % 2, P * k:P * (k + 1)]
                    mm(ps, w, right_hi[:, k, :], start=(k == 0), stop=False)
                    mm(ps, w, right_lo[:, k, :], start=False, stop=False)

                def lower(k):
                    return mm(ps, w_lo[:, n % 2, P * k:P * (k + 1)], right_hi[:, k, :],
                              start=False, stop=(k == KB - 1))
                if when:
                    for k in range(KB):
                        pe.wait_ge(when[0], when[1] + k)
                        upper(k)
                        if k == 2:
                            pe.wait_ge(lo_ready, off(n + 1))
                        if k >= 2:
                            lower(k - 2)
                    if between:
                        between()
                    lower(KB - 2)
                    last = lower(KB - 1)
                else:
                    for k in range(KB):
                        upper(k)
                    if between:
                        between()
                    pe.wait_ge(lo_ready, off(n + 1))
                    for k in range(KB):
                        last = lower(k)
                last.then_inc(tile_done, 1)

            def sum_squares(first):
                pe.wait_ge(sq_read, KB * (first + 1))
                mm(bank[MI][:], ones[:], stat[:], start=True, stop=True).then_inc(ss_ready, 1)

            def head(j):
                x = tmp[:, j % 2, :] if j < 2 else buf_a[:, j - 2, :]
                pe.wait_ge(head_gained, j + 1)
                if j >= 2:
                    pe.wait_ge(head_done, j - 1)
                b0 = (TR0, SC0)[j % 2]
                if j < 2:
                    mm(bank[b0][:], blocks[:], tmp2[:, j % 2, :], start=True, stop=True)
                else:
                    for b in range(TBLOCKS):
                        at = 2 * (TBLOCKS * (j - 2) + b)
                        mm(bank[TR0][:, at:at + 2], tmp2[:, j % 2, P * b:P * (b + 1)],
                           blocks[:, 0:P:CHUNK], start=True, stop=True)
                mm(bank[b0 + 1][:], rot, x, start=True, stop=True).then_inc(head_mm, 1)

            def turn_v(w):
                t0, kw = window(w)
                if w >= 2:
                    pe.wait_ge(vt_evac, w - 1)
                for a in range(2):
                    last = nc.tensor.transpose(bank[(MI, PV)[w % 2]][0:kw, P * a:P * (a + 1)],
                                               v_raw[:, a, t0:t0 + kw], ident)
                last.then_inc(vt_ready, 1)

            def scores(c):
                t0, kw = window(c)
                if c:
                    pe.wait_ge(exp_ready, 2 * c)
                pe.wait_ge(diag_ready, c + 1)
                for p in range(PAIRS):
                    last = mm(bank[SC0 + p // 4][:, P * (p % 4):P * (p % 4) + kw], q_diag[:, p, :],
                              kdup[:, p // 2, t0:t0 + kw], start=True, stop=True)
                last.then_inc(scores_ready, 1)

            def turn_probs(c):
                _, kw = window(c)
                if c:
                    pe.wait_ge(pt_ready, c)
                for p in range(PAIRS):
                    if p % 4 == 0:
                        pe.wait_ge(probs_ready, 2 * c + p // 4 + 1)
                    last = nc.tensor.transpose(bank[TR0 + p // 4][0:kw, P * (p % 4):P * (p % 4 + 1)],
                                               prob[:, p, 0:kw], ident)
                last.then_inc(pt_psum, 1)

            def weigh(c):
                _, kw = window(c)
                pe.wait_ge(pt_ready, c + 1)
                if c:
                    pe.wait_ge(pv_lo, c)
                for kv in range(N_KV):
                    for h in range(2):
                        at = P * (kv // 2) + 64 * (kv % 2)
                        last = mm(bank[PV][64 * h:64 * h + 64, P * kv:P * (kv + 1)],
                                  vwin[0:kw, c, at:at + 64],
                                  prob_t[0:kw, 2 * kv:2 * kv + 2, 64 * h:64 * h + 64],
                                  start=True, stop=True)
                last.then_inc(pv_ready, 1)

            def lru_gates(m):
                b0 = (SC0, TR0)[m % 2]
                pe.wait_ge(conv_ready, m + 1)
                if m >= 2:
                    pe.wait_ge(gate_sig, m - 1)
                for g in range(2):
                    last = mm(bank[b0 + g][:], gw[:, g, P * m:P * (m + 1)], xc[:, m, :],
                              start=True, stop=True)
                last.then_inc(gate_mm, 1)

            def chunk_products(c):
                if c:
                    weigh(c - 1)
                if c < CHUNKS - 1:
                    scores(c + 1)
                else:
                    pe.wait_ge(exp_ready, 2 * CHUNKS)
                    pe.wait_ge(gw_loaded, 16)
                    lru_gates(0)
                turn_probs(c)

            pe.wait_ge(consts_ready, 1)
            for n in range(OL_TILES):
                if 4 <= n < 14:
                    if n == 4:
                        pe.wait_ge(mat_loaded, 16)
                        pe.wait_ge(xlo_ready, KB)
                    head(n - 4)
                if 5 <= n < 13:
                    if n == 5:
                        pe.wait_ge(kv_biased, 4)
                    turn_v(n - 5)
                if n == X_TILES + 2:
                    pe.wait_ge(head_done, 10)
                    pe.wait_ge(kdup_ready, 8)
                    pe.wait_ge(vt_evac, CHUNKS)
                    scores(0)
                if n == OA_TILES:
                    weigh(CHUNKS - 1)
                for m in GATES_WITH.get(n, ()):
                    if m:
                        lru_gates(m)
                if n == OA_TILES:
                    pe.wait_ge(pv_lo, CHUNKS)
                if n == 0:
                    tile(0, y_hi, y_lo, when=(xg_lo, 1), between=lambda: sum_squares(0))
                elif n < Q_TILES or OA_TILES <= n < OA_TILES + KB:
                    tile(n, y_hi, y_lo)
                elif n == OA_TILES - 1:
                    tile(n, x_hi, x_lo, between=lambda: chunk_products(CHUNKS - 1))
                else:
                    tile(n, x_hi, x_lo)
                    for c in chunks_at(n):
                        chunk_products(c)

            def stage(first, rounds, right_hi, right_lo):
                with pe.Fori(0, rounds) as it:
                    for c in range(4):
                        tile(first + c, right_hi, right_lo, it)

            def stage_by_block(first, ready, right_hi, right_lo):
                for c in range(4):
                    tile(first + c, right_hi, right_lo, when=ready if c == 0 else None)
                with pe.Fori(1, 2) as it:
                    for c in range(4):
                        tile(first + c, right_hi, right_lo, it)

            stage_by_block(OL_TILES, (y_lo_ready, 1), y_hi, y_lo)
            stage(GATE_TILES, 4, x_hi, x_lo)
            stage_by_block(OUT_TILES, (m_lo_ready, BASE + 1), y_hi, y_lo)

            def key_scores(n, c):
                pe.wait_ge(q_ready, n + 1)
                if not isinstance(n, int) or n >= 2:
                    pe.wait_ge(s_evac, n - 1)
                at = slice(n, n + 1) if isinstance(n, int) else bass.ds(n, 1)
                for b in range(TBLOCKS):
                    last = mm(bank[2 + c % 2][:, P * b:P * (b + 1)], q_pk[:, c % 2, P * b:P * (b + 1)],
                              keys[:, at, :], start=True, stop=True)
                last.then_inc(s_mm, 1)

            for c in range(4):
                n = PQ_TILES + c
                if c == 0:
                    tile(n, x_hi, x_lo, when=(xg_lo, KB + 1), between=lambda: sum_squares(1))
                else:
                    tile(n, x_hi, x_lo)
                    if c == 1:
                        pe.wait_ge(keys_loaded, 16)
                    key_scores(c - 1, c - 1)
            with pe.Fori(1, 4) as it:
                for c in range(4):
                    tile(PQ_TILES + c, x_hi, x_lo, it)
                    key_scores(it * 4 + (c - 1), c - 1)
            key_scores(15, 15)

            pe.wait_ge(xlo_ready, 2 * KB)
            with pe.Fori(0, TBLOCKS) as it:
                for c in range(16):
                    tile(U_TILES + c, h_hi, h_lo, it, 16)
                    if c == 13:
                        pe.wait_ge(sel_ready, it + 1)
                        for k in range(3):
                            last = nc.tensor.transpose(bank[4][:, P * k:P * (k + 1)], sel[:, k, :], ident)
                        last.then_inc(sel_t, 1)

            with pe.Fori(0, 4) as it:
                for c in range(8):
                    tile(U_TILES + 64 + c, h_hi, h_lo, it, 8)
                    pe.wait_ge(onehot_ready, it * 8 + (BASE + c + 1))
                    for h in range(4):
                        pe.wait_ge(g_evac, it * 32 + (BASE + 4 * c + h - 3))
                        for t in range(4):
                            for n in range(3):
                                last = mm(bank[2 + h][:, P * t:P * (t + 1)], eq_j[:, c % 2, :, 4 * h + t],
                                          gi[n][:, c % 2, :, 4 * h + t], start=(n == 0), stop=(n == 2))
                        last.then_inc(tok_done, 1)
            with pe.Fori(0, 4) as it:
                for c in range(8):
                    tile(U_TILES + 96 + c, h_hi, h_lo, it, 8)

            def experts(it, first, final):
                for c in range(8):
                    k = c // 4
                    if isinstance(it, int):
                        off = it * 8 + V_TILES + c
                        group = it * 2 + k + 1
                    else:
                        off = it * 8 + (V_TILES + c)
                        group = it * 2 + (k + 1)
                    pe.wait_ge(hi_ready, off + 1)
                    if c % 4 == 0:
                        pe.wait_ge(e_lo_ready, group)
                    if final and c == 7:
                        pe.wait_ge(lo_ready, off + 1)
                        for m in range(KB):
                            w = w_hi[:, 1, P * m:P * (m + 1)]
                            mm(bank[m][:], w, e_hi[:, 1, 3, :], start=False, stop=False)
                            mm(bank[m][:], w, e_lo[:, 1, 3, :], start=False, stop=False)
                            mm(bank[m][:], w_lo[:, 1, P * m:P * (m + 1)], e_hi[:, 1, 3, :],
                               start=False, stop=True).then_inc(bank_done, 1)
                        continue
                    start = first and c == 0
                    order = [m % KB for m in range(2, KB + 2)] if start else range(KB)
                    for m in order:
                        if start and m < 2:
                            pe.wait_ge(bank_free, V_TILES - 1 + m)
                        w = w_hi[:, c % 2, P * m:P * (m + 1)]
                        mm(bank[m][:], w, e_hi[:, k, c % 4, :], start=start, stop=False)
                        mm(bank[m][:], w, e_lo[:, k, c % 4, :], start=False, stop=False)
                    pe.wait_ge(lo_ready, off + 1)
                    for m in range(KB):
                        last = mm(bank[m][:], w_lo[:, c % 2, P * m:P * (m + 1)],
                                  e_hi[:, k, c % 4, :], start=False, stop=False)
                    last.then_inc(tile_done, 1)

            pe.wait_ge(g_evac, BASE + T // 4)
            experts(0, True, False)
            with pe.Fori(1, 15) as it:
                experts(it, False, False)
            experts(15, False, True)


_NAMES = ["x_t", "dense_w", "u_t", "v_t", "gates_w", "sub_keys", "vecs", "rope", "mats"]


def _columns(a, n):
    return np.ascontiguousarray(np.asarray(a).reshape(n, P).T)


def _tiles(w):
    w = np.asarray(w)
    return w.reshape(KB, P, -1, P).transpose(2, 1, 0, 3).reshape(-1, P, D)


def _rope_tables():
    dim = HEAD_DIM // 4
    half = dim // 2
    inv = np.float32(500000.0) ** (-np.arange(0, dim, 2, dtype=np.float32) / np.float32(dim))
    ang = np.arange(T, dtype=np.float32)[None, :] * inv.astype(np.float32)[:, None]
    table = np.zeros((HEAD_DIM, 2, T), np.float32)
    table[:, 0] = 1.0
    table[0:half, 0] = table[half:dim, 0] = np.cos(ang)
    table[0:half, 1] = table[half:dim, 1] = np.sin(ang)
    return np.concatenate([table, table])


def _matrices():
    dim = HEAD_DIM // 4
    half = dim // 2
    swap = np.zeros((P, P), np.float32)
    for h in range(2):
        for d in range(half):
            a, b = HEAD_DIM * h + d, HEAD_DIM * h + half + d
            swap[b, a] = -1.0
            swap[a, b] = 1.0
    return np.ascontiguousarray(np.stack([np.eye(P, dtype=np.float32), swap], axis=1))


def kernel(**inputs):
    import concourse.bacc as bacc
    from concourse.bass_utils import run_bass_kernel_spmd

    a = {k: np.asarray(v) for k, v in inputs.items()}
    w_in, b_in = _tiles(a["w_in"][0]), a["b_in"][0].reshape(-1, P)
    dense_w = np.concatenate([
        w_in[W_IN_FIRST], w_in[W_IN_G[:2]], _tiles(a["w_o_attn"][0]), w_in[W_IN_G[2:]],
        _tiles(a["w_o_lru"][0]),
        w_in[W_IN_GATES], _tiles(a["w_out"][0]), _tiles(a["peer_w_q"][0])])
    none = np.zeros((KB, P), np.float32)
    biases = np.concatenate([b_in[W_IN_FIRST], b_in[W_IN_G[:2]], none, b_in[W_IN_G[2:]], none,
                             b_in[W_IN_GATES], none,
                             a["peer_b_q"][0].reshape(-1, P)])
    gates_w = np.zeros((P, 2, KB, P), np.float32)
    for g, name in enumerate(("w_rg", "w_ig")):
        w = a[name][0].reshape(KB, 2, 64, 64)
        for h in range(2):
            gates_w[64 * h:64 * h + 64, g, :, 64 * h:64 * h + 64] = w[:, h].transpose(1, 0, 2)
    sinks = np.repeat(a["attn_sinks"][0].reshape(PAIRS, 2).T, CHUNK, axis=0)
    vecs = np.concatenate([
        biases.T, _columns(a["conv_w"][0], 32), _columns(a["conv_b"][0], 8), _columns(a["b_rg"][0], 8),
        _columns(a["b_ig"][0], 8), _columns(a["lru_L"][0], 8), _columns(a["norm_mix_g"][0], 8),
        _columns(a["norm_ffn_g"][0], 8), np.tile(a["q_norm_g"][0], 2)[:, None],
        np.tile(a["k_norm_g"][0], 2)[:, None], sinks], axis=1)
    arrays = {
        "x_t": a["x"][0].T.reshape(KB, P, T).transpose(1, 0, 2),
        "dense_w": dense_w,
        "u_t": a["peer_u"][0].reshape(N_KEYS, N_KEYS, KB, P).transpose(0, 3, 2, 1).reshape(N_KEYS, P, D),
        "v_t": a["peer_v"][0].reshape(N_KEYS, P, D),
        "gates_w": gates_w.reshape(P, 2, D),
        "sub_keys": a["peer_sub_keys"][0].reshape(16, N_KEYS, P).transpose(2, 0, 1),
        "vecs": vecs,
        "rope": _rope_tables(),
        "mats": _matrices(),
    }
    arrays = {k: np.ascontiguousarray(v) for k, v in arrays.items()}
    nc = bacc.Bacc("TRN2", target_bir_lowering=False, num_devices=1)
    aps = [nc.dram_tensor(n, arrays[n].shape, F32, kind="ExternalInput").ap() for n in _NAMES]
    out = nc.dram_tensor("out", [P, KB, T], F32, kind="ExternalOutput").ap()
    build(nc, *aps, out)
    r = run_bass_kernel_spmd(nc, [arrays], core_ids=[0])
    y = np.asarray(r.results[0]["out"])
    return np.ascontiguousarray(y.transpose(2, 1, 0).reshape(1, T, D))
```
